# Optimizing a Trainium2 kernel written in Bass

```python
import jax, jax.numpy as jnp
from jax import lax
import numpy as np

D_MODEL = 2048
BATCH = 1
SEQ = 256
DEPTH = 1

MIX_WIDTH = D_MODEL
POOL_WIDTH = MIX_WIDTH // 2
POOL_WINDOWS = (2, 4, 8, 16)
POOL_GROUP = POOL_WIDTH // len(POOL_WINDOWS)
FOX_WIDTH = MIX_WIDTH - POOL_WIDTH
FOX_HEADS = 8
FOX_HEAD_DIM = FOX_WIDTH // FOX_HEADS
Q_BLOCK = 128
IN_COLS = POOL_WIDTH + 3 * FOX_WIDTH + FOX_HEADS
N_MEM = 256
XATTN_HEADS = 4
XATTN_HEAD_DIM = D_MODEL // XATTN_HEADS
PEER_HEADS = 8
PEER_KEYS = 128
PEER_EXPERTS = PEER_KEYS * PEER_KEYS
PEER_QUERY_DIM = 256
PEER_HALF = PEER_QUERY_DIM // 2
PEER_TOPK = 16
PEER_TOKEN_CHUNK = 128
EPS = 1e-6

kernel_name = "hymba_pool_fox_peer_layer"

def rms_norm(x, g):
    xf = x.astype(jnp.float32)
    y = xf * lax.rsqrt(jnp.mean(xf * xf, axis=-1, keepdims=True) + EPS)
    return (y * g.astype(jnp.float32)).astype(x.dtype)

def causal_window_mean(x, w):
    S = x.shape[1]
    cs = jnp.pad(jnp.cumsum(x.astype(jnp.float32), axis=1), ((0, 0), (1, 0), (0, 0)))
    upper = cs[:, 1:]
    lower = jnp.pad(cs, ((0, 0), (w - 1, 0), (0, 0)))[:, :S]
    count = jnp.minimum(jnp.arange(S) + 1, w).astype(jnp.float32)[None, :, None]
    return ((upper - lower) / count).astype(x.dtype)

def pool_mixer(a, pool_w, pool_scale):
    B, S, _ = a.shape
    groups = a.reshape(B, S, len(POOL_WINDOWS), POOL_GROUP)
    diffs = jnp.stack([causal_window_mean(groups[:, :, i], w) - groups[:, :, i]
                       for i, w in enumerate(POOL_WINDOWS)], axis=2)
    y = jnp.einsum('bsgc,gcd->bsgd', diffs, pool_w).reshape(B, S, POOL_WIDTH)
    return y * pool_scale

def forgetting_attention(q, k, v, f_logit):
    B, S, H, Dh = q.shape
    c = jnp.cumsum(jax.nn.log_sigmoid(f_logit.astype(jnp.float32)), axis=1).transpose(0, 2, 1)
    qh = q.transpose(0, 2, 1, 3) * (Dh ** -0.5)
    kh = k.transpose(0, 2, 1, 3)
    vh = v.transpose(0, 2, 1, 3)
    outs = []
    for start in range(0, S, Q_BLOCK):
        end = start + Q_BLOCK
        s = jnp.einsum('bhqd,bhkd->bhqk', qh[:, :, start:end], kh[:, :, :end]).astype(jnp.float32)
        s = s + c[:, :, start:end, None] - c[:, :, None, :end]
        causal = jnp.arange(end)[None, :] <= jnp.arange(start, end)[:, None]
        s = jnp.where(causal, s, -jnp.inf)
        p = jax.nn.softmax(s, axis=-1).astype(vh.dtype)
        outs.append(jnp.einsum('bhqk,bhkd->bhqd', p, vh[:, :, :end]))
    o = jnp.concatenate(outs, axis=2)
    return o.transpose(0, 2, 1, 3).reshape(B, S, H * Dh)

def memory_cross_attention(h, m, wq, wk, wv, wo):
    B, S, D = h.shape
    M = m.shape[1]
    q = (h @ wq).reshape(B, S, XATTN_HEADS, XATTN_HEAD_DIM)
    k = (m @ wk).reshape(B, M, XATTN_HEADS, XATTN_HEAD_DIM)
    v = (m @ wv).reshape(B, M, XATTN_HEADS, XATTN_HEAD_DIM)
    s = jnp.einsum('bshd,bmhd->bhsm', q, k).astype(jnp.float32) * (XATTN_HEAD_DIM ** -0.5)
    p = jax.nn.softmax(s, axis=-1).astype(v.dtype)
    o = jnp.einsum('bhsm,bmhd->bshd', p, v).reshape(B, S, D)
    return o @ wo

def peer_ffn(h, w_query, sub_keys, expert_u, expert_v):
    B, S, D = h.shape
    q = (h @ w_query).reshape(B, S, PEER_HEADS, 2, PEER_HALF)
    scores = jnp.einsum('bshcd,hckd->bshck', q, sub_keys).astype(jnp.float32)
    s_top, i_top = lax.top_k(scores, PEER_TOPK)
    cand = s_top[..., 0, :, None] + s_top[..., 1, None, :]
    cand_idx = i_top[..., 0, :, None] * PEER_KEYS + i_top[..., 1, None, :]
    cand = cand.reshape(B, S, PEER_HEADS, PEER_TOPK * PEER_TOPK)
    cand_idx = cand_idx.reshape(B, S, PEER_HEADS, PEER_TOPK * PEER_TOPK)
    best, pos = lax.top_k(cand, PEER_TOPK)
    expert_idx = jnp.take_along_axis(cand_idx, pos, axis=-1)
    gate = jax.nn.softmax(best, axis=-1).astype(h.dtype)
    T = B * S
    n_chunks = T // PEER_TOKEN_CHUNK
    K = PEER_HEADS * PEER_TOPK
    xs = h.reshape(n_chunks, PEER_TOKEN_CHUNK, D)
    idx = expert_idx.reshape(n_chunks, PEER_TOKEN_CHUNK, K)
    gs = gate.reshape(n_chunks, PEER_TOKEN_CHUNK, K)

    def chunk_fn(args):
        xc, ic, gc = args
        u = jnp.take(expert_u, ic, axis=0)
        act = jax.nn.gelu(jnp.einsum('ckd,cd->ck', u, xc), approximate=False)
        vv = jnp.take(expert_v, ic, axis=0)
        return jnp.einsum('ck,ckd->cd', gc * act, vv)

    out = lax.map(chunk_fn, (xs, idx, gs))
    return out.reshape(B, S, D)

def setup_inputs(seed: int = 0) -> dict:
    key = jax.random.key(seed)
    ks = jax.random.split(key, 24)
    n = jax.random.normal
    D = D_MODEL
    f32 = jnp.float32
    return {
        "x": n(ks[0], (BATCH, SEQ, D), f32),
        "mem": n(ks[1], (BATCH, N_MEM, D), f32),
        "mix_norm": 1.0 + 0.05 * n(ks[2], (DEPTH, D), f32),
        "w_in": n(ks[3], (DEPTH, D, IN_COLS), f32) * D ** -0.5,
        "b_forget": 3.0 + 0.1 * n(ks[4], (DEPTH, FOX_HEADS), f32),
        "pool_w": n(ks[5], (DEPTH, len(POOL_WINDOWS), POOL_GROUP, POOL_GROUP), f32) * POOL_GROUP ** -0.5,
        "pool_scale": 1.0 + 0.1 * n(ks[6], (DEPTH, POOL_WIDTH), f32),
        "w_out": n(ks[7], (DEPTH, MIX_WIDTH, D), f32) * MIX_WIDTH ** -0.5,
        "xattn_norm": 1.0 + 0.05 * n(ks[8], (DEPTH, D), f32),
        "mem_norm": 1.0 + 0.05 * n(ks[9], (DEPTH, D), f32),
        "xattn_wq": n(ks[10], (DEPTH, D, D), f32) * D ** -0.5,
        "xattn_wk": n(ks[11], (DEPTH, D, D), f32) * D ** -0.5,
        "xattn_wv": n(ks[12], (DEPTH, D, D), f32) * D ** -0.5,
        "xattn_wo": n(ks[13], (DEPTH, D, D), f32) * D ** -0.5,
        "peer_norm": 1.0 + 0.05 * n(ks[14], (DEPTH, D), f32),
        "peer_wq": n(ks[15], (DEPTH, D, PEER_HEADS * PEER_QUERY_DIM), f32) * D ** -0.5,
        "peer_sub_keys": n(ks[16], (DEPTH, PEER_HEADS, 2, PEER_KEYS, PEER_HALF), f32) * PEER_HALF ** -0.5,
        "peer_u": n(ks[17], (DEPTH, PEER_EXPERTS, D), f32) * D ** -0.5,
        "peer_v": n(ks[18], (DEPTH, PEER_EXPERTS, D), f32) * 0.3,
        "final_norm": 1.0 + 0.05 * n(ks[19], (D,), f32),
    }

def reference(x, mem, mix_norm, w_in, b_forget, pool_w, pool_scale, w_out,
              xattn_norm, mem_norm, xattn_wq, xattn_wk, xattn_wv, xattn_wo,
              peer_norm, peer_wq, peer_sub_keys, peer_u, peer_v, final_norm):
    B, S, _ = x.shape
    h = x
    for l in range(DEPTH):
        a = rms_norm(h, mix_norm[l])
        proj = a @ w_in[l]
        o0 = POOL_WIDTH
        a_pool = proj[..., :o0]
        q = proj[..., o0:o0 + FOX_WIDTH].reshape(B, S, FOX_HEADS, FOX_HEAD_DIM)
        k = proj[..., o0 + FOX_WIDTH:o0 + 2 * FOX_WIDTH].reshape(B, S, FOX_HEADS, FOX_HEAD_DIM)
        v = proj[..., o0 + 2 * FOX_WIDTH:o0 + 3 * FOX_WIDTH].reshape(B, S, FOX_HEADS, FOX_HEAD_DIM)
        f_logit = proj[..., o0 + 3 * FOX_WIDTH:] + b_forget[l]
        y_pool = pool_mixer(a_pool, pool_w[l], pool_scale[l])
        y_fox = forgetting_attention(q, k, v, f_logit)
        h = h + jnp.concatenate([y_pool, y_fox], axis=-1) @ w_out[l]
        m = rms_norm(mem, mem_norm[l])
        h = h + memory_cross_attention(rms_norm(h, xattn_norm[l]), m,
                                       xattn_wq[l], xattn_wk[l], xattn_wv[l], xattn_wo[l])
        h = h + peer_ffn(rms_norm(h, peer_norm[l]), peer_wq[l], peer_sub_keys[l], peer_u[l], peer_v[l])
    return rms_norm(h, final_norm)


_drawn_inputs = setup_inputs


def setup_inputs(seed=0):
    import zlib

    import numpy as np

    out = dict(_drawn_inputs(seed))
    spreads = {}
    factors = {'b_forget': 24.424, 'xattn_norm': 5.683, 'mem_norm': 4.429, 'peer_norm': 6.705}
    for name, (base, spread) in spreads.items():
        noise = np.random.default_rng([zlib.crc32(name.encode()), seed]).standard_normal(out[name].shape)
        drawn = base * np.exp(spread * noise) if base else spread * noise
        out[name] = __import__('jax').numpy.asarray(drawn.astype(out[name].dtype))
    for name, factor in factors.items():
        out[name] = (out[name] * factor).astype(out[name].dtype)
    return out
```

```python
import concourse.bass as bass
from concourse import mybir
from contextlib import ExitStack


class Steps:

    def __init__(self, engine, semaphore, passed=None):
        self.engine, self.semaphore, self.passed, self.n = engine, semaphore, passed, 0

    def __call__(self, instruction, apart=False):
        instruction.then_inc(self.semaphore, 1)
        self.n, self.steps = self.n + 1, self.steps + 1
        self.engine.wait_ge(self.semaphore, self.n)
        if apart:
            self.engine.sem_inc(self.passed, 1)

    steps = 0

    def enter(self, i, per_turn):
        self.start, self.steps, self.per_turn = self.n, 0, per_turn
        self.n = i * per_turn + self.start

    def leave(self, turns):
        assert self.steps == self.per_turn, (self.steps, self.per_turn)
        self.n = self.start + turns * self.per_turn



def hybrid_layer(
    nc: bass.Bass, x, mem, mix_norm, w_in, b_forget, pool_w, pool_scale, w_out, xattn_norm, mem_norm,
    xattn_wq, xattn_wk, xattn_wv, xattn_wo, peer_norm, peer_wq, peer_sub_keys, peer_u, peer_v,
    final_norm, out,
):
    F32, F32R, BF16, U32 = mybir.dt.float32, mybir.dt.float32r, mybir.dt.bfloat16, mybir.dt.uint32
    ALU, ACT, AX = mybir.AluOpType, mybir.ActivationFunctionType, mybir.AxisListType

    P = 128
    S, D = x.shape[1], x.shape[2]
    TT = S // P
    KT = D // P
    PW = pool_scale.shape[1]
    FH = b_forget.shape[1]
    FD = (D - PW) // FH
    WINDOWS = (2, 4, 8, 16)
    GT = PW // len(WINDOWS) // P
    XH = 4
    XT = D // XH // P
    XSCALE, FSCALE = float(D // XH) ** -0.5, float(FD) ** -0.5
    PH = peer_sub_keys.shape[1]
    KEYS = peer_sub_keys.shape[3]
    TOP = 16
    EPS = 1e-6
    LOW, MASKED = -3.0e38, -1.0e30
    assert TT == 2 and FD == P and XT == 4 and KEYS == P and S == mem.shape[1]

    CW, KC = 512, 2
    CH = KT // KC
    RING = 4
    HALF = CH // 2
    CT = CW // P
    assert HALF == RING
    ITEMS = {}
    at = 0
    for name, cols in (("in", PW + 3 * (D - PW)), ("k", D), ("v", D), ("out", D), ("q", D), ("o", D), ("peer", D)):
        ITEMS[name] = (at, cols // CW)
        at += cols // CW
    LAST = at - 1
    T_IN = (PW + 2 * (D - PW)) // CW
    GROUPS = TT * PH

    def rows(w):
        return w.rearrange("o (k p) n -> p (o k) n", p=P)

    base = 16512
    KB = 1024
    at_h, at_t1, at_t2 = base, base + 16 * KB, base + 48 * KB
    at_k, at_v, at_f = base + 80 * KB, base + 96 * KB, base + 120 * KB
    at_raw, at_split, at_small = base + 140 * KB, base + 156 * KB, base + 188 * KB
    small = [at_small]

    def put(name, shape, dt, offset=None):
        size = 4 if dt != BF16 else 2
        for n in shape[1:]:
            size *= n
        if offset is None:
            offset, small[0] = small[0], small[0] + (size + 31) // 32 * 32
        return nc.alloc_sbuf_tensor_at(name, shape, dt, offset=offset)

    h = put("h", [P, TT, D], F32, at_h)
    t1_hi, t1_lo = put("t1_hi", [P, KT, S], F32R, at_t1), put("t1_lo", [P, KT, S], F32R, at_t1 + 16 * KB)
    t2_hi, t2_lo = put("t2_hi", [P, KT, S], F32R, at_t2), put("t2_lo", [P, KT, S], F32R, at_t2 + 16 * KB)
    raw = put("raw", [P, RING, KC, CW], F32, at_raw)
    w_hi = put("w_hi", [P, RING, KC, CW], F32R, at_split)
    w_lo = put("w_lo", [P, RING, KC, CW], F32R, at_split + 16 * KB)
    poolw = put("poolw", [P, len(WINDOWS), GT, GT * P], F32, at_t2)
    inv = put("inv", [P, len(WINDOWS), S], F32, at_t2 + 8 * KB)
    diff = put("diff", [P, len(WINDOWS) * GT, S], F32, at_t2 + 12 * KB)
    sel = put("sel", [FH, FH, S], F32, at_t2 + 20 * KB)
    cum = put("cum", [FH, S], F32, at_t2 + 28 * KB)
    ncum = put("ncum", [FH, S], F32, at_t2 + 29 * KB)
    wf = put("wf", [P, KT, FH], F32, at_t2 + 30 * KB)
    wf_hi = put("wf_hi", [P, KT, FH], F32R, at_t2 + 30 * KB + 512)
    wf_lo = put("wf_lo", [P, KT, FH], F32R, at_t2 + 31 * KB)
    normed = put("normed", [P, TT, D], F32, at_k)
    memk = put("memk", [P, KT, S], F32, at_k)
    hn = put("hn", [P, TT, D], F32, at_k)
    foxT = put("foxT", [P, PW // P + 2 * FH, S], F32, at_v)
    memv = put("memv", [P, TT, D], F32, at_v)
    peer_gain = put("peer_gain", [P, D], F32, at_v)
    scores = put("scores", [P, TT, PH * 2 * KEYS], F32, at_v)
    skT = put("skT", [P, PH * 2, KEYS], F32, at_v + 16 * KB)
    foxv = put("foxv", [P, TT, FH * P], F32, at_f)
    foxs = put("foxs", [P, FH, 3 * P], F32, at_f + 8 * KB)
    pad = 16
    winA = put("winA", [P, GT, pad + S], F32, at_f + 8 * KB)
    winB = put("winB", [P, GT, pad + S], F32, at_f + 8 * KB + 2304)
    fz, fa, fe, fones = (put(n, [FH, S], F32, at_f + (13 + k) * KB) for k, n in enumerate(("fz", "fa", "fe", "fones")))
    hs = put("hs", [P, 2, TT, CW], F32, at_f)
    qs = put("qs", [P, 2, XT, S], F32, at_f)
    xp = put("xp", [P, XH, TT, S], F32, at_f + 8 * KB)
    xpT = put("xpT", [P, XH, TT, S], F32, at_f)
    skraw = put("skraw", [P, PH * 2, P], F32, at_f + 8 * KB)
    pq = put("pq", [P, 2, CT, S], F32, at_f)
    u_ring = put("u_ring", [P, 4, D], F32, at_t1)
    v_ring = put("v_ring", [P, 4, D], F32, at_split)
    final_gain = put("final_gain", [P, D], F32, at_raw)
    product = put("product", [P, 2, D], BF16, at_raw + 8 * KB)
    y_sum = put("y_sum", [P, TT, D], F32, at_t2)
    y_out = put("y_out", [P, TT, D], F32, at_t2 + 16 * KB)
    ident = put("ident", [P, P], F32)
    mask = put("mask", [P, 2 * P], F32)
    zeros = put("zeros", [P, CW], BF16)
    junk = put("junk", [P, 2, CW], BF16)
    NG = 4 * KT + PW // P
    gain_rows = put("gain_rows", [NG, P], F32)
    gains = put("gains", [P, NG], F32)
    G_MIX, G_MEM, G_X, G_PEER, G_POOL = 0, KT, 2 * KT, 3 * KT, 4 * KT
    bf = put("bf", [FH, 1], F32)
    fsb = put("fsb", [P, TT, FH], F32)
    sq = put("sq", [P, TT, 4], F32)
    ss = put("ss", [P, TT], F32)
    rt = put("rt", [P, TT], F32)
    rstd = put("rstd", [P, TT], F32)
    xfac = put("xfac", [P, TT], F32)
    fmax = put("fmax", [P, FH, TT], F32)
    fneg = put("fneg", [P, FH, TT], F32)
    fsum = put("fsum", [P, FH, TT], F32)
    frec = put("frec", [P, FH, TT], F32)
    pT = put("pT", [P, 2, 3 * P], F32)
    xmax = put("xmax", [P, 2, TT], F32)
    xneg = put("xneg", [P, 2, TT], F32)
    xsum = put("xsum", [P, 2, TT], F32)
    xrec = put("xrec", [P, 2, TT], F32)
    cur = put("cur", [P, 2, KEYS], F32, at_f + 8 * KB)
    rest = put("rest", [P, 2, KEYS], F32, at_f + 9 * KB)
    top = put("top", [P, 2, TOP], F32)
    top_at = put("top_at", [P, 2, TOP], U32)
    cand = put("cand", [P, TOP, TOP], F32, at_f + 10 * KB)
    cand_rest = put("cand_rest", [P, TOP, TOP], F32, at_f + 11 * KB)
    best = put("best", [P, TOP], F32)
    pos = put("pos", [P, TOP], U32)
    ab = put("ab", [P, 2, TOP], U32)
    hot = put("hot", [P, 2, TOP, TOP], F32, at_f + 12 * KB)
    picked = put("picked", [P, 2, TOP], F32)
    iota = put("iota", [P, TOP], F32)
    neg_best = put("neg_best", [P, 1], F32)
    exps = put("exps", [P, TOP], F32)
    exp_sum = put("exp_sum", [P, 1], F32)
    exp_rec = put("exp_rec", [P, 1], F32)
    gate = put("gate", [P, 2, TOP], F32)
    idx_u = put("idx_u", [P, 2, TOP], U32)
    idx_v = put("idx_v", [P, 2, TOP], U32)
    dots = put("dots", [P, 2, TOP], F32)
    acts = put("acts", [P, 2, TOP], F32)
    wts = put("wts", [P, 2, TOP], F32)
    diag = put("diag", [P, 4, P], F32, at_f + 14 * KB)
    assert small[0] <= 229344, small[0]

    w_in_r, w_k_r, w_v_r, w_out_r = rows(w_in), rows(xattn_wk), rows(xattn_wv), rows(w_out)
    w_q_r, w_o_r, w_peer_r = rows(xattn_wq), rows(xattn_wo), rows(peer_wq)
    u_rows, v_rows = peer_u.rearrange("o n d -> (o n) d"), peer_v.rearrange("o n d -> (o n) d")

    with ExitStack() as ctx:
        acc = ctx.enter_context(nc.psum_tensor("acc", [P, 2, 2, CW], F32))
        misc = ctx.enter_context(nc.psum_tensor("misc", [P, 4, CW], F32))

        def sem(name):
            return ctx.enter_context(nc.semaphore(name))

        x_landed, mem_landed, small_landed, pool_landed = sem("x_landed"), sem("mem_landed"), sem("small_landed"), sem("pool_landed")
        sk_landed, pgain_landed, fgain_landed, out_landed = sem("sk_landed"), sem("pgain_landed"), sem("fgain_landed"), sem("out_landed")
        raw_landed = [sem(f"raw_landed{s}") for s in range(RING)]
        hi_done, lo_even, lo_odd, chunk_used = sem("hi_done"), sem("lo_even"), sem("lo_odd"), sem("chunk_used")
        acc_done, acc_free = sem("acc_done"), sem("acc_free")
        consts, gains_T, gains_ready, wf_hi_done, wf_ready = sem("consts"), sem("gains_T"), sem("gains_ready"), sem("wf_hi_done"), sem("wf_ready")
        inv_ready = sem("inv_ready")
        squares, var_ready, root_ready, rstd_ready, normed_ready = sem("squares"), sem("var_ready"), sem("root_ready"), sem("rstd_ready"), sem("normed_ready")
        tr_ready, tr_hi, tr_lo = sem("tr_ready"), sem("tr_hi"), sem("tr_lo")
        f_done, f_copied, fT_done, fa_ready, fl_ready, cum_ready = sem("f_done"), sem("f_copied"), sem("fT_done"), sem("fa_ready"), sem("fl_ready"), sem("cum_ready")
        diff_ready, poolT_done = sem("diff_ready"), sem("poolT_done")
        qk_done, qk_read, fneg_ready, fexp_done, fp_ready = sem("qk_done"), sem("qk_read"), sem("fneg_ready"), sem("fexp_done"), sem("fp_ready")
        pT_done, pT_copied, fo_done, fo_hi, fo_lo = sem("pT_done"), sem("pT_copied"), sem("fo_done"), sem("fo_hi"), sem("fo_lo")
        h_copied = sem("h_copied")
        xs_done, xneg_ready, xexp_done, xp_ready = sem("xs_done"), sem("xneg_ready"), sem("xexp_done"), sem("xp_ready")
        xpT_done, xpT_copied, xo_done, xo_hi, xo_lo = sem("xpT_done"), sem("xpT_copied"), sem("xo_done"), sem("xo_hi"), sem("xo_lo")
        skT_done, skT_copied, ps_done, scores_ready = sem("skT_done"), sem("skT_copied"), sem("ps_done"), sem("scores_ready")
        u_landed = [sem(f"u_landed{s}") for s in range(4)]
        v_landed = [sem(f"v_landed{s}") for s in range(4)]
        routed, idx_v_ready, nbest_ready, gexp_done = sem("routed"), sem("idx_v_ready"), sem("nbest_ready"), sem("gexp_done")
        dot_done, gelu_done, wts_ready, diag_ready, v_used = sem("dot_done"), sem("gelu_done"), sem("wts_ready"), sem("diag_ready"), sem("v_used")
        y_done, y_added, y_squared, y_var, y_root, y_ready = sem("y_done"), sem("y_added"), sem("y_squared"), sem("y_var"), sem("y_root"), sem("y_ready")
        dve_step, act_step, pool_step, passed = sem("dve_step"), sem("act_step"), sem("pool_step"), sem("passed")
        block = ctx.enter_context(nc.Block())

        def wait_apart(engine, semaphore, value):
            engine.wait_ge(semaphore, value)
            engine.sem_inc(passed, 1)


        PAIRS = KT // 2
        PAIR0 = {"x": 0, "mem": PAIRS, "h1": 2 * PAIRS, "h2": 3 * PAIRS}

        @block.sync
        def _(sp):
            def item(n, w, i, first=False):
                for j in range(CH):
                    if not (first and j < RING):
                        sp.wait_ge((lo_even, lo_odd)[j % 2], n * HALF + (j // 2 - 1))
                    sp.dma_start(raw[:, j % RING, :, :],
                                 w[:, j * KC:(j + 1) * KC, bass.ts(i, CW)]).then_inc(raw_landed[j % RING], 16)

            sp.dma_start(h[:, 0, :], x[0, 0:P, :]).then_inc(x_landed, 16)
            sp.dma_start(h[:, 1, :], x[0, P:S, :]).then_inc(x_landed, 16)
            for v, r in ((mix_norm, G_MIX), (mem_norm, G_MEM), (xattn_norm, G_X), (peer_norm, G_PEER), (pool_scale, G_POOL)):
                v2 = v.rearrange("o (k p) -> (o k) p", p=P)
                sp.dma_start(gain_rows[r:r + v2.shape[0], :], v2).then_inc(small_landed, 16)
            sp.dma_start(bf[:, :], b_forget.rearrange("o f -> f o")).then_inc(small_landed, 16)
            sp.dma_start(wf[:, :, :], w_in_r[:, :, PW + 3 * FH * P:]).then_inc(small_landed, 16)
            n0, _ = ITEMS["in"]
            item(0, w_in_r, 0, first=True)
            sp.dma_start(poolw[:, :, :, :], pool_w[0].rearrange("g (c p) d -> p g c d", p=P)).then_inc(pool_landed, 16)
            sp.wait_ge(tr_ready, PAIRS)
            sp.dma_start(normed[:, :, :], mem[0].rearrange("(t p) d -> p t d", p=P)).then_inc(mem_landed, 16)
            with sp.Fori(1, ITEMS["in"][1]) as i:
                item(i, w_in_r, i)
            for name, w in (("k", w_k_r), ("v", w_v_r), ("out", w_out_r), ("q", w_q_r)):
                n0, items = ITEMS[name]
                with sp.Fori(0, items) as i:
                    item(i + n0, w, i)
            n0, items = ITEMS["o"]
            item(n0, w_o_r, 0)
            sp.wait_ge(xpT_done, XH)
            sp.dma_start(skraw[:, :, :], peer_sub_keys[0].rearrange("h c k d -> k (h c) d")).then_inc(sk_landed, 16)
            sp.wait_ge(xo_done, 2 * XH)
            sp.dma_start(peer_gain[:, :], peer_norm[0:1, :].to_broadcast([P, D])).then_inc(pgain_landed, 16)
            with sp.Fori(1, items) as i:
                item(i + n0, w_o_r, i)
            n0, items = ITEMS["peer"]
            with sp.Fori(0, items) as i:
                item(i + n0, w_peer_r, i)
            sp.wait_ge(scores_ready, items)
            sp.dma_start(final_gain[:, :], final_norm.rearrange("(o d) -> o d", o=1).to_broadcast([P, D])).then_inc(fgain_landed, 16)
            for c in range(TT):
                sp.wait_ge(y_ready, c + 1)
                sp.dma_start(out[0, c * P:(c + 1) * P, :], y_out[:, c, :]).then_inc(out_landed, 16)
            sp.wait_ge(out_landed, 16 * TT)

        @block.gpsimd
        def _(pool):
            step = Steps(pool, pool_step)
            step(nc.gpsimd.memset(ident[:, :], 0.0))
            nc.gpsimd.affine_select(out=ident[:, :], in_=ident[:, :], compare_op=ALU.not_equal, fill=1.0,
                                    base=0, pattern=[[-1, P]], channel_multiplier=1).then_inc(consts, 1)

            def low_parts(n, half):
                for j in range(half * HALF, half * HALF + HALF, 2):
                    pool.wait_ge(hi_done, n * CH + (j + 1))
                    nc.gpsimd.tensor_tensor(w_lo[:, j % RING, :, :], raw[:, j % RING, :, :],
                                            w_hi[:, j % RING, :, :].bitcast(F32), ALU.subtract).then_inc(lo_even, 1)

            low_parts(0, 0)
            step(nc.gpsimd.memset(mask[:, :], 0.0))
            nc.gpsimd.affine_select(out=mask[:, P:2 * P], in_=mask[:, P:2 * P], compare_op=ALU.is_ge, fill=MASKED,
                                    base=0, pattern=[[-1, P]], channel_multiplier=1).then_inc(consts, 1)
            step(nc.gpsimd.memset(sel[:, :, :], 0.0))
            nc.gpsimd.affine_select(out=sel[:, :, :], in_=sel[:, :, :], compare_op=ALU.not_equal, fill=1.0,
                                    base=0, pattern=[[-1, FH], [0, S]], channel_multiplier=1).then_inc(consts, 1)
            nc.gpsimd.memset(zeros[:, :], 0.0).then_inc(consts, 1)
            nc.gpsimd.memset(fones[:, :], 1.0).then_inc(consts, 1)
            nc.gpsimd.iota(iota[:, :], pattern=[[1, TOP]], base=0, channel_multiplier=0,
                           allow_small_or_imprecise_dtypes=True).then_inc(consts, 1)
            step(nc.gpsimd.iota(inv[:, 0, :], pattern=[[1, S]], base=1, channel_multiplier=0,
                                allow_small_or_imprecise_dtypes=True))
            for g in range(len(WINDOWS) - 1, -1, -1):
                step(nc.gpsimd.tensor_scalar(inv[:, g, :], inv[:, 0, :], float(WINDOWS[g]), None, ALU.min))
            pool.sem_inc(inv_ready, 1)
            with pool.Fori(0, LAST) as n:
                low_parts(n, 1)
                low_parts(n + 1, 0)
            low_parts(LAST, 1)

            def gather_u(p, q, k, fresh=False):
                if not (fresh and k < 4):
                    wait_apart(pool, dot_done, p * TOP + (k - 3))
                nc.gpsimd.indirect_dma_start(
                    out=u_ring[:, k % 4, :], out_offset=None, in_=u_rows,
                    in_offset=bass.IndirectOffsetOnAxis(ap=idx_u[:, q, k:k + 1], axis=0)).then_inc(u_landed[k % 4], 16)

            def gather_v(g, q, k, fresh=False):
                if not (fresh and k < 4):
                    wait_apart(pool, v_used, g * TOP + (k - 3))
                nc.gpsimd.indirect_dma_start(
                    out=v_ring[:, k % 4, :], out_offset=None, in_=v_rows,
                    in_offset=bass.IndirectOffsetOnAxis(ap=idx_v[:, q, k:k + 1], axis=0)).then_inc(v_landed[k % 4], 16)

            def period(p, q, first=False, second=False):
                pool.wait_ge(routed, p + 1)
                if not first:
                    pool.wait_ge(idx_v_ready, p)
                for k in range(TOP):
                    gather_u(p, q, k, fresh=first)
                    if not first:
                        gather_v(p - 1, 1 - q, k, fresh=second)

            period(0, 0, first=True)
            period(1, 1, second=True)
            with pool.Fori(1, GROUPS // 2) as b:
                period(b * 2, 0)
                period(b * 2 + 1, 1)
            pool.wait_ge(idx_v_ready, GROUPS)
            for k in range(TOP):
                gather_v(GROUPS - 1, 1, k)

        @block.scalar
        def _(act):
            def high_parts(n, half, first=False):
                for j in range(half * HALF, half * HALF + HALF):
                    act.wait_ge(raw_landed[j % RING], n * (2 * 16) + 16 * (j // RING + 1))
                    if not first:
                        act.wait_ge(chunk_used, n * CH + (j - RING + 1))
                    nc.scalar.activation(w_hi[:, j % RING, :, :], raw[:, j % RING, :, :], ACT.Copy).then_inc(hi_done, 1)

            def square_sums(src, i, before, fresh=False):
                for t in range(TT):
                    if not fresh:
                        act.wait_ge(squares, before * TT + (t - 1))
                    nc.scalar.activation(junk[:, t, :], src(t), ACT.Square, accum_out=sq[:, t, bass.ds(i, 1)]).then_inc(squares, 1)

            def root(k):
                act.wait_ge(var_ready, k)
                nc.scalar.activation(rt[:, :], ss[:, :], ACT.Sqrt).then_inc(root_ready, 1)

            def pair_hi(pair, bank, hi, kt, gain):
                act.wait_ge(tr_ready, pair + 1)
                for kk in range(2):
                    ins = nc.scalar.activation(hi[:, bass.ds(kt + kk, 1), :], misc[:, bank, kk * S:(kk + 1) * S], ACT.Copy,
                                               scale=gains[:, bass.ds(kt + (gain + kk), 1)])
                ins.then_inc(tr_hi, 1)

            act.wait_ge(x_landed, 16 * TT)
            for i in range(4):
                square_sums(lambda t: h[:, t, i * CW:(i + 1) * CW], i, i, fresh=i == 0)
            root(1)
            act.wait_ge(rstd_ready, 1)
            nc.scalar.activation(normed[:, 1, :], h[:, 1, :], ACT.Copy, scale=rstd[:, 1:2]).then_inc(normed_ready, 1)
            high_parts(0, 0, first=True)
            act.wait_ge(small_landed, 16 * 7)
            nc.scalar.activation(wf_hi[:, :, :], wf[:, :, :], ACT.Copy).then_inc(wf_hi_done, 1)
            act.wait_ge(gains_ready, 1)
            for p in range(PAIRS):
                pair_hi(PAIR0["x"] + p, p % 4, t1_hi, 2 * p, G_MIX)
            with act.Fori(0, T_IN) as n:
                high_parts(n, 1)
                high_parts(n + 1, 0)
            act.wait_ge(mem_landed, 16)
            for i in range(4):
                square_sums(lambda t: normed[:, t, i * CW:(i + 1) * CW], i, 4 + i)
            high_parts(T_IN, 1)
            root(2)
            high_parts(T_IN + 1, 0)
            act.wait_ge(rstd_ready, 2)
            nc.scalar.activation(normed[:, 1, :], normed[:, 1, :], ACT.Copy, scale=rstd[:, 1:2]).then_inc(normed_ready, 1)
            act.wait_ge(fa_ready, 1)
            nc.scalar.activation(fe[:, :], fa[:, :], ACT.Exp, scale=-1.0).then_inc(act_step, 1)
            act.wait_ge(act_step, 1)
            nc.scalar.activation(fe[:, :], fe[:, :], ACT.Ln, bias=1.0).then_inc(fl_ready, 1)
            high_parts(T_IN + 1, 1)
            high_parts(T_IN + 2, 0)
            for g in range(len(WINDOWS)):
                act.wait_ge(poolT_done, g + 1)
                for dt in range(GT):
                    col = G_POOL + g * GT + dt
                    ins = nc.scalar.activation(t1_hi[:, g * GT + dt, :], misc[:, g, dt * S:(dt + 1) * S], ACT.Copy,
                                               scale=gains[:, col:col + 1])
                ins.then_inc(tr_hi, 1)
            for p in range(PAIRS):
                act.wait_ge(tr_ready, PAIR0["mem"] + p + 1)
                for kk in range(2):
                    ins = nc.scalar.activation(t2_hi[:, 2 * p + kk, :], misc[:, p % 4, kk * S:(kk + 1) * S], ACT.Copy,
                                               scale=gains[:, G_MEM + 2 * p + kk:G_MEM + 2 * p + kk + 1])
                ins.then_inc(tr_hi, 1)
            act.wait_ge(fneg_ready, 1)
            for f in range(FH):
                for t in range(TT):
                    part = foxs[:, f, t * P:(2 * t + 1) * P]
                    nc.scalar.activation(part, part, ACT.Exp, bias=fneg[:, f, t:t + 1], scale=FSCALE,
                                         accum_out=fsum[:, f, t:t + 1]).then_inc(fexp_done, 1)
            for name in ("k", "v"):
                n0, items = ITEMS[name]
                with act.Fori(0, items) as i:
                    high_parts(i + n0, 1)
                    high_parts(i + (n0 + 1), 0)
                if name == "k":
                    for f in range(FH):
                        act.wait_ge(fo_done, f + 1)
                        nc.scalar.activation(t1_hi[:, PW // P + f, :], misc[:, 2 + f % 2, 0:S], ACT.Copy).then_inc(fo_hi, 1)

            def residual_items(name, hi, gain, pair0, squares0):
                n0, items = ITEMS[name]
                with act.Fori(0, items // 2) as b:
                    for q in range(2):
                        i = b * 2 + q
                        high_parts(i + n0, 1)
                        if q:
                            for p in range(2):
                                pair_hi(b * 4 + (pair0 + p), p, hi, b * 8 + 2 * p, gain)
                        high_parts(i + (n0 + 1), 0)
                        act.wait_ge(acc_free, i + (n0 + 1))
                        nc.scalar.activation(h[:, :, bass.ds(i * CW, CW)], hs[:, q, :, :], ACT.Copy).then_inc(h_copied, 1)
                        square_sums(lambda t: hs[:, q, t, :], i, i + squares0)
                    for p in range(2):
                        pair_hi(b * 4 + (pair0 + 2 + p), 2 + p, hi, b * 8 + (4 + 2 * p), gain)

            residual_items("out", t2_hi, G_X, PAIR0["h1"], 8)
            root(3)
            n0, items = ITEMS["q"]

            def x_exps(i, q):
                for t in range(TT):
                    act.wait_ge(xneg_ready, i * TT + (t + 1))
                    nc.scalar.activation(xp[:, bass.ds(i, 1), t, :], misc[:, 2 * q + t, 0:S], ACT.Exp, bias=xneg[:, q, t:t + 1],
                                         scale=xfac[:, t:t + 1], accum_out=xsum[:, q, t:t + 1]).then_inc(xexp_done, 1)

            with act.Fori(0, items // 2) as b:
                high_parts(b * 2 + n0, 1)
                high_parts(b * 2 + (n0 + 1), 0)
                high_parts(b * 2 + (n0 + 1), 1)
                x_exps(b * 2, 0)
                high_parts(b * 2 + (n0 + 2), 0)
                x_exps(b * 2 + 1, 1)
            for u in range(2 * XH):
                act.wait_ge(xo_done, u + 1)
                nc.scalar.activation(t1_hi[:, 2 * u:2 * u + 2, :], misc[:, 2 + u % 2, :].rearrange("p (a s) -> p a s", a=2),
                                     ACT.Copy).then_inc(xo_hi, 1)
            residual_items("o", t2_hi, G_PEER, PAIR0["h2"], 12)
            root(4)
            n0, items = ITEMS["peer"]
            with act.Fori(0, items - 1) as i:
                high_parts(i + n0, 1)
                high_parts(i + (n0 + 1), 0)
            high_parts(LAST, 1)

            def gate_exp(g):
                act.wait_ge(nbest_ready, g + 1)
                nc.scalar.activation(exps[:, :], best[:, :], ACT.Exp, bias=neg_best[:, 0:1],
                                     accum_out=exp_sum[:, 0:1]).then_inc(gexp_done, 1)

            def diagonals(g, q, fresh=False):
                act.wait_ge(wts_ready, g + 1)
                for k in range(TOP):
                    if not (fresh and k < 4):
                        act.wait_ge(v_used, g * TOP + (k - 3))
                    nc.scalar.activation(diag[:, k % 4, :], ident[:, :], ACT.Copy, scale=wts[:, q, k:k + 1]).then_inc(diag_ready, 1)

            def gelu(g, q):
                act.wait_ge(dot_done, g * TOP + TOP)
                nc.scalar.activation(acts[:, q, :], dots[:, q, :], ACT.Gelu).then_inc(gelu_done, 1)

            def period(p, q, first=False, second=False, last=False):
                if not last:
                    gate_exp(p + 1)
                if not first:
                    diagonals(p - 1, 1 - q, fresh=second)
                gelu(p, q)

            def finish(c):
                act.wait_ge(y_added, c + 1)
                for i in range(4):
                    if c or i >= 2:
                        act.wait_ge(y_squared, 4 * c + i - 1)
                    nc.scalar.activation(junk[:, i % 2, :], y_sum[:, c, i * CW:(i + 1) * CW], ACT.Square,
                                         accum_out=sq[:, c, i:i + 1]).then_inc(y_squared, 1)
                act.wait_ge(y_var, c + 1)
                nc.scalar.activation(rt[:, c:c + 1], ss[:, c:c + 1], ACT.Sqrt).then_inc(y_root, 1)

            gate_exp(0)
            period(0, 0, first=True)
            period(1, 1, second=True)
            with act.Fori(1, GROUPS // 2 - 1) as b:
                period(b * 2, 0)
                period(b * 2 + 1, 1)
            finish(0)
            period(GROUPS - 2, 0)
            period(GROUPS - 1, 1, last=True)
            diagonals(GROUPS - 1, 1)
            finish(1)

        @block.vector
        def _(dve):
            step = Steps(dve, dve_step, passed=passed)

            def low_parts(n, half):
                for j in range(half * HALF + 1, half * HALF + HALF, 2):
                    dve.wait_ge(hi_done, n * CH + (j + 1))
                    nc.vector.tensor_tensor(w_lo[:, j % RING, :, :], raw[:, j % RING, :, :],
                                            w_hi[:, j % RING, :, :].bitcast(F32), ALU.subtract).then_inc(lo_odd, 1)

            def reciprocal_root(k, sums):
                dve.wait_ge(squares, sums)
                step(nc.vector.tensor_reduce(ss[:, :], sq[:, :, :], AX.X, ALU.add))
                nc.vector.tensor_scalar(ss[:, :], ss[:, :], 1.0 / D, EPS, ALU.mult, ALU.add).then_inc(var_ready, 1)
                dve.wait_ge(root_ready, k)
                nc.vector.reciprocal(rstd[:, :], rt[:, :]).then_inc(rstd_ready, 1)
                dve.wait_ge(rstd_ready, k)

            def pair_lo(done, count, bank, hi, lo, kt, gain):
                dve.wait_ge(done, count)
                for kk in range(2):
                    ins = nc.vector.scalar_tensor_tensor(
                        lo[:, bass.ds(kt + kk, 1), :], misc[:, bank:bank + 1, kk * S:(kk + 1) * S],
                        gains[:, bass.ds(kt + (gain + kk), 1)], hi[:, bass.ds(kt + kk, 1), :].bitcast(F32),
                        ALU.mult, ALU.subtract)
                ins.then_inc(tr_lo, 1)

            def evacuate(n, q, dst):
                dve.wait_ge(acc_done, n + 1)
                nc.vector.tensor_copy(dst, acc[:, q, :, :]).then_inc(acc_free, 1)

            def transposed(q):
                return acc[:, q, :, :].rearrange("p b (c s) -> p (b c) s", s=S)

            def evacuate_T(n, q, dst):
                dve.wait_ge(acc_done, n + 1)
                nc.vector.tensor_copy(dst, transposed(q)).then_inc(acc_free, 1)

            dve.wait_ge(consts, 1)
            reciprocal_root(1, 4 * TT)
            nc.vector.tensor_scalar(normed[:, 0, :], h[:, 0, :], rstd[:, 0:1], None, ALU.mult).then_inc(normed_ready, 1)
            dve.wait_ge(gains_T, 1)
            nc.vector.tensor_copy(gains[:, :], misc[:, 3, 0:NG]).then_inc(gains_ready, 1)
            low_parts(0, 0)
            dve.wait_ge(wf_hi_done, 1)
            nc.vector.tensor_tensor(wf_lo[:, :, :], wf[:, :, :], wf_hi[:, :, :].bitcast(F32), ALU.subtract).then_inc(wf_ready, 1)
            dve.wait_ge(gains_ready, 1)
            for p in range(PAIRS):
                pair_lo(tr_hi, PAIR0["x"] + p + 1, p % 4, t1_hi, t1_lo, 2 * p, G_MIX)
            dve.wait_ge(inv_ready, 1)
            step(nc.vector.reciprocal(inv[:, :, :], inv[:, :, :]))
            with dve.Fori(0, T_IN // 2) as b:
                for q in range(2):
                    n = b * 2 + q
                    low_parts(n, 1)
                    low_parts(n + 1, 0)
                    evacuate_T(n, q, foxT[:, bass.ds(n * CT, CT), :])
            dve.wait_ge(f_done, TT)
            nc.vector.tensor_copy(fsb[:, :, :], misc[:, 0, 0:TT * FH].rearrange("p (t f) -> p t f", t=TT)).then_inc(f_copied, 1)

            def window_diff(g):
                src = foxT[:, g * GT:(g + 1) * GT, :]
                a, b = winA, winB
                step(nc.vector.tensor_copy(a[:, :, pad:], src))
                w = 1
                while w < WINDOWS[g]:
                    step(nc.vector.tensor_tensor(b[:, :, pad:], a[:, :, pad:], a[:, :, pad - w:pad - w + S], ALU.add))
                    a, b, w = b, a, 2 * w
                row = inv[:, g:g + 1, :].to_broadcast([P, GT, S])
                step(nc.vector.tensor_tensor(b[:, :, pad:], a[:, :, pad:], row, ALU.mult))
                nc.vector.tensor_tensor(diff[:, g * GT:(g + 1) * GT, :], b[:, :, pad:], src, ALU.subtract).then_inc(diff_ready, 1)
                dve.wait_ge(diff_ready, len(done_diffs) + 1)
                done_diffs.append(g)

            done_diffs = []
            step(nc.vector.memset(winA[:, :, 0:pad], 0.0))
            step(nc.vector.memset(winB[:, :, 0:pad], 0.0))
            window_diff(3)
            window_diff(2)
            low_parts(T_IN, 1)
            reciprocal_root(2, 2 * 4 * TT)
            nc.vector.tensor_scalar(normed[:, 0, :], normed[:, 0, :], rstd[:, 0:1], None, ALU.mult).then_inc(normed_ready, 1)
            low_parts(T_IN + 1, 0)
            evacuate(T_IN, 0, foxv[:, :, 0:CW])
            dve.wait_ge(fT_done, TT)
            step(nc.vector.tensor_scalar(fz[:, :], misc[0:FH, 1, 0:S], bf[:, 0:1], None, ALU.add))
            nc.vector.scalar_tensor_tensor(fa[:, :], fz[:, :], -1.0, fz[:, :], ALU.mult, ALU.max).then_inc(fa_ready, 1)
            dve.wait_ge(fa_ready, 1)
            step(nc.vector.tensor_scalar(fz[:, :], fz[:, :], 0.0, None, ALU.min))
            dve.wait_ge(fl_ready, 1)
            step(nc.vector.tensor_tensor(fz[:, :], fz[:, :], fe[:, :], ALU.subtract))
            step(nc.vector.tensor_tensor_scan(fa[:, :], fones[:, :], fz[:, :], 0.0, ALU.mult, ALU.add))
            nc.vector.tensor_scalar(cum[:, :], fa[:, :], 1.0 / FSCALE, None, ALU.mult).then_inc(cum_ready, 1)
            nc.vector.tensor_scalar(ncum[:, :], fa[:, :], -1.0 / FSCALE, None, ALU.mult).then_inc(cum_ready, 1)
            low_parts(T_IN + 1, 1)
            window_diff(1)
            window_diff(0)
            low_parts(T_IN + 2, 0)
            evacuate(T_IN + 1, 1, foxv[:, :, CW:2 * CW])
            dve.wait_ge(consts, 6)
            for f in range(FH):
                for t in range(TT):
                    u = f * TT + t
                    dve.wait_ge(qk_done, u + 1)
                    nc.vector.tensor_tensor_reduce(
                        out=foxs[:, f, t * P:(2 * t + 1) * P], in0=misc[:, u % 4, 0:(t + 1) * P], in1=mask[:, (1 - t) * P:2 * P],
                        scale=1.0, scalar=LOW, op0=ALU.add, op1=ALU.max, accum_out=fmax[:, f, t:t + 1]).then_inc(qk_read, 1)
            dve.wait_ge(qk_read, FH * TT)
            nc.vector.tensor_scalar(fneg[:, :, :], fmax[:, :, :], -FSCALE, None, ALU.mult).then_inc(fneg_ready, 1)
            for g in range(len(WINDOWS)):
                dve.wait_ge(tr_hi, PAIRS + g + 1)
                for dt in range(GT):
                    col = G_POOL + g * GT + dt
                    ins = nc.vector.scalar_tensor_tensor(
                        t1_lo[:, g * GT + dt, :], misc[:, g, dt * S:(dt + 1) * S], gains[:, col:col + 1],
                        t1_hi[:, g * GT + dt, :].bitcast(F32), ALU.mult, ALU.subtract)
                ins.then_inc(tr_lo, 1)
            for p in range(PAIRS):
                pair_lo(tr_hi, PAIRS + 4 + p + 1, p % 4, t2_hi, t2_lo, 2 * p, G_MEM)
            dve.wait_ge(fexp_done, FH * TT)
            step(nc.vector.reciprocal(frec[:, :, :], fsum[:, :, :]))
            for f in range(FH):
                for t in range(TT):
                    part = foxs[:, f, t * P:(2 * t + 1) * P]
                    ins = nc.vector.tensor_scalar(part, part, frec[:, f, t:t + 1], None, ALU.mult)
                ins.then_inc(fp_ready, 1)
            n0, items = ITEMS["k"]
            with dve.Fori(0, items // 2) as b:
                for q in range(2):
                    i = b * 2 + q
                    low_parts(i + n0, 1)
                    low_parts(i + (n0 + 1), 0)
                    evacuate_T(i + n0, q, memk[:, bass.ds(i * CT, CT), :])
            for f in range(FH + 1):
                if f < FH:
                    dve.wait_ge(pT_done, f + 1)
                    nc.vector.tensor_copy(pT[:, f % 2, :], misc[:, f % 2, 0:3 * P]).then_inc(pT_copied, 1)
                if f:
                    dve.wait_ge(fo_hi, f)
                    kt = PW // P + f - 1
                    nc.vector.tensor_tensor(t1_lo[:, kt, :], misc[:, 2 + (f - 1) % 2, 0:S], t1_hi[:, kt, :].bitcast(F32),
                                            ALU.subtract).then_inc(fo_lo, 1)
            n0, items = ITEMS["v"]
            with dve.Fori(0, items // 2) as b:
                for q in range(2):
                    i = b * 2 + q
                    low_parts(i + n0, 1)
                    low_parts(i + (n0 + 1), 0)
                    evacuate(i + n0, q, memv[:, :, bass.ds(i * CW, CW)])

            def residual_items(name, hi, lo, gain, pair0):
                n0, items = ITEMS[name]
                with dve.Fori(0, items // 2) as b:
                    for q in range(2):
                        i = b * 2 + q
                        low_parts(i + n0, 1)
                        if q:
                            for p in range(2):
                                pair_lo(tr_hi, b * 4 + (pair0 + 4 + p + 1), p, hi, lo, b * 8 + 2 * p, gain)
                        low_parts(i + (n0 + 1), 0)
                        dve.wait_ge(acc_done, i + (n0 + 1))
                        nc.vector.tensor_tensor(hs[:, q, :, :], acc[:, q, :, :], h[:, :, bass.ds(i * CW, CW)],
                                                ALU.add).then_inc(acc_free, 1)
                    for p in range(2):
                        pair_lo(tr_hi, b * 4 + (pair0 + 4 + 2 + p + 1), 2 + p, hi, lo, b * 8 + (4 + 2 * p), gain)

            residual_items("out", t2_hi, t2_lo, G_X, PAIR0["h1"])
            reciprocal_root(3, 3 * 4 * TT)
            step(nc.vector.tensor_scalar(xfac[:, :], rstd[:, :], XSCALE, None, ALU.mult))
            n0, items = ITEMS["q"]

            def x_softmax(i, q):
                for t in range(TT):
                    dve.wait_ge(xs_done, i * TT + (t + 1))
                    step(nc.vector.tensor_reduce(xmax[:, q, t:t + 1], misc[:, 2 * q + t, 0:S], AX.X, ALU.max))
                    nc.vector.tensor_scalar(xneg[:, q, t:t + 1], xmax[:, q, t:t + 1], xfac[:, t:t + 1], -1.0,
                                            ALU.mult, ALU.mult).then_inc(xneg_ready, 1)
                for t in range(TT):
                    dve.wait_ge(xexp_done, i * TT + (t + 1))
                    step(nc.vector.reciprocal(xrec[:, q, t:t + 1], xsum[:, q, t:t + 1]))
                    nc.vector.tensor_scalar(xp[:, bass.ds(i, 1), t, :], xp[:, bass.ds(i, 1), t, :], xrec[:, q, t:t + 1], None,
                                            ALU.mult).then_inc(xp_ready, 1)

            with dve.Fori(0, items // 2) as b:
                step.enter(b, 8)
                low_parts(b * 2 + n0, 1)
                low_parts(b * 2 + (n0 + 1), 0)
                evacuate_T(b * 2 + n0, 0, qs[:, 0, :, :])
                low_parts(b * 2 + (n0 + 1), 1)
                x_softmax(b * 2, 0)
                low_parts(b * 2 + (n0 + 2), 0)
                evacuate_T(b * 2 + (n0 + 1), 1, qs[:, 1, :, :])
                x_softmax(b * 2 + 1, 1)
            step.leave(items // 2)
            for hd in range(XH + 1):
                if hd < XH:
                    dve.wait_ge(xpT_done, hd + 1)
                    nc.vector.tensor_copy(xpT[:, hd, :, :], misc[:, hd % 2, :].rearrange("p (m s) -> p m s", m=TT)).then_inc(xpT_copied, 1)
                if hd:
                    for u in (2 * hd - 2, 2 * hd - 1):
                        dve.wait_ge(xo_hi, u + 1)
                        nc.vector.tensor_tensor(t1_lo[:, 2 * u:2 * u + 2, :], misc[:, 2 + u % 2, :].rearrange("p (a s) -> p a s", a=2),
                                                t1_hi[:, 2 * u:2 * u + 2, :].bitcast(F32), ALU.subtract).then_inc(xo_lo, 1)
            residual_items("o", t2_hi, t2_lo, G_PEER, PAIR0["h2"])
            for p in range(4):
                dve.wait_ge(skT_done, p + 1)
                nc.vector.tensor_copy(skT[:, 4 * p:4 * p + 4, :], misc[:, p, :].rearrange("p (a s) -> p a s", a=4)).then_inc(skT_copied, 1)
            reciprocal_root(4, 4 * 4 * TT)
            dve.wait_ge(pgain_landed, 16)
            dve.wait_ge(h_copied, 8)
            for t in range(TT):
                step(nc.vector.scalar_tensor_tensor(hn[:, t, :], h[:, t, :], rstd[:, t:t + 1], peer_gain[:, :], ALU.mult, ALU.mult))

            def peer_scores(i, q):
                for t in range(TT):
                    dve.wait_ge(ps_done, i * TT + (t + 1))
                    ins = nc.vector.tensor_scalar(scores[:, t, bass.ds(i * CW, CW)], misc[:, 2 * q + t, :], rstd[:, t:t + 1], None, ALU.mult)
                ins.then_inc(scores_ready, 1)

            def peer_items(b, last=False):
                n0, _ = ITEMS["peer"]
                low_parts(b * 2 + n0, 1)
                low_parts(b * 2 + (n0 + 1), 0)
                evacuate_T(b * 2 + n0, 0, pq[:, 0, :, :])
                low_parts(b * 2 + (n0 + 1), 1)
                peer_scores(b * 2, 0)
                if not last:
                    low_parts(b * 2 + (n0 + 2), 0)
                evacuate_T(b * 2 + (n0 + 1), 1, pq[:, 1, :, :])
                peer_scores(b * 2 + 1, 1)

            n0, items = ITEMS["peer"]
            for b in range(items // 2):
                peer_items(b, last=b == items // 2 - 1)
            dve.wait_ge(scores_ready, items)

            def top16(values, left, maxima, places):
                step(nc.vector.max(maxima[:, 0:8], values), apart=True)
                nc.vector.max_index(places[:, 0:8], maxima[:, 0:8], values)
                step(nc.vector.match_replace(left, maxima[:, 0:8], values, LOW), apart=True)
                step(nc.vector.max(maxima[:, 8:16], left), apart=True)
                step(nc.vector.max_index(places[:, 8:16], maxima[:, 8:16], left), apart=True)

            def route(g, q, c, head):
                step(nc.vector.tensor_copy(cur[:, :, :], scores[:, c, bass.ds(head * (2 * KEYS), 2 * KEYS)].rearrange("p (a k) -> p a k", a=2)),
                     apart=True)
                for a in range(2):
                    top16(cur[:, a, :], rest[:, a, :], top[:, a, :], top_at[:, a, :])
                step(nc.vector.tensor_tensor(cand[:, :, :], top[:, 0, :].unsqueeze(2).to_broadcast([P, TOP, TOP]),
                                             top[:, 1, :].unsqueeze(1).to_broadcast([P, TOP, TOP]), ALU.add), apart=True)
                top16(cand[:, :, :].rearrange("p a b -> p (a b)"), cand_rest[:, :, :].rearrange("p a b -> p (a b)"), best, pos)
                nc.vector.tensor_scalar(neg_best[:, :], best[:, 0:1], -1.0, None, ALU.mult).then_inc(nbest_ready, 1)
                nc.vector.tensor_scalar(ab[:, 0, :], pos[:, :], 4, None, ALU.logical_shift_right)
                step(nc.vector.tensor_scalar(ab[:, 1, :], pos[:, :], TOP - 1, None, ALU.bitwise_and))
                step(nc.vector.tensor_tensor(hot[:, :, :, :].rearrange("p a k i -> p (a k) i"),
                                             ab[:, :, :].rearrange("p a k -> p (a k)").unsqueeze(2).to_broadcast([P, 2 * TOP, TOP]),
                                             iota[:, :].unsqueeze(1).to_broadcast([P, 2 * TOP, TOP]), ALU.is_equal))
                step(nc.vector.tensor_tensor(hot[:, :, :, :], hot[:, :, :, :],
                                             top_at[:, :, :].unsqueeze(2).to_broadcast([P, 2, TOP, TOP]), ALU.mult))
                step(nc.vector.tensor_reduce(picked[:, :, :], hot[:, :, :, :], AX.X, ALU.add))
                nc.vector.scalar_tensor_tensor(idx_u[:, q, :], picked[:, 0, :], float(KEYS), picked[:, 1, :],
                                               ALU.mult, ALU.add).then_inc(routed, 1)
                dve.wait_ge(gexp_done, g + 1)
                step(nc.vector.reciprocal(exp_rec[:, :], exp_sum[:, :]))
                step(nc.vector.tensor_scalar(gate[:, q, :], exps[:, :], exp_rec[:, 0:1], None, ALU.mult))

            ROUTE_STEPS = 1 + 2 * 4 + 1 + 4 + 1 + 3 + 2

            def weights(g, q, fresh=False):
                dve.wait_ge(gelu_done, g + 1)
                if not fresh:
                    dve.wait_ge(diag_ready, g * TOP - (TOP - 1))
                nc.vector.tensor_tensor(wts[:, q, :], acts[:, q, :], gate[:, q, :], ALU.mult).then_inc(wts_ready, 1)

            def period(g, q, c, next_c, next_head, first=False, second=False, last=False):
                if not (first or second):
                    for s in range(4):
                        dve.wait_ge(v_landed[s], g * (16 * TOP // 4) - 16 * TOP // 4)
                dve.wait_ge(routed, g + 1)
                nc.vector.tensor_copy(idx_v[:, q, :], idx_u[:, q, :]).then_inc(idx_v_ready, 1)
                if not first:
                    weights(g - 1, 1 - q, fresh=second)
                    dve.wait_ge(wts_ready, g)
                if not last:
                    route(g + 1, 1 - q, next_c, next_head)
                for k in range(TOP):
                    dve.wait_ge(u_landed[k % 4], g * (16 * TOP // 4) + 16 * (k // 4 + 1))
                    if not (first and k < 2):
                        dve.wait_ge(dot_done, g * TOP + (k - 1))
                    nc.vector.tensor_tensor_reduce(out=product[:, k % 2, :], in0=u_ring[:, k % 4, :], in1=hn[:, c, :], scale=1.0, scalar=0.0,
                                                   op0=ALU.mult, op1=ALU.add, accum_out=dots[:, q, k:k + 1]).then_inc(dot_done, 1)

            def finish(c):
                dve.wait_ge(y_done, c + 1)
                bank = misc[:, :, :] if c == 0 else acc[:, :, :, :].rearrange("p a b n -> p (a b) n")
                nc.vector.tensor_tensor(y_sum[:, c, :].rearrange("p (b n) -> p b n", n=CW), bank,
                                        h[:, c, :].rearrange("p (b n) -> p b n", n=CW), ALU.add).then_inc(y_added, 1)
                dve.wait_ge(y_squared, 4 * (c + 1))
                step(nc.vector.tensor_reduce(ss[:, c:c + 1], sq[:, c, :], AX.X, ALU.add))
                nc.vector.tensor_scalar(ss[:, c:c + 1], ss[:, c:c + 1], 1.0 / D, EPS, ALU.mult, ALU.add).then_inc(y_var, 1)
                dve.wait_ge(y_root, c + 1)
                step(nc.vector.reciprocal(rstd[:, c:c + 1], rt[:, c:c + 1]))
                dve.wait_ge(fgain_landed, 16)
                nc.vector.scalar_tensor_tensor(y_out[:, c, :], y_sum[:, c, :], rstd[:, c:c + 1], final_gain[:, :],
                                               ALU.mult, ALU.mult).then_inc(y_ready, 1)

            def two_periods(b, c, next_c, **kw):
                g0 = b * 2
                head = g0 - c * PH
                period(g0, 0, c, c, head + 1, **{k: v for k, v in kw.items() if k == "first"})
                last = bool(kw.get("last"))
                period(g0 + 1, 1, c, next_c, (head + 2) if next_c == c else 0, second=bool(kw.get("first")), last=last)

            route(0, 0, 0, 0)
            HB = PH // 2
            two_periods(0, 0, 0, first=True)
            with dve.Fori(0, HB - 2) as i:
                step.enter(i, 2 * ROUTE_STEPS)
                two_periods(i + 1, 0, 0)
            step.leave(HB - 2)
            two_periods(HB - 1, 0, 1)
            with dve.Fori(0, HB - 1) as i:
                step.enter(i, 2 * ROUTE_STEPS)
                two_periods(i + HB, 1, 1)
            step.leave(HB - 1)
            finish(0)
            two_periods(2 * HB - 1, 1, 1, last=True)
            weights(GROUPS - 1, 1)
            finish(1)

        @block.tensor
        def _(pe):
            def chunk_ready(n, j):
                pe.wait_ge((lo_even, lo_odd)[j % 2], n * HALF + (j // 2 + 1))

            def products(n, q, hi, lo, turned, between=None, fresh=False):
                if not fresh:
                    pe.wait_ge(acc_free, n - 1)
                for j in range(CH):
                    chunk_ready(n, j)
                    s = j % RING
                    for kk in range(KC):
                        kt = j * KC + kk
                        first, last = kt == 0, kt == KT - 1
                        if turned:
                            for ct in range(CT):
                                o = acc[:, q, ct // 2, ct % 2 * S:(ct % 2 + 1) * S]
                                wh, wl = (w[:, s, kk, ct * P:(ct + 1) * P] for w in (w_hi, w_lo))
                                nc.tensor.matmul(o, wh, hi[:, kt, :], start=first and ct % 2 == 0, stop=False, skip_group_check=True)
                                nc.tensor.matmul(o, wh, lo[:, kt, :], start=False, stop=False, skip_group_check=True)
                                ins = nc.tensor.matmul(o, wl, hi[:, kt, :], start=False, stop=last and ct % 2 == 1, skip_group_check=True)
                        else:
                            for t in range(TT):
                                o = acc[:, q, t, :]
                                xh, xl = (a[:, kt, t * P:(t + 1) * P] for a in (hi, lo))
                                nc.tensor.matmul(o, xh, w_hi[:, s, kk, :], start=first, stop=False)
                                nc.tensor.matmul(o, xh, w_lo[:, s, kk, :], start=False, stop=False)
                                ins = nc.tensor.matmul(o, xl, w_hi[:, s, kk, :], start=False, stop=last)
                    ins.then_inc(chunk_used, 1)
                    if j == HALF - 1 and between is not None:
                        between()
                pe.wait_ge(chunk_used, n * CH + CH)
                pe.sem_inc(acc_done, 1)

            def transposes(pair, bank, src, free=None, count=0):
                if free is not None:
                    pe.wait_ge(free, count)
                for kk in range(2):
                    for t in range(TT):
                        ins = nc.tensor.transpose(misc[:, bank, kk * S + t * P:kk * S + (t + 1) * P], src(t, kk), ident[:, :])
                ins.then_inc(tr_ready, 1)

            pe.wait_ge(consts, 1)
            pe.wait_ge(small_landed, 16 * 7)
            nc.tensor.transpose(misc[:, 3, 0:NG], gain_rows[:, :], ident[0:NG, 0:NG]).then_inc(gains_T, 1)
            pe.wait_ge(normed_ready, 2)
            pe.wait_ge(gains_ready, 1)
            for p in range(PAIRS):
                transposes(p, p % 4, lambda t, kk: normed[:, t, (2 * p + kk) * P:(2 * p + kk + 1) * P],
                           tr_lo if p >= 4 else None, p - 3)
            pe.wait_ge(tr_lo, PAIRS)
            products(0, 0, t1_hi, t1_lo, True, fresh=True)
            products(1, 1, t1_hi, t1_lo, True, fresh=True)
            with pe.Fori(1, T_IN // 2) as b:
                for q in range(2):
                    products(b * 2 + q, q, t1_hi, t1_lo, True)
            pe.wait_ge(wf_ready, 1)
            for t in range(TT):
                o = misc[:, 0, t * FH:(t + 1) * FH]
                for kt in range(KT):
                    xh, xl = (a[:, kt, t * P:(t + 1) * P] for a in (t1_hi, t1_lo))
                    nc.tensor.matmul(o, xh, wf_hi[:, kt, :], start=kt == 0, stop=False)
                    nc.tensor.matmul(o, xh, wf_lo[:, kt, :], start=False, stop=False)
                    ins = nc.tensor.matmul(o, xl, wf_hi[:, kt, :], start=False, stop=kt == KT - 1)
                ins.then_inc(f_done, 1)
            products(T_IN, 0, t1_hi, t1_lo, False)
            pe.wait_ge(f_copied, 1)
            for t in range(TT):
                nc.tensor.transpose(misc[0:FH, 1, t * P:(t + 1) * P], fsb[:, t, :], ident[:, :]).then_inc(fT_done, 1)
            products(T_IN + 1, 1, t1_hi, t1_lo, False)
            pe.wait_ge(cum_ready, 2)
            pe.wait_ge(consts, 6)
            for f in range(FH):
                for t in range(TT):
                    u = f * TT + t
                    if u >= 4:
                        pe.wait_ge(qk_read, u - 3)
                    keys = (t + 1) * P
                    o = misc[:, u % 4, 0:keys]
                    nc.tensor.matmul(o, foxT[:, PW // P + f, t * P:(t + 1) * P], foxT[:, PW // P + FH + f, 0:keys], start=True, stop=False)
                    nc.tensor.matmul(o, cum[:, t * P:(t + 1) * P], sel[:, f, 0:keys], start=False, stop=False)
                    nc.tensor.matmul(o, sel[:, f, 0:P], ncum[:, 0:keys], start=False, stop=True).then_inc(qk_done, 1)
            pe.wait_ge(qk_read, FH * TT)
            pe.wait_ge(diff_ready, len(WINDOWS))
            pe.wait_ge(pool_landed, 16)
            for g in range(len(WINDOWS)):
                for dt in range(GT):
                    for ct in range(GT):
                        ins = nc.tensor.matmul(misc[:, g, dt * S:(dt + 1) * S], poolw[:, g, ct, dt * P:(dt + 1) * P],
                                               diff[:, g * GT + ct, :], start=ct == 0, stop=ct == GT - 1)
                ins.then_inc(poolT_done, 1)
            pe.wait_ge(normed_ready, 4)
            for p in range(PAIRS):
                transposes(PAIRS + p, p % 4, lambda t, kk: normed[:, t, (2 * p + kk) * P:(2 * p + kk + 1) * P], tr_lo, PAIRS + p + 1)
            pe.wait_ge(tr_lo, 2 * PAIRS + 4)
            n0, items = ITEMS["k"]
            with pe.Fori(0, items // 2) as b:
                for q in range(2):
                    products(b * 2 + (n0 + q), q, t2_hi, t2_lo, True)
            pe.wait_ge(fp_ready, FH)
            for f in range(FH + 1):
                if f < FH:
                    if f >= 2:
                        pe.wait_ge(pT_copied, f - 1)
                    b = f % 2
                    nc.tensor.transpose(misc[:, b, 0:P], foxs[:, f, 0:P], ident[:, :])
                    nc.tensor.transpose(misc[:, b, P:2 * P], foxs[:, f, P:2 * P], ident[:, :])
                    nc.tensor.transpose(misc[:, b, 2 * P:3 * P], foxs[:, f, 2 * P:3 * P], ident[:, :]).then_inc(pT_done, 1)
                if f:
                    e = f - 1
                    pe.wait_ge(pT_copied, e + 1)
                    if e >= 2:
                        pe.wait_ge(fo_lo, e - 1)
                    o = misc[:, 2 + e % 2, 0:S]
                    nc.tensor.matmul(o, foxv[:, 0, e * P:(e + 1) * P], pT[:, e % 2, 0:2 * P], start=True, stop=False)
                    nc.tensor.matmul(misc[:, 2 + e % 2, P:S], foxv[:, 1, e * P:(e + 1) * P], pT[:, e % 2, 2 * P:3 * P],
                                     start=False, stop=True).then_inc(fo_done, 1)
            n0, items = ITEMS["v"]
            with pe.Fori(0, items // 2) as b:
                for q in range(2):
                    products(b * 2 + (n0 + q), q, t2_hi, t2_lo, False)
            pe.wait_ge(fo_lo, FH)

            def residual_items(name, hi, lo, pair0):
                n0, items = ITEMS[name]
                with pe.Fori(0, items // 2) as b:
                    def turn(q):
                        pe.wait_ge(acc_free, b * 2 + (n0 + q + 1))
                        for p in range(2):
                            transposes(None, 2 * q + p, lambda t, kk: hs[:, q, t, (2 * p + kk) * P:(2 * p + kk + 1) * P],
                                       tr_lo, b * 4 + (pair0 + 4 + 2 * q + p + 1 - 4))
                    products(b * 2 + n0, 0, hi, lo, False)
                    products(b * 2 + (n0 + 1), 1, hi, lo, False, between=lambda: turn(0))
                    turn(1)
                pe.wait_ge(tr_lo, pair0 + 4 + PAIRS)

            residual_items("out", t1_hi, t1_lo, PAIR0["h1"])
            n0, items = ITEMS["q"]
            with pe.Fori(0, items // 2) as b:
                def x_scores(q):
                    i = b * 2 + q
                    pe.wait_ge(acc_free, i + (n0 + 1))
                    for t in range(TT):
                        for c in range(XT):
                            ins = nc.tensor.matmul(misc[:, 2 * q + t, 0:S], qs[:, q, c, t * P:(t + 1) * P],
                                                   memk[:, bass.ds(i * XT + c, 1), :], start=c == 0, stop=c == XT - 1)
                        ins.then_inc(xs_done, 1)
                products(b * 2 + n0, 0, t2_hi, t2_lo, True)
                products(b * 2 + (n0 + 1), 1, t2_hi, t2_lo, True, between=lambda: x_scores(0))
                x_scores(1)
                pe.wait_ge(xexp_done, b * 4 + 4)
            for hd in range(XH + 1):
                if hd < XH:
                    pe.wait_ge(xp_ready, TT * (hd + 1))
                    if hd >= 2:
                        pe.wait_ge(xpT_copied, hd - 1)
                    for m in range(TT):
                        for t in range(TT):
                            ins = nc.tensor.transpose(misc[:, hd % 2, m * S + t * P:m * S + (t + 1) * P],
                                                      xp[:, hd, t, m * P:(m + 1) * P], ident[:, :])
                    ins.then_inc(xpT_done, 1)
                if hd:
                    e = hd - 1
                    pe.wait_ge(xpT_copied, e + 1)
                    for half in range(2):
                        u = 2 * e + half
                        if u >= 2:
                            pe.wait_ge(xo_lo, u - 1)
                        for d2 in range(2):
                            dt = e * XT + half * 2 + d2
                            for m in range(TT):
                                ins = nc.tensor.matmul(misc[:, 2 + u % 2, d2 * S:(d2 + 1) * S], memv[:, m, dt * P:(dt + 1) * P],
                                                       xpT[:, e, m, :], start=m == 0, stop=m == TT - 1)
                        ins.then_inc(xo_done, 1)
            pe.wait_ge(xo_lo, 2 * XH)
            residual_items("o", t1_hi, t1_lo, PAIR0["h2"])
            pe.wait_ge(sk_landed, 16)
            for p in range(4):
                for a in range(4):
                    ins = nc.tensor.transpose(misc[:, p, a * P:(a + 1) * P], skraw[:, 4 * p + a, :], ident[:, :])
                ins.then_inc(skT_done, 1)
            pe.wait_ge(skT_copied, 4)
            n0, items = ITEMS["peer"]
            with pe.Fori(0, items // 2) as b:
                def p_scores(q):
                    i = b * 2 + q
                    pe.wait_ge(acc_free, i + (n0 + 1))
                    for t in range(TT):
                        for c in range(CT):
                            ins = nc.tensor.matmul(misc[:, 2 * q + t, c * KEYS:(c + 1) * KEYS], pq[:, q, c, t * P:(t + 1) * P],
                                                   skT[:, bass.ds(i * CT + c, 1), :], start=True, stop=True)
                        ins.then_inc(ps_done, 1)
                products(b * 2 + n0, 0, t2_hi, t2_lo, True)
                products(b * 2 + (n0 + 1), 1, t2_hi, t2_lo, True, between=lambda: p_scores(0))
                p_scores(1)
                pe.wait_ge(scores_ready, b * 2 + 2)
            for c in range(TT):
                banks = [misc[:, n, :] for n in range(4)] if c == 0 else [acc[:, n // 2, n % 2, :] for n in range(4)]
                for o in banks:
                    nc.tensor.matmul(o, zeros[:, 0:P], zeros[:, :], start=True, stop=False)
                with pe.Fori(c * PH, (c + 1) * PH) as g:
                    for k in range(TOP):
                        pe.wait_ge(v_landed[k % 4], g * (16 * TOP // 4) + 16 * (k // 4 + 1))
                        pe.wait_ge(diag_ready, g * TOP + (k + 1))
                        for n, o in enumerate(banks):
                            ins = nc.tensor.matmul(o, diag[:, k % 4, :], v_ring[:, k % 4, n * CW:(n + 1) * CW], start=False, stop=False)
                        ins.then_inc(v_used, 1)
                for o in banks:
                    ins = nc.tensor.matmul(o, zeros[:, 0:P], zeros[:, :], start=False, stop=True)
                ins.then_inc(y_done, 1)


_INS = ['x', 'mem', 'mix_norm', 'w_in', 'b_forget', 'pool_w', 'pool_scale', 'w_out', 'xattn_norm', 'mem_norm', 'xattn_wq',
        'xattn_wk', 'xattn_wv', 'xattn_wo', 'peer_norm', 'peer_wq', 'peer_sub_keys', 'peer_u', 'peer_v', 'final_norm']
_OUTS = [((1, 256, 2048), 'float32')]


def kernel(**inputs):
    import numpy as _np
    import concourse.bacc as _bacc
    from concourse import mybir as _mybir
    from concourse.bass_utils import run_bass_kernel_spmd as _run

    nc = _bacc.Bacc("TRN2", target_bir_lowering=False, num_devices=1)
    arrays, args = {}, []
    for name in _INS:
        a = _np.ascontiguousarray(inputs[name])
        arrays[f"in_{name}_dram"] = a
        args.append(nc.dram_tensor(f"in_{name}_dram", a.shape, _mybir.dt.from_np(a.dtype), kind="ExternalInput").ap())
    for i, (shape, dtype) in enumerate(_OUTS):
        dt = _mybir.dt.from_np(_np.dtype(dtype))
        args.append(nc.dram_tensor(f"out_{i}_dram", shape, dt, kind="ExternalOutput").ap())
    hybrid_layer(nc, *args)
    r = _run(nc, [arrays], core_ids=[0])
    return r.results[0]["out_0_dram"]
```

```python
import concourse.bass as bass
from concourse import mybir
from contextlib import ExitStack


class Steps:

    def __init__(self, engine, semaphore, passed=None):
        self.engine, self.semaphore, self.passed, self.n = engine, semaphore, passed, 0

    def __call__(self, instruction, apart=False):
        instruction.then_inc(self.semaphore, 1)
        self.n, self.steps = self.n + 1, self.steps + 1
        self.engine.wait_ge(self.semaphore, self.n)
        if apart:
            self.engine.sem_inc(self.passed, 1)

    steps = 0

    def enter(self, i, per_turn):
        self.start, self.steps, self.per_turn = self.n, 0, per_turn
        self.n = i * per_turn + self.start

    def leave(self, turns):
        assert self.steps == self.per_turn, (self.steps, self.per_turn)
        self.n = self.start + turns * self.per_turn



def hybrid_layer(
    nc: bass.Bass, x, mem, mix_norm, w_in, b_forget, pool_w, pool_scale, w_out, xattn_norm, mem_norm,
    xattn_wq, xattn_wk, xattn_wv, xattn_wo, peer_norm, peer_wq, peer_sub_keys, peer_u, peer_v,
    final_norm, out,
):
    F32, F32R, BF16, U32 = mybir.dt.float32, mybir.dt.float32r, mybir.dt.bfloat16, mybir.dt.uint32
    ALU, ACT, AX = mybir.AluOpType, mybir.ActivationFunctionType, mybir.AxisListType

    P = 128
    S, D = x.shape[1], x.shape[2]
    TT = S // P
    KT = D // P
    PW = pool_scale.shape[1]
    FH = b_forget.shape[1]
    FD = (D - PW) // FH
    WINDOWS = (2, 4, 8, 16)
    GT = PW // len(WINDOWS) // P
    XH = 4
    XT = D // XH // P
    XSCALE, FSCALE = float(D // XH) ** -0.5, float(FD) ** -0.5
    PH = peer_sub_keys.shape[1]
    KEYS = peer_sub_keys.shape[3]
    TOP = 16
    EPS = 1e-6
    LOW, MASKED = -3.0e38, -1.0e30
    assert TT == 2 and FD == P and XT == 4 and KEYS == P and S == mem.shape[1]

    CW, KC = 512, 2
    CH = KT // KC
    RING = 4
    HALF = CH // 2
    CT = CW // P
    assert HALF == RING
    ITEMS = {}
    at = 0
    for name, cols in (("in", PW + 3 * (D - PW)), ("k", D), ("v", D), ("out", D), ("q", D), ("o", D), ("peer", D)):
        ITEMS[name] = (at, cols // CW)
        at += cols // CW
    LAST = at - 1
    T_IN = (PW + 2 * (D - PW)) // CW
    GROUPS = TT * PH

    def rows(w):
        return w.rearrange("o (k p) n -> p (o k) n", p=P)

    base = 16512
    KB = 1024
    at_h, at_t1, at_t2 = base, base + 16 * KB, base + 48 * KB
    at_k, at_v, at_f = base + 80 * KB, base + 96 * KB, base + 120 * KB
    at_raw, at_split, at_small = base + 140 * KB, base + 156 * KB, base + 188 * KB
    small = [at_small]

    def put(name, shape, dt, offset=None):
        size = 4 if dt != BF16 else 2
        for n in shape[1:]:
            size *= n
        if offset is None:
            offset, small[0] = small[0], small[0] + (size + 31) // 32 * 32
        return nc.alloc_sbuf_tensor_at(name, shape, dt, offset=offset)

    h = put("h", [P, TT, D], F32, at_h)
    t1_hi, t1_lo = put("t1_hi", [P, KT, S], F32R, at_t1), put("t1_lo", [P, KT, S], F32R, at_t1 + 16 * KB)
    t2_hi, t2_lo = put("t2_hi", [P, KT, S], F32R, at_t2), put("t2_lo", [P, KT, S], F32R, at_t2 + 16 * KB)
    raw = put("raw", [P, RING, KC, CW], F32, at_raw)
    w_hi = put("w_hi", [P, RING, KC, CW], F32R, at_split)
    w_lo = put("w_lo", [P, RING, KC, CW], F32R, at_split + 16 * KB)
    poolw = put("poolw", [P, len(WINDOWS), GT, GT * P], F32, at_t2)
    inv = put("inv", [P, len(WINDOWS), S], F32, at_t2 + 8 * KB)
    diff = put("diff", [P, len(WINDOWS) * GT, S], F32, at_t2 + 12 * KB)
    sel = put("sel", [FH, FH, P], F32, at_t2 + 20 * KB)
    sel_r = put("sel_r", [FH, FH, P], F32R, at_t2 + 24 * KB)
    cum = put("cum", [FH, S], F32, at_t2 + 28 * KB)
    cum_hi = put("cum_hi", [FH, S], F32R, at_t2 + 29 * KB)
    cum_lo = put("cum_lo", [FH, S], F32R, at_t2 + 30 * KB)
    wf = put("wf", [P, KT, FH], F32, at_t2 + 31 * KB)
    wf_hi = put("wf_hi", [P, KT, P], F32R, at_f)
    wf_lo = put("wf_lo", [P, KT, P], F32R, at_f + 8 * KB)
    normed = put("normed", [P, TT, D], F32, at_k)
    memk = put("memk", [P, KT, S], F32, at_k)
    hn = put("hn", [P, TT, D], F32, at_k)
    foxT = put("foxT", [P, PW // P + 2 * FH, S], F32, at_v)
    memv = put("memv", [P, TT, D], F32, at_v)
    peer_gain = put("peer_gain", [P, D], F32, at_v)
    scores = put("scores", [P, TT, PH * 2 * KEYS], F32, at_v)
    skT = put("skT", [P, PH * 2, KEYS], F32, at_v + 16 * KB)
    foxv = put("foxv", [P, TT, FH * P], F32, at_f)
    foxs = put("foxs", [P, FH, 3 * P], F32, at_f + 8 * KB)
    pad = 16
    winA = put("winA", [P, GT, pad + S], F32, at_f + 8 * KB)
    winB = put("winB", [P, GT, pad + S], F32, at_f + 8 * KB + 2304)
    fz, fa, fe, fones = (put(n, [FH, S], F32, at_f + (16 + k) * KB) for k, n in enumerate(("fz", "fa", "fe", "fones")))
    hs = put("hs", [P, 2, TT, CW], F32, at_f)
    qs = put("qs", [P, 2, XT, S], F32, at_f)
    xp = put("xp", [P, XH, TT, S], F32, at_f + 8 * KB)
    xpT = put("xpT", [P, 2, TT, S], F32, at_f)
    skraw = put("skraw", [P, PH * 2, P], F32, at_f + 8 * KB)
    pq = put("pq", [P, 2, CT, S], F32, at_f)
    u_ring = put("u_ring", [P, 4, D], F32, at_t1)
    v_ring = put("v_ring", [P, 4, D], F32, at_split)
    final_gain = put("final_gain", [P, D], F32, at_raw)
    product = put("product", [P, D], BF16, at_f + 16 * KB)
    y_sum = put("y_sum", [P, TT, D], F32, at_t2)
    y_out = put("y_out", [P, TT, D], F32, at_t2 + 16 * KB)
    ident = put("ident", [P, P], F32)
    mask = put("mask", [P, 2 * P], F32)
    zeros = put("zeros", [P, CW], BF16)
    junk = put("junk", [P, 2, CW], BF16)
    NG = 4 * KT + PW // P
    gain_rows = put("gain_rows", [NG, P], F32)
    gains = put("gains", [P, NG], F32)
    G_MIX, G_MEM, G_X, G_PEER, G_POOL = 0, KT, 2 * KT, 3 * KT, 4 * KT
    bf = put("bf", [FH, 1], F32)
    warm = put("warm", [P, 1], F32)
    sq = put("sq", [P, TT, 4], F32)
    ss = put("ss", [P, TT], F32)
    rt = put("rt", [P, TT], F32)
    rstd = put("rstd", [P, TT], F32)
    xfac = put("xfac", [P, TT], F32)
    fmax = put("fmax", [P, FH, TT], F32)
    fneg = put("fneg", [P, FH, TT], F32)
    fsum = put("fsum", [P, FH, TT], F32)
    frec = put("frec", [P, FH, TT], F32)
    pT = put("pT", [P, 2, 3 * P], F32)
    xmax = put("xmax", [P, 2, TT], F32)
    xneg = put("xneg", [P, 2, TT], F32)
    xsum = put("xsum", [P, 2, TT], F32)
    xrec = put("xrec", [P, 2, TT], F32)
    cur = put("cur", [P, 2, KEYS], F32, at_f + 8 * KB)
    rest = put("rest", [P, 2, KEYS], F32, at_f + 9 * KB)
    top = put("top", [P, 2, TOP], F32)
    top_at = put("top_at", [P, 2, TOP], U32)
    cand = put("cand", [P, TOP, TOP], F32, at_f + 10 * KB)
    cand_rest = put("cand_rest", [P, TOP, TOP], F32, at_f + 11 * KB)
    best = put("best", [P, TOP], F32)
    pos = put("pos", [P, TOP], U32)
    ab = put("ab", [P, 2, TOP], U32)
    hot = put("hot", [P, 2, TOP, TOP], F32, at_f + 12 * KB)
    picked = put("picked", [P, 2, TOP], F32)
    iota = put("iota", [P, TOP], F32)
    neg_best = put("neg_best", [P, 1], F32)
    exps = put("exps", [P, TOP], F32)
    exp_sum = put("exp_sum", [P, 1], F32)
    exp_rec = put("exp_rec", [P, 1], F32)
    gate = put("gate", [P, 2, TOP], F32)
    idx_u = put("idx_u", [P, 2, TOP], U32)
    idx_v = put("idx_v", [P, 2, TOP], U32)
    dots = put("dots", [P, 2, TOP], F32)
    acts = put("acts", [P, 2, TOP], F32)
    wts = put("wts", [P, 2, TOP], F32)
    diag = put("diag", [P, 4, P], F32, at_f + 14 * KB)
    assert small[0] <= 229344, small[0]

    w_in_r, w_k_r, w_v_r, w_out_r = rows(w_in), rows(xattn_wk), rows(xattn_wv), rows(w_out)
    w_q_r, w_o_r, w_peer_r = rows(xattn_wq), rows(xattn_wo), rows(peer_wq)
    u_rows, v_rows = peer_u.rearrange("o n d -> (o n) d"), peer_v.rearrange("o n d -> (o n) d")

    with ExitStack() as ctx:
        acc = ctx.enter_context(nc.psum_tensor("acc", [P, 2, 2, CW], F32))
        misc = ctx.enter_context(nc.psum_tensor("misc", [P, 4, CW], F32))

        def sem(name):
            return ctx.enter_context(nc.semaphore(name))

        mem_landed, small_landed, pool_landed = sem("mem_landed"), sem("small_landed"), sem("pool_landed")
        sk_landed, pgain_landed, fgain_landed, out_landed = sem("sk_landed"), sem("pgain_landed"), sem("fgain_landed"), sem("out_landed")
        x_landed = [sem(f"x_landed{t}") for t in range(TT)]
        raw_landed = [sem(f"raw_landed{s}") for s in range(RING)]
        hi_done, lo_even, lo_odd, chunk_used = sem("hi_done"), sem("lo_even"), sem("lo_odd"), sem("chunk_used")
        acc_free, half_read = sem("acc_free"), sem("half_read")
        consts, gains_T, gains_ready, wf_hi_done, wf_ready = sem("consts"), sem("gains_T"), sem("gains_ready"), sem("wf_hi_done"), sem("wf_ready")
        inv_ready = sem("inv_ready")
        squares, var_ready, root_ready, rstd_ready, normed_ready = sem("squares"), sem("var_ready"), sem("root_ready"), sem("rstd_ready"), sem("normed_ready")
        tr_ready, tr_hi, tr_lo = sem("tr_ready"), sem("tr_hi"), sem("tr_lo")
        f_done, fa_ready, fl_ready, cum_ready = sem("f_done"), sem("fa_ready"), sem("fl_ready"), sem("cum_ready")
        diff_ready, poolT_done = sem("diff_ready"), sem("poolT_done")
        qk_done, qk_read, fneg_ready, fexp_done, fp_ready = sem("qk_done"), sem("qk_read"), sem("fneg_ready"), sem("fexp_done"), sem("fp_ready")
        pT_done, pT_copied, fo_done, fo_hi, fo_lo = sem("pT_done"), sem("pT_copied"), sem("fo_done"), sem("fo_hi"), sem("fo_lo")
        h_copied = sem("h_copied")
        xs_done, xneg_ready, xexp_done, xp_ready = sem("xs_done"), sem("xneg_ready"), sem("xexp_done"), sem("xp_ready")
        xpT_done, xpT_copied, xo_done, xo_hi, xo_lo = sem("xpT_done"), sem("xpT_copied"), sem("xo_done"), sem("xo_hi"), sem("xo_lo")
        skT_done, skT_copied, ps_done, scores_ready = sem("skT_done"), sem("skT_copied"), sem("ps_done"), sem("scores_ready")
        u_landed = [sem(f"u_landed{s}") for s in range(4)]
        v_landed = [sem(f"v_landed{s}") for s in range(4)]
        routed, idx_v_ready, nbest_ready, gexp_done = sem("routed"), sem("idx_v_ready"), sem("nbest_ready"), sem("gexp_done")
        dot_done, gelu_done, wts_ready, diag_ready, v_used = sem("dot_done"), sem("gelu_done"), sem("wts_ready"), sem("diag_ready"), sem("v_used")
        y_gained, y_rstd = sem("y_gained"), sem("y_rstd")
        y_done, y_added, y_squared, y_var, y_root, y_ready = sem("y_done"), sem("y_added"), sem("y_squared"), sem("y_var"), sem("y_root"), sem("y_ready")
        dve_step, act_step, pool_step, passed = sem("dve_step"), sem("act_step"), sem("pool_step"), sem("passed")
        x_squared, table_ready, zero_ready, v_added, y_scaled = sem("x_squared"), sem("table_ready"), sem("zero_ready"), sem("v_added"), sem("y_scaled")
        block = ctx.enter_context(nc.Block())

        def wait_apart(engine, semaphore, value):
            engine.wait_ge(semaphore, value)
            engine.sem_inc(passed, 1)

        HW = CW // 2
        WKC = KC * CW // HW
        FIRST = ITEMS["peer"][0]

        def head_chunk(slot, kt, col, width):
            at = kt * HW + col
            return slot[:, at // CW, at % CW:at % CW + width]

        def xo_bank(u):
            return acc[:, 1, u % 2, :] if u % 4 < 2 else misc[:, u % 4, :]

        PAIRS = KT // 2
        PAIR0 = {"x": 0, "mem": PAIRS, "h1": 2 * PAIRS, "h2": 3 * PAIRS}

        BY_DVE = [k for k in range(TOP) if k % 3 == 2]
        BY_PE = [k for k in range(TOP) if k % 3 != 2]

        E0 = ITEMS["peer"][0]
        EARLY = [(None, range(0, 4)), ((E0 + 1, 1), range(4, 7)), ((E0 + 2, 0), range(7, 9)), ((E0 + 2, 1), range(9, 12)),
                 ((E0 + 3, 0), range(12, 14)), ((E0 + 3, 1), range(14, 16))]

        @block.sync
        def _(sp):
            def item(n, w, i, first=False, chunks=range(CH)):
                for j in chunks:
                    if not (first and j < RING):
                        sp.wait_ge((lo_even, lo_odd)[j % 2], n * HALF + (j // 2 - 1))
                    sp.dma_start(raw[:, j % RING, :, :],
                                 w[:, j * KC:(j + 1) * KC, bass.ts(i, CW)]).then_inc(raw_landed[j % RING], 16)

            for t in range(TT):
                sp.dma_start(h[:, t, :], x[0, t * P:(t + 1) * P, :]).then_inc(x_landed[t], 16)
            for v, r in ((mix_norm, G_MIX), (mem_norm, G_MEM), (xattn_norm, G_X), (peer_norm, G_PEER), (pool_scale, G_POOL)):
                v2 = v.rearrange("o (k p) -> (o k) p", p=P)
                sp.dma_start(gain_rows[r:r + v2.shape[0], :], v2).then_inc(small_landed, 16)
            sp.dma_start(bf[:, :], b_forget.rearrange("o f -> f o")).then_inc(small_landed, 16)
            sp.dma_start(wf[:, :, :], w_in_r[:, :, PW + 3 * FH * P:]).then_inc(small_landed, 16)
            n0, _ = ITEMS["in"]
            item(0, w_in_r, 0, first=True)
            sp.dma_start(poolw[:, :, :, :], pool_w[0].rearrange("g (c p) d -> p g c d", p=P)).then_inc(pool_landed, 16)
            sp.wait_ge(tr_ready, PAIRS)
            sp.dma_start(normed[:, :, :], mem[0].rearrange("(t p) d -> p t d", p=P)).then_inc(mem_landed, 16)
            with sp.Fori(1, ITEMS["in"][1]) as i:
                item(i, w_in_r, i)
            for name, w in (("k", w_k_r), ("v", w_v_r), ("out", w_out_r), ("q", w_q_r)):
                n0, items = ITEMS[name]
                with sp.Fori(0, items) as i:
                    item(i + n0, w, i)
            n0, items = ITEMS["o"]
            item(n0, w_o_r, 0, chunks=range(HALF))
            sp.wait_ge(xpT_done, XH)
            sp.dma_start(skraw[:, :, :], peer_sub_keys[0].rearrange("h c k d -> k (h c) d")).then_inc(sk_landed, 16)
            item(n0, w_o_r, 0, chunks=range(HALF, CH))
            sp.wait_ge(xo_done, 2 * XH)
            sp.dma_start(peer_gain[:, :], peer_norm[0:1, :].to_broadcast([P, D])).then_inc(pgain_landed, 16)
            with sp.Fori(1, items) as i:
                item(i + n0, w_o_r, i)
            n0, items = ITEMS["peer"]
            for j in range(CH):
                sp.wait_ge((lo_even, lo_odd)[j % 2], n0 * HALF + (j // 2 - 1))
                kt = j % HALF * WKC
                sp.dma_start(raw[:, j % RING, :, :].rearrange("p k (a c) -> p (k a) c", c=HW),
                             w_peer_r[:, kt:kt + WKC, j // HALF * HW:(j // HALF + 1) * HW]).then_inc(raw_landed[j % RING], 16)
            with sp.Fori(1, items) as i:
                item(i + n0, w_peer_r, i)
            sp.wait_ge(scores_ready, items + 1)
            sp.dma_start(final_gain[:, :], final_norm.rearrange("(o d) -> o d", o=1).to_broadcast([P, D])).then_inc(fgain_landed, 16)
            for c in range(TT):
                for half in range(2):
                    sp.wait_ge((y_scaled, y_ready)[half], c + 1)
                    cols = slice(half * D // 2, (half + 1) * D // 2)
                    sp.dma_start(out[0, c * P:(c + 1) * P, cols], y_out[:, c, cols]).then_inc(out_landed, 16)
            sp.wait_ge(out_landed, 16 * 2 * TT)

        @block.gpsimd
        def _(pool):
            step = Steps(pool, pool_step)
            step(nc.gpsimd.memset(ident[:, :], 0.0))
            nc.gpsimd.affine_select(out=ident[:, :], in_=ident[:, :], compare_op=ALU.not_equal, fill=1.0,
                                    base=0, pattern=[[-1, P]], channel_multiplier=1).then_inc(consts, 1)

            def low_parts(n, half):
                for j in range(half * HALF, half * HALF + HALF, 2):
                    pool.wait_ge(hi_done, n * CH + (j + 1))
                    nc.gpsimd.tensor_tensor(w_lo[:, j % RING, :, :], raw[:, j % RING, :, :],
                                            w_hi[:, j % RING, :, :].bitcast(F32), ALU.subtract).then_inc(lo_even, 1)

            low_parts(0, 0)
            step(nc.gpsimd.memset(mask[:, :], 0.0))
            nc.gpsimd.affine_select(out=mask[:, P:2 * P], in_=mask[:, P:2 * P], compare_op=ALU.is_ge, fill=MASKED,
                                    base=0, pattern=[[-1, P]], channel_multiplier=1).then_inc(consts, 1)
            step(nc.gpsimd.memset(sel[:, :, :], 0.0))
            nc.gpsimd.affine_select(out=sel[:, :, :], in_=sel[:, :, :], compare_op=ALU.not_equal, fill=1.0,
                                    base=0, pattern=[[-1, FH], [0, P]], channel_multiplier=1).then_inc(consts, 1)
            nc.gpsimd.memset(zeros[:, :], 0.0).then_inc(consts, 1)
            nc.gpsimd.memset(fones[:, :], 1.0).then_inc(consts, 1)
            nc.gpsimd.iota(iota[:, :], pattern=[[1, TOP]], base=0, channel_multiplier=0,
                           allow_small_or_imprecise_dtypes=True).then_inc(consts, 1)
            step(nc.gpsimd.iota(inv[:, 0, :], pattern=[[1, S]], base=1, channel_multiplier=0,
                                allow_small_or_imprecise_dtypes=True))
            for g in range(len(WINDOWS) - 1, -1, -1):
                step(nc.gpsimd.tensor_scalar(inv[:, g, :], inv[:, 0, :], float(WINDOWS[g]), None, ALU.min))
            pool.sem_inc(inv_ready, 1)
            with pool.Fori(0, ITEMS["peer"][0]) as n:
                low_parts(n, 1)
                low_parts(n + 1, 0)

            def gather_u(p, q, k, fresh=False):
                if not (fresh and k < 4):
                    wait_apart(pool, dot_done, p * TOP + (k - 3))
                nc.gpsimd.indirect_dma_start(
                    out=u_ring[:, k % 4, :], out_offset=None, in_=u_rows,
                    in_offset=bass.IndirectOffsetOnAxis(ap=idx_u[:, q, k:k + 1], axis=0)).then_inc(u_landed[k % 4], 16)

            def gather_v(g, q, k, fresh=False):
                if not (fresh and k < 4):
                    wait_apart(pool, v_used, g * TOP + (k - 3))
                nc.gpsimd.indirect_dma_start(
                    out=v_ring[:, k % 4, :], out_offset=None, in_=v_rows,
                    in_offset=bass.IndirectOffsetOnAxis(ap=idx_v[:, q, k:k + 1], axis=0)).then_inc(v_landed[k % 4], 16)

            def period(p, q):
                pool.wait_ge(routed, p + 1)
                pool.wait_ge(idx_v_ready, p)
                for k in range(TOP):
                    gather_u(p, q, k)
                    gather_v(p - 1, 1 - q, k)

            n0, _ = ITEMS["peer"]
            low_parts(n0, 1)
            low_parts(n0 + 1, 0)
            pool.wait_ge(routed, 1)
            for part, ks in EARLY:
                if part is not None:
                    low_parts(*part)
                for k in ks:
                    gather_u(0, 0, k, fresh=True)
            pool.wait_ge(idx_v_ready, 1)
            pool.wait_ge(chunk_used, LAST * CH + CH)
            pool.wait_ge(routed, 2)
            for k in range(TOP):
                gather_v(0, 0, k, fresh=True)
                gather_u(1, 1, k)
            with pool.Fori(1, GROUPS // 2) as b:
                period(b * 2, 0)
                period(b * 2 + 1, 1)
            pool.wait_ge(idx_v_ready, GROUPS)
            for k in range(TOP):
                if k - 4 in BY_DVE:
                    pool.wait_ge(v_added, BY_DVE.index(k - 4) + 1)
                elif k >= 4:
                    pool.wait_ge(v_used, (GROUPS - 1) * TOP + BY_PE.index(k - 4) + 1)
                else:
                    pool.wait_ge(v_used, (GROUPS - 1) * TOP + k - 3)
                nc.gpsimd.indirect_dma_start(
                    out=v_ring[:, k % 4, :], out_offset=None, in_=v_rows,
                    in_offset=bass.IndirectOffsetOnAxis(ap=idx_v[:, 1, k:k + 1], axis=0)).then_inc(v_landed[k % 4], 16)

        @block.scalar
        def _(act):
            def high_parts(n, half, first=False, chunks=None):
                for j in chunks or range(half * HALF, half * HALF + HALF):
                    act.wait_ge(raw_landed[j % RING], n * (2 * 16) + 16 * (j // RING + 1))
                    if not first:
                        act.wait_ge(chunk_used, n * CH + (j - RING + 1))
                    nc.scalar.activation(w_hi[:, j % RING, :, :], raw[:, j % RING, :, :], ACT.Copy).then_inc(hi_done, 1)

            def square_sums(src, i, before, fresh=False):
                for t in range(TT):
                    if not fresh:
                        act.wait_ge(squares, before * TT + (t - 1))
                    nc.scalar.activation(junk[:, t, :], src(t), ACT.Square, accum_out=sq[:, t, bass.ds(i, 1)]).then_inc(squares, 1)

            def root(k):
                act.wait_ge(var_ready, k)
                nc.scalar.activation(rt[:, :], ss[:, :], ACT.Sqrt).then_inc(root_ready, 1)

            def pair_hi(pair, bank, hi, kt, gain):
                act.wait_ge(tr_ready, pair + 1)
                for kk in range(2):
                    ins = nc.scalar.activation(hi[:, bass.ds(kt + kk, 1), :], misc[:, bank, kk * S:(kk + 1) * S], ACT.Copy,
                                               scale=gains[:, bass.ds(kt + (gain + kk), 1)])
                ins.then_inc(tr_hi, 1)

            act.wait_ge(zero_ready, 1)
            nc.scalar.activation(rt[:, 0:1], warm[:, :], ACT.Sqrt).then_inc(table_ready, 1)
            act.wait_ge(x_landed[0], 16)
            nc.scalar.activation(normed[:, 0, :], h[:, 0, :], ACT.Square, accum_out=ss[:, 0:1]).then_inc(x_squared, 1)
            act.wait_ge(table_ready, 1)
            root(1)
            act.wait_ge(rstd_ready, 1)
            nc.scalar.activation(normed[:, 1, :], h[:, 1, :], ACT.Copy, scale=rstd[:, 1:2]).then_inc(normed_ready, 1)
            high_parts(0, 0, first=True, chunks=range(2))
            act.wait_ge(gains_ready, 1)
            for p in range(PAIRS):
                pair_hi(PAIR0["x"] + p, p % 4, t1_hi, 2 * p, G_MIX)
                if p == 1:
                    high_parts(0, 0, first=True, chunks=range(2, HALF))
            act.wait_ge(small_landed, 16 * 7)
            act.wait_ge(zero_ready, 3)
            nc.scalar.activation(wf_hi[:, :, 0:FH], wf[:, :, :], ACT.Copy).then_inc(wf_hi_done, 1)
            with act.Fori(0, T_IN) as n:
                high_parts(n, 1)
                high_parts(n + 1, 0)
            act.wait_ge(fa_ready, 1)
            nc.scalar.activation(fe[:, :], fa[:, :], ACT.Exp, scale=-1.0).then_inc(act_step, 1)
            act.wait_ge(act_step, 1)
            nc.scalar.activation(fe[:, :], fe[:, :], ACT.Ln, bias=1.0).then_inc(fl_ready, 1)
            act.wait_ge(mem_landed, 16)
            for i in range(4):
                square_sums(lambda t: normed[:, t, i * CW:(i + 1) * CW], i, i, fresh=i == 0)
            high_parts(T_IN, 1)
            root(2)
            high_parts(T_IN + 1, 0)
            act.wait_ge(rstd_ready, 2)
            nc.scalar.activation(normed[:, 1, :], normed[:, 1, :], ACT.Copy, scale=rstd[:, 1:2]).then_inc(normed_ready, 1)
            high_parts(T_IN + 1, 1)
            high_parts(T_IN + 2, 0)
            for g in range(len(WINDOWS)):
                act.wait_ge(poolT_done, g + 1)
                for dt in range(GT):
                    col = G_POOL + g * GT + dt
                    ins = nc.scalar.activation(t1_hi[:, g * GT + dt, :], misc[:, g, dt * S:(dt + 1) * S], ACT.Copy,
                                               scale=gains[:, col:col + 1])
                ins.then_inc(tr_hi, 1)
            for p in range(PAIRS):
                act.wait_ge(tr_ready, PAIR0["mem"] + p + 1)
                for kk in range(2):
                    ins = nc.scalar.activation(t2_hi[:, 2 * p + kk, :], misc[:, p % 4, kk * S:(kk + 1) * S], ACT.Copy,
                                               scale=gains[:, G_MEM + 2 * p + kk:G_MEM + 2 * p + kk + 1])
                ins.then_inc(tr_hi, 1)
            n0, _ = ITEMS["k"]
            high_parts(n0, 1)
            high_parts(n0 + 1, 0)
            act.wait_ge(fneg_ready, 1)
            for f in range(FH):
                if f == FH // 2:
                    high_parts(n0 + 1, 1)
                for t in range(TT):
                    part = foxs[:, f, t * P:(2 * t + 1) * P]
                    nc.scalar.activation(part, part, ACT.Exp, bias=fneg[:, f, t:t + 1], scale=FSCALE,
                                         accum_out=fsum[:, f, t:t + 1]).then_inc(fexp_done, 1)
            high_parts(n0 + 2, 0)
            for name in ("k", "v"):
                n0, items = ITEMS[name]
                with act.Fori(2 if name == "k" else 0, items) as i:
                    high_parts(i + n0, 1)
                    high_parts(i + (n0 + 1), 0)
                if name == "k":
                    for f in range(FH):
                        act.wait_ge(fo_done, f + 1)
                        nc.scalar.activation(t1_hi[:, PW // P + f, :], misc[:, 2 + f % 2, 0:S], ACT.Copy).then_inc(fo_hi, 1)

            def turn_hi(pair0, i, hi, gain):
                for p in range(2):
                    pair_hi(pair0 + 2 * i + p, 2 * (i % 2) + p, hi, 4 * i + 2 * p, gain)

            def residual_items(name, hi, gain, pair0, squares0):
                n0, items = ITEMS[name]
                for i in range(items):
                    high_parts(n0 + i, 1)
                    if i:
                        turn_hi(pair0, i - 1, hi, gain)
                    high_parts(n0 + i + 1, 0)
                    act.wait_ge(acc_free, n0 + i + 3)
                    nc.scalar.activation(h[:, :, i * CW:(i + 1) * CW], hs[:, i % 2, :, :], ACT.Copy).then_inc(h_copied, 1)
                    square_sums(lambda t: hs[:, i % 2, t, :], i, i + squares0)

            def x_exps(i):
                q = i % 2
                for t in range(TT):
                    act.wait_ge(xneg_ready, i * TT + t + 1)
                    nc.scalar.activation(xp[:, i, t, :], misc[:, 2 * q + t, 0:S], ACT.Exp, bias=xneg[:, q, t:t + 1],
                                         scale=xfac[:, t:t + 1], accum_out=xsum[:, q, t:t + 1]).then_inc(xexp_done, 1)

            residual_items("out", t2_hi, G_X, PAIR0["h1"], 4)
            n0, items = ITEMS["q"]
            for i in range(items):
                high_parts(n0 + i, 1)
                if i:
                    x_exps(i - 1)
                else:
                    turn_hi(PAIR0["h1"], ITEMS["out"][1] - 1, t2_hi, G_X)
                    root(3)
                high_parts(n0 + i + 1, 0)
            x_exps(XH - 1)
            for u in range(2 * XH):
                act.wait_ge(xo_done, u + 1)
                nc.scalar.activation(t1_hi[:, 2 * u:2 * u + 2, :], xo_bank(u).rearrange("p (a s) -> p a s", a=2),
                                     ACT.Copy).then_inc(xo_hi, 1)
            residual_items("o", t2_hi, G_PEER, PAIR0["h2"], 8)
            n0, items = ITEMS["peer"]
            turn_hi(PAIR0["h2"], ITEMS["o"][1] - 1, t2_hi, G_PEER)
            high_parts(n0, 1, chunks=(HALF,))
            root(4)
            high_parts(n0, 1, chunks=range(HALF + 1, CH))
            high_parts(n0 + 1, 0)

            def gate_exp(g):
                act.wait_ge(nbest_ready, g + 1)
                nc.scalar.activation(exps[:, :], best[:, :], ACT.Exp, bias=neg_best[:, 0:1],
                                     accum_out=exp_sum[:, 0:1]).then_inc(gexp_done, 1)

            def diagonals(g, q, ks=range(TOP), fresh=False):
                act.wait_ge(wts_ready, g + 1)
                for k in ks:
                    if not fresh:
                        act.wait_ge(v_used, g * TOP + (k - 3))
                    nc.scalar.activation(diag[:, k % 4, :], ident[:, :], ACT.Copy, scale=wts[:, q, k:k + 1]).then_inc(diag_ready, 1)

            def gelu(g, q, c):
                act.wait_ge(dot_done, g * TOP + TOP)
                nc.scalar.activation(acts[:, q, :], dots[:, q, :], ACT.Gelu, scale=rstd[:, c:c + 1]).then_inc(gelu_done, 1)

            def period(p, q, c, second=False, last=False):
                if second:
                    diagonals(p - 1, 1 - q, range(4), fresh=True)
                if not last:
                    gate_exp(p + 1)
                diagonals(p - 1, 1 - q, range(4 if second else 0, TOP))
                gelu(p, q, c)

            def finish(c):
                for i in range(4):
                    act.wait_ge(y_added, 4 * c + i + 1)
                    if c or i >= 2:
                        act.wait_ge(y_squared, 4 * c + i - 1)
                    nc.scalar.activation(junk[:, i % 2, :], y_sum[:, c, i * CW:(i + 1) * CW], ACT.Square,
                                         accum_out=sq[:, c, i:i + 1]).then_inc(y_squared, 1)
                act.wait_ge(y_var, c + 1)
                nc.scalar.activation(rt[:, c:c + 1], ss[:, c:c + 1], ACT.Sqrt).then_inc(y_root, 1)
                act.wait_ge(y_rstd, c + 1)
                nc.scalar.activation(y_out[:, c, 0:D // 2], y_out[:, c, 0:D // 2], ACT.Copy, scale=rstd[:, c:c + 1]).then_inc(y_scaled, 1)

            gate_exp(0)
            for i in range(1, items):
                high_parts(n0 + i, 1)
                if i < items - 1:
                    high_parts(n0 + i + 1, 0)
            gate_exp(1)
            gelu(0, 0, 0)
            period(1, 1, 0, second=True)
            for c in range(TT):
                with act.Fori(c * PH // 2 + 1 - c, (c + 1) * PH // 2 - c) as b:
                    period(b * 2, 0, c)
                    period(b * 2 + 1, 1, c)
            finish(0)
            period(GROUPS - 2, 0, 1)
            period(GROUPS - 1, 1, 1, last=True)
            nc.scalar.activation(warm[:, :], zeros[:, 0:1], ACT.Sqrt).then_inc(table_ready, 1)
            act.wait_ge(wts_ready, GROUPS)
            for m, k in enumerate(BY_PE):
                act.wait_ge(v_used, (GROUPS - 1) * TOP + m - 3)
                nc.scalar.activation(diag[:, m % 4, :], ident[:, :], ACT.Copy, scale=wts[:, 1, k:k + 1]).then_inc(diag_ready, 1)
            finish(1)

        @block.vector
        def _(dve):
            step = Steps(dve, dve_step, passed=passed)

            def low_parts(n, half, chunks=None):
                for j in chunks or range(half * HALF + 1, half * HALF + HALF, 2):
                    dve.wait_ge(hi_done, n * CH + (j + 1))
                    nc.vector.tensor_tensor(w_lo[:, j % RING, :, :], raw[:, j % RING, :, :],
                                            w_hi[:, j % RING, :, :].bitcast(F32), ALU.subtract).then_inc(lo_odd, 1)

            def reciprocal_root(k, sums):
                if sums is not None:
                    dve.wait_ge(squares, sums)
                    step(nc.vector.tensor_reduce(ss[:, :], sq[:, :, :], AX.X, ALU.add))
                nc.vector.tensor_scalar(ss[:, :], ss[:, :], 1.0 / D, EPS, ALU.mult, ALU.add).then_inc(var_ready, 1)
                dve.wait_ge(root_ready, k)
                nc.vector.reciprocal(rstd[:, :], rt[:, :]).then_inc(rstd_ready, 1)
                dve.wait_ge(rstd_ready, k)

            def pair_lo(done, count, bank, hi, lo, kt, gain):
                dve.wait_ge(done, count)
                for kk in range(2):
                    ins = nc.vector.scalar_tensor_tensor(
                        lo[:, bass.ds(kt + kk, 1), :], misc[:, bank:bank + 1, kk * S:(kk + 1) * S],
                        gains[:, bass.ds(kt + (gain + kk), 1)], hi[:, bass.ds(kt + kk, 1), :].bitcast(F32),
                        ALU.mult, ALU.subtract)
                ins.then_inc(tr_lo, 1)

            def evacuate(n, q, dst):
                dve.wait_ge(chunk_used, n * CH + CH)
                nc.vector.tensor_copy(dst, acc[:, q, :, :]).then_inc(acc_free, 1)

            def transposed(q):
                return acc[:, q, :, :].rearrange("p b (c s) -> p (b c) s", s=S)

            def evacuate_T(n, q, dst):
                dve.wait_ge(chunk_used, n * CH + CH)
                nc.vector.tensor_copy(dst, transposed(q)).then_inc(acc_free, 1)

            dve.wait_ge(consts, 1)
            dve.sem_inc(acc_free, 2)
            nc.vector.memset(warm[:, :], 0.0).then_inc(zero_ready, 1)
            nc.vector.memset(wf_hi[:, :, :].bitcast(F32), 0.0).then_inc(zero_ready, 1)
            nc.vector.memset(wf_lo[:, :, :].bitcast(F32), 0.0).then_inc(zero_ready, 1)
            dve.wait_ge(x_landed[1], 16)
            step(nc.vector.tensor_tensor_reduce(out=normed[:, 1, :], in0=h[:, 1, :], in1=h[:, 1, :], scale=1.0, scalar=0.0,
                                                op0=ALU.mult, op1=ALU.add, accum_out=ss[:, 1:2]))
            dve.wait_ge(x_squared, 1)
            reciprocal_root(1, None)
            nc.vector.tensor_scalar(normed[:, 0, :], h[:, 0, :], rstd[:, 0:1], None, ALU.mult).then_inc(normed_ready, 1)
            dve.wait_ge(gains_T, 1)
            nc.vector.tensor_copy(gains[:, :], misc[:, 3, 0:NG]).then_inc(gains_ready, 1)
            dve.wait_ge(gains_ready, 1)
            for p in range(PAIRS):
                pair_lo(tr_hi, PAIR0["x"] + p + 1, p % 4, t1_hi, t1_lo, 2 * p, G_MIX)
                if p in (0, 2):
                    low_parts(0, 0, chunks=(p + 1,))
            dve.wait_ge(wf_hi_done, 1)
            dve.wait_ge(zero_ready, 3)
            nc.vector.tensor_tensor(wf_lo[:, :, 0:FH], wf[:, :, :], wf_hi[:, :, 0:FH].bitcast(F32), ALU.subtract).then_inc(wf_ready, 1)
            dve.wait_ge(inv_ready, 1)
            step(nc.vector.reciprocal(inv[:, :, :], inv[:, :, :]))
            with dve.Fori(0, T_IN // 2) as b:
                for q in range(2):
                    n = b * 2 + q
                    low_parts(n, 1)
                    low_parts(n + 1, 0, chunks=(1,))
                    evacuate_T(n, q, foxT[:, bass.ds(n * CT, CT), :])
                    low_parts(n + 1, 0, chunks=(3,))
            dve.wait_ge(f_done, 1)
            step(nc.vector.tensor_scalar(fz[:, :], misc[0:FH, 0, 0:S], bf[:, 0:1], None, ALU.add))
            nc.vector.scalar_tensor_tensor(fa[:, :], fz[:, :], -1.0, fz[:, :], ALU.mult, ALU.max).then_inc(fa_ready, 1)
            dve.wait_ge(fa_ready, 1)
            step(nc.vector.tensor_scalar(fz[:, :], fz[:, :], 0.0, None, ALU.min))

            def window_diff(g):
                src = foxT[:, g * GT:(g + 1) * GT, :]
                a, b = winA, winB
                step(nc.vector.tensor_copy(a[:, :, pad:], src))
                w = 1
                while w < WINDOWS[g]:
                    step(nc.vector.tensor_tensor(b[:, :, pad:], a[:, :, pad:], a[:, :, pad - w:pad - w + S], ALU.add))
                    a, b, w = b, a, 2 * w
                row = inv[:, g:g + 1, :].to_broadcast([P, GT, S])
                step(nc.vector.tensor_tensor(b[:, :, pad:], a[:, :, pad:], row, ALU.mult))
                nc.vector.tensor_tensor(diff[:, g * GT:(g + 1) * GT, :], b[:, :, pad:], src, ALU.subtract).then_inc(diff_ready, 1)
                dve.wait_ge(diff_ready, len(done_diffs) + 1)
                done_diffs.append(g)

            done_diffs = []
            step(nc.vector.memset(winA[:, :, 0:pad], 0.0))
            step(nc.vector.memset(winB[:, :, 0:pad], 0.0))
            window_diff(3)
            window_diff(2)
            low_parts(T_IN, 1)
            reciprocal_root(2, 4 * TT)
            nc.vector.tensor_scalar(normed[:, 0, :], normed[:, 0, :], rstd[:, 0:1], None, ALU.mult).then_inc(normed_ready, 1)
            low_parts(T_IN + 1, 0, chunks=(1,))
            evacuate(T_IN, 0, foxv[:, :, 0:CW])
            low_parts(T_IN + 1, 0, chunks=(3,))
            dve.wait_ge(fl_ready, 1)
            step(nc.vector.tensor_tensor(fz[:, :], fz[:, :], fe[:, :], ALU.subtract))
            dve.wait_ge(consts, 6)
            step(nc.vector.tensor_tensor_scan(fa[:, :], fones[:, :], fz[:, :], 0.0, ALU.mult, ALU.add))
            step(nc.vector.tensor_scalar(cum[:, :], fa[:, :], -1.0 / FSCALE, None, ALU.mult))
            step(nc.vector.tensor_copy(cum_hi[:, :], cum[:, :]))
            nc.vector.tensor_tensor(cum_lo[:, :], cum[:, :], cum_hi[:, :].bitcast(F32), ALU.subtract).then_inc(cum_ready, 1)
            nc.vector.tensor_copy(sel_r[:, :, :], sel[:, :, :]).then_inc(cum_ready, 1)
            low_parts(T_IN + 1, 1)
            window_diff(1)
            window_diff(0)
            low_parts(T_IN + 2, 0, chunks=(1,))
            evacuate(T_IN + 1, 1, foxv[:, :, CW:2 * CW])
            low_parts(T_IN + 2, 0, chunks=(3,))
            dve.wait_ge(consts, 6)
            for f in range(FH):
                for t in range(TT):
                    u = f * TT + t
                    dve.wait_ge(qk_done, u + 1)
                    nc.vector.tensor_tensor_reduce(
                        out=foxs[:, f, t * P:(2 * t + 1) * P], in0=misc[:, u % 4, 0:(t + 1) * P], in1=mask[:, (1 - t) * P:2 * P],
                        scale=1.0, scalar=LOW, op0=ALU.add, op1=ALU.max, accum_out=fmax[:, f, t:t + 1]).then_inc(qk_read, 1)
            dve.wait_ge(qk_read, FH * TT)
            nc.vector.tensor_scalar(fneg[:, :, :], fmax[:, :, :], -FSCALE, None, ALU.mult).then_inc(fneg_ready, 1)
            for g in range(len(WINDOWS)):
                dve.wait_ge(tr_hi, PAIRS + g + 1)
                for dt in range(GT):
                    col = G_POOL + g * GT + dt
                    ins = nc.vector.scalar_tensor_tensor(
                        t1_lo[:, g * GT + dt, :], misc[:, g, dt * S:(dt + 1) * S], gains[:, col:col + 1],
                        t1_hi[:, g * GT + dt, :].bitcast(F32), ALU.mult, ALU.subtract)
                ins.then_inc(tr_lo, 1)
            for p in range(PAIRS):
                pair_lo(tr_hi, PAIRS + 4 + p + 1, p % 4, t2_hi, t2_lo, 2 * p, G_MEM)
            n0, items = ITEMS["k"]

            def key_items(b):
                for q in range(2):
                    i = b * 2 + q
                    low_parts(i + n0, 1)
                    low_parts(i + (n0 + 1), 0, chunks=(1,))
                    evacuate_T(i + n0, q, memk[:, bass.ds(i * CT, CT), :])
                    low_parts(i + (n0 + 1), 0, chunks=(3,))

            key_items(0)
            dve.wait_ge(fexp_done, FH * TT)
            step(nc.vector.reciprocal(frec[:, :, :], fsum[:, :, :]))
            for f in range(FH):
                for t in range(TT):
                    part = foxs[:, f, t * P:(2 * t + 1) * P]
                    ins = nc.vector.tensor_scalar(part, part, frec[:, f, t:t + 1], None, ALU.mult)
                ins.then_inc(fp_ready, 1)
            key_items(1)
            for f in range(FH + 1):
                if f < FH:
                    dve.wait_ge(pT_done, f + 1)
                    nc.vector.tensor_copy(pT[:, f % 2, :], misc[:, f % 2, 0:3 * P]).then_inc(pT_copied, 1)
                if f:
                    dve.wait_ge(fo_hi, f)
                    kt = PW // P + f - 1
                    nc.vector.tensor_tensor(t1_lo[:, kt, :], misc[:, 2 + (f - 1) % 2, 0:S], t1_hi[:, kt, :].bitcast(F32),
                                            ALU.subtract).then_inc(fo_lo, 1)
            n0, items = ITEMS["v"]
            with dve.Fori(0, items // 2) as b:
                for q in range(2):
                    i = b * 2 + q
                    low_parts(i + n0, 1)
                    low_parts(i + (n0 + 1), 0, chunks=(1,))
                    evacuate(i + n0, q, memv[:, :, bass.ds(i * CW, CW)])
                    low_parts(i + (n0 + 1), 0, chunks=(3,))

            def turn_lo(pair0, i, hi, lo, gain):
                for p in range(2):
                    pair_lo(tr_hi, pair0 + 4 + 2 * i + p + 1, 2 * (i % 2) + p, hi, lo, 4 * i + 2 * p, gain)

            def residual_items(name, hi, lo, gain, pair0):
                n0, items = ITEMS[name]
                for i in range(items):
                    low_parts(n0 + i, 1)
                    if i:
                        turn_lo(pair0, i - 1, hi, lo, gain)
                    elif name == "o":
                        for p in range(4):
                            dve.wait_ge(skT_done, p + 1)
                            nc.vector.tensor_copy(skT[:, 4 * p:4 * p + 4, :], misc[:, p, :].rearrange("p (a s) -> p a s", a=4)).then_inc(skT_copied, 1)
                    low_parts(n0 + i + 1, 0, chunks=(1,))
                    dve.wait_ge(chunk_used, (n0 + i) * CH + CH)
                    nc.vector.tensor_tensor(hs[:, i % 2, :, :], acc[:, i % 2, :, :], h[:, :, i * CW:(i + 1) * CW],
                                            ALU.add).then_inc(acc_free, 1)
                    low_parts(n0 + i + 1, 0, chunks=(3,))
                    if name == "o":
                        dve.wait_ge(pgain_landed, 16)
                        dve.wait_ge(acc_free, n0 + i + 3)
                        step(nc.vector.tensor_tensor(hn[:, :, i * CW:(i + 1) * CW], hs[:, i % 2, :, :],
                                                     peer_gain[:, i * CW:(i + 1) * CW].unsqueeze(1).to_broadcast([P, TT, CW]), ALU.mult))

            def x_max(i):
                q = i % 2
                for t in range(TT):
                    dve.wait_ge(xs_done, i * TT + t + 1)
                    step(nc.vector.tensor_reduce(xmax[:, q, t:t + 1], misc[:, 2 * q + t, 0:S], AX.X, ALU.max))
                    nc.vector.tensor_scalar(xneg[:, q, t:t + 1], xmax[:, q, t:t + 1], xfac[:, t:t + 1], -1.0,
                                            ALU.mult, ALU.mult).then_inc(xneg_ready, 1)

            def x_norm(i):
                q = i % 2
                for t in range(TT):
                    dve.wait_ge(xexp_done, i * TT + t + 1)
                    step(nc.vector.reciprocal(xrec[:, q, t:t + 1], xsum[:, q, t:t + 1]))
                    nc.vector.tensor_scalar(xp[:, i, t, :], xp[:, i, t, :], xrec[:, q, t:t + 1], None,
                                            ALU.mult).then_inc(xp_ready, 1)

            residual_items("out", t2_hi, t2_lo, G_X, PAIR0["h1"])
            n0, items = ITEMS["q"]
            for i in range(items):
                low_parts(n0 + i, 1)
                if i:
                    x_max(i - 1)
                    x_norm(i - 1)
                else:
                    turn_lo(PAIR0["h1"], ITEMS["out"][1] - 1, t2_hi, t2_lo, G_X)
                    reciprocal_root(3, 2 * 4 * TT)
                    step(nc.vector.tensor_scalar(xfac[:, :], rstd[:, :], XSCALE, None, ALU.mult))
                low_parts(n0 + i + 1, 0, chunks=(1,))
                evacuate_T(n0 + i, i % 2, qs[:, i % 2, :, :])
                low_parts(n0 + i + 1, 0, chunks=(3,))

            def x_turned(hd):
                dve.wait_ge(xpT_done, hd + 1)
                nc.vector.tensor_copy(xpT[:, hd % 2, :, :], misc[:, hd % 2, :].rearrange("p (m s) -> p m s", m=TT)).then_inc(xpT_copied, 1)

            def xo_low(u):
                dve.wait_ge(xo_hi, u + 1)
                nc.vector.tensor_tensor(t1_lo[:, 2 * u:2 * u + 2, :], xo_bank(u).rearrange("p (a s) -> p a s", a=2),
                                        t1_hi[:, 2 * u:2 * u + 2, :].bitcast(F32), ALU.subtract).then_inc(xo_lo, 1)

            x_turned(0)
            x_max(XH - 1)
            x_turned(1)
            x_norm(XH - 1)
            for hd in range(2, XH):
                xo_low(2 * hd - 4)
                xo_low(2 * hd - 3)
                x_turned(hd)
            for u in range(2 * XH - 4, 2 * XH):
                xo_low(u)
            residual_items("o", t2_hi, t2_lo, G_PEER, PAIR0["h2"])
            n0, items = ITEMS["peer"]
            turn_lo(PAIR0["h2"], ITEMS["o"][1] - 1, t2_hi, t2_lo, G_PEER)
            reciprocal_root(4, 3 * 4 * TT)
            low_parts(n0, 1, chunks=(HALF + 1,))

            def peer_scores(b):
                at, width = (b * HW, HW) if b < 2 else ((b - 1) * CW, CW)
                for t in range(TT):
                    dve.wait_ge(ps_done, b * TT + t + 1)
                    ins = nc.vector.tensor_scalar(scores[:, t, at:at + width], misc[:, 2 * (b % 2) + t, 0:width],
                                                  rstd[:, t:t + 1], None, ALU.mult)
                ins.then_inc(scores_ready, 1)

            dve.wait_ge(chunk_used, n0 * CH + HALF)
            nc.vector.tensor_copy(pq[:, 0, 0:2, :], acc[:, 0, 0, :].rearrange("p (c s) -> p c s", s=S)).then_inc(half_read, 1)
            low_parts(n0, 1, chunks=(HALF + 3,))
            peer_scores(0)
            dve.wait_ge(scores_ready, 1)

            def top16(values, left, maxima, places):
                step(nc.vector.max(maxima[:, 0:8], values), apart=True)
                nc.vector.max_index(places[:, 0:8], maxima[:, 0:8], values)
                step(nc.vector.match_replace(left, maxima[:, 0:8], values, LOW), apart=True)
                step(nc.vector.max(maxima[:, 8:16], left), apart=True)
                step(nc.vector.max_index(places[:, 8:16], maxima[:, 8:16], left), apart=True)

            def route(g, q, c, head, amid=None):
                step(nc.vector.tensor_copy(cur[:, :, :], scores[:, c, bass.ds(head * (2 * KEYS), 2 * KEYS)].rearrange("p (a k) -> p a k", a=2)),
                     apart=True)
                for a in range(2):
                    top16(cur[:, a, :], rest[:, a, :], top[:, a, :], top_at[:, a, :])
                    if a == 0 and amid is not None:
                        amid()
                step(nc.vector.tensor_tensor(cand[:, :, :], top[:, 0, :].unsqueeze(2).to_broadcast([P, TOP, TOP]),
                                             top[:, 1, :].unsqueeze(1).to_broadcast([P, TOP, TOP]), ALU.add), apart=True)
                top16(cand[:, :, :].rearrange("p a b -> p (a b)"), cand_rest[:, :, :].rearrange("p a b -> p (a b)"), best, pos)
                nc.vector.tensor_scalar(neg_best[:, :], best[:, 0:1], -1.0, None, ALU.mult).then_inc(nbest_ready, 1)
                nc.vector.tensor_scalar(ab[:, 0, :], pos[:, :], 4, None, ALU.logical_shift_right)
                step(nc.vector.tensor_scalar(ab[:, 1, :], pos[:, :], TOP - 1, None, ALU.bitwise_and))
                step(nc.vector.tensor_tensor(hot[:, :, :, :].rearrange("p a k i -> p (a k) i"),
                                             ab[:, :, :].rearrange("p a k -> p (a k)").unsqueeze(2).to_broadcast([P, 2 * TOP, TOP]),
                                             iota[:, :].unsqueeze(1).to_broadcast([P, 2 * TOP, TOP]), ALU.is_equal))
                step(nc.vector.tensor_tensor(hot[:, :, :, :], hot[:, :, :, :],
                                             top_at[:, :, :].unsqueeze(2).to_broadcast([P, 2, TOP, TOP]), ALU.mult))
                step(nc.vector.tensor_reduce(picked[:, :, :], hot[:, :, :, :], AX.X, ALU.add))
                nc.vector.scalar_tensor_tensor(idx_u[:, q, :], picked[:, 0, :], float(KEYS), picked[:, 1, :],
                                               ALU.mult, ALU.add).then_inc(routed, 1)

            def gates(g, q):
                dve.wait_ge(gexp_done, g + 1)
                step(nc.vector.reciprocal(exp_rec[:, :], exp_sum[:, :]))
                step(nc.vector.tensor_scalar(gate[:, q, :], exps[:, :], exp_rec[:, 0:1], None, ALU.mult))

            ROUTE_STEPS = 1 + 2 * 4 + 1 + 4 + 1 + 3 + 2

            def weights(g, q, fresh=False):
                dve.wait_ge(gelu_done, g + 1)
                if not fresh:
                    dve.wait_ge(diag_ready, g * TOP - (TOP - 1))
                nc.vector.tensor_tensor(wts[:, q, :], acts[:, q, :], gate[:, q, :], ALU.mult).then_inc(wts_ready, 1)

            def dot_products(g, q, c, ks, first=False):
                for k in ks:
                    dve.wait_ge(u_landed[k % 4], g * (16 * TOP // 4) + 16 * (k // 4 + 1))
                    if not (first and k == 0):
                        dve.wait_ge(dot_done, g * TOP + k)
                    nc.vector.tensor_tensor_reduce(out=product[:, :], in0=u_ring[:, k % 4, :], in1=hn[:, c, :], scale=1.0, scalar=0.0,
                                                   op0=ALU.mult, op1=ALU.add, accum_out=dots[:, q, k:k + 1]).then_inc(dot_done, 1)

            def period(g, q, c, next_c, next_head, second=False, last=False):
                if not second:
                    for s in range(4):
                        dve.wait_ge(v_landed[s], g * (16 * TOP // 4) - 16 * TOP // 4)
                dve.wait_ge(routed, g + 1)
                nc.vector.tensor_copy(idx_v[:, q, :], idx_u[:, q, :]).then_inc(idx_v_ready, 1)
                weights(g - 1, 1 - q, fresh=second)
                dve.wait_ge(wts_ready, g)
                if second:
                    dot_products(g, q, c, range(0, 4))
                if not last:
                    route(g + 1, 1 - q, next_c, next_head)
                    gates(g + 1, 1 - q)
                dot_products(g, q, c, range(4 if second else 0, TOP))

            def finish(c):
                dve.wait_ge(y_done, c + 1)
                base = h if c == 0 else y_sum
                for i in range(4):
                    bank = misc[:, i, :] if c == 0 else acc[:, i // 2, i % 2, :]
                    nc.vector.tensor_tensor(y_sum[:, c, i * CW:(i + 1) * CW], bank, base[:, c, i * CW:(i + 1) * CW],
                                            ALU.add).then_inc(y_added, 1)
                dve.wait_ge(fgain_landed, 16)
                dve.wait_ge(y_added, 4 * c + 4)
                step(nc.vector.tensor_tensor(y_out[:, c, 0:D // 2], y_sum[:, c, 0:D // 2], final_gain[:, 0:D // 2], ALU.mult))
                dve.wait_ge(y_squared, 4 * (c + 1))
                step(nc.vector.tensor_reduce(ss[:, c:c + 1], sq[:, c, :], AX.X, ALU.add))
                nc.vector.tensor_scalar(ss[:, c:c + 1], ss[:, c:c + 1], 1.0 / D, EPS, ALU.mult, ALU.add).then_inc(y_var, 1)
                dve.wait_ge(y_root, c + 1)
                nc.vector.reciprocal(rstd[:, c:c + 1], rt[:, c:c + 1]).then_inc(y_rstd, 1)
                dve.wait_ge(y_rstd, c + 1)
                nc.vector.scalar_tensor_tensor(y_out[:, c, D // 2:D], y_sum[:, c, D // 2:D], rstd[:, c:c + 1], final_gain[:, D // 2:D],
                                               ALU.mult, ALU.mult).then_inc(y_ready, 1)

            def two_periods(b, c, next_c, last=False):
                head = b * 2 - c * PH
                period(b * 2, 0, c, c, head + 1)
                period(b * 2 + 1, 1, c, next_c, (head + 2) if next_c == c else 0, last=last)

            route(0, 0, 0, 0, amid=lambda: low_parts(n0 + 1, 0, chunks=(1,)))
            dve.wait_ge(routed, 1)
            nc.vector.tensor_copy(idx_v[:, 0, :], idx_u[:, 0, :]).then_inc(idx_v_ready, 1)
            dve.wait_ge(chunk_used, n0 * CH + CH)
            nc.vector.tensor_copy(pq[:, 0, 2:4, :], acc[:, 0, 1, :].rearrange("p (c s) -> p c s", s=S)).then_inc(acc_free, 1)
            low_parts(n0 + 1, 0, chunks=(3,))
            gates(0, 0)
            low_parts(n0 + 1, 1)
            dot_products(0, 0, 0, range(0, 3), first=True)
            low_parts(n0 + 2, 0, chunks=(1,))
            evacuate_T(n0 + 1, 1, pq[:, 1, :, :])
            low_parts(n0 + 2, 0, chunks=(3,))
            peer_scores(1)
            dot_products(0, 0, 0, range(3, 5))
            low_parts(n0 + 2, 1)
            peer_scores(2)
            dot_products(0, 0, 0, range(5, 8))
            low_parts(n0 + 3, 0, chunks=(1,))
            evacuate_T(n0 + 2, 0, pq[:, 0, :, :])
            low_parts(n0 + 3, 0, chunks=(3,))
            dot_products(0, 0, 0, range(8, 10))
            route(1, 1, 0, 1, amid=lambda: low_parts(n0 + 3, 1, chunks=(HALF + 1,)))
            low_parts(n0 + 3, 1, chunks=(HALF + 3,))
            peer_scores(3)
            dot_products(0, 0, 0, range(10, 13))
            gates(1, 1)
            evacuate_T(n0 + 3, 1, pq[:, 1, :, :])
            dot_products(0, 0, 0, range(13, 16))
            peer_scores(4)
            dve.wait_ge(scores_ready, 5)
            period(1, 1, 0, 0, 2, second=True)
            HB = PH // 2
            with dve.Fori(0, HB - 2) as i:
                step.enter(i, 2 * ROUTE_STEPS)
                two_periods(i + 1, 0, 0)
            step.leave(HB - 2)
            two_periods(HB - 1, 0, 1)
            with dve.Fori(0, HB - 1) as i:
                step.enter(i, 2 * ROUTE_STEPS)
                two_periods(i + HB, 1, 1)
            step.leave(HB - 1)
            finish(0)
            two_periods(2 * HB - 1, 1, 1, last=True)
            weights(GROUPS - 1, 1)
            dve.wait_ge(wts_ready, GROUPS)
            for m, k in enumerate(BY_DVE):
                dve.wait_ge(v_landed[k % 4], (GROUPS - 1) * (16 * TOP // 4) + 16 * (k // 4 + 1))
                nc.vector.scalar_tensor_tensor(y_sum[:, 1, :], v_ring[:, k % 4, :], wts[:, 1, k:k + 1], (y_sum if m else h)[:, 1, :],
                                               ALU.mult, ALU.add).then_inc(v_added, 1)
                dve.wait_ge(v_added, m + 1)
            finish(1)

        @block.tensor
        def _(pe):
            def chunk_ready(n, j):
                pe.wait_ge((lo_even, lo_odd)[j % 2], n * HALF + (j // 2 + 1))

            def products(n, q, hi, lo, turned, between=None, ready=None):
                pe.wait_ge(acc_free, n + 1)
                for j in range(CH):
                    if ready is not None:
                        pe.wait_ge(ready[0], ready[1] + j + 1)
                    chunk_ready(n, j)
                    s = j % RING
                    for kk in range(KC):
                        kt = j * KC + kk
                        first, last = kt == 0, kt == KT - 1
                        if turned:
                            for ct in range(CT):
                                o = acc[:, q, ct // 2, ct % 2 * S:(ct % 2 + 1) * S]
                                wh, wl = (w[:, s, kk, ct * P:(ct + 1) * P] for w in (w_hi, w_lo))
                                nc.tensor.matmul(o, wh, hi[:, kt, :], start=first and ct % 2 == 0, stop=False, skip_group_check=True)
                                nc.tensor.matmul(o, wh, lo[:, kt, :], start=False, stop=False, skip_group_check=True)
                                ins = nc.tensor.matmul(o, wl, hi[:, kt, :], start=False, stop=last and ct % 2 == 1, skip_group_check=True)
                        else:
                            for t in range(TT):
                                o = acc[:, q, t, :]
                                xh, xl = (a[:, kt, t * P:(t + 1) * P] for a in (hi, lo))
                                nc.tensor.matmul(o, xh, w_hi[:, s, kk, :], start=first, stop=False)
                                nc.tensor.matmul(o, xh, w_lo[:, s, kk, :], start=False, stop=False)
                                ins = nc.tensor.matmul(o, xl, w_hi[:, s, kk, :], start=False, stop=last)
                    ins.then_inc(chunk_used, 1)
                    if j == HALF - 1 and between is not None:
                        between()

            def transposes(pair, bank, src, free=None, count=0):
                if free is not None:
                    pe.wait_ge(free, count)
                for kk in range(2):
                    for t in range(TT):
                        ins = nc.tensor.transpose(misc[:, bank, kk * S + t * P:kk * S + (t + 1) * P], src(t, kk), ident[:, :])
                ins.then_inc(tr_ready, 1)

            pe.wait_ge(consts, 1)
            pe.wait_ge(small_landed, 16 * 7)
            nc.tensor.transpose(misc[:, 3, 0:NG], gain_rows[:, :], ident[0:NG, 0:NG]).then_inc(gains_T, 1)
            pe.wait_ge(normed_ready, 2)
            pe.wait_ge(gains_ready, 1)
            for p in range(PAIRS):
                transposes(p, p % 4, lambda t, kk: normed[:, t, (2 * p + kk) * P:(2 * p + kk + 1) * P],
                           tr_lo if p >= 4 else None, p - 3)
            with pe.Fori(0, T_IN // 2) as b:
                for q in range(2):
                    products(b * 2 + q, q, t1_hi, t1_lo, True, ready=(tr_lo, 0) if q == 0 else None)
            pe.wait_ge(wf_ready, 1)
            o = misc[:, 0, 0:S]
            for kt in range(KT):
                nc.tensor.matmul(o, wf_hi[:, kt, :], t1_hi[:, kt, :], start=kt == 0, stop=False)
                nc.tensor.matmul(o, wf_hi[:, kt, :], t1_lo[:, kt, :], start=False, stop=False)
                ins = nc.tensor.matmul(o, wf_lo[:, kt, :], t1_hi[:, kt, :], start=False, stop=kt == KT - 1)
            ins.then_inc(f_done, 1)
            products(T_IN, 0, t1_hi, t1_lo, False)
            products(T_IN + 1, 1, t1_hi, t1_lo, False)
            pe.wait_ge(cum_ready, 2)
            pe.wait_ge(consts, 6)
            for f in range(FH):
                for t in range(TT):
                    u = f * TT + t
                    if u >= 4:
                        pe.wait_ge(qk_read, u - 3)
                    keys = (t + 1) * P
                    o = misc[:, u % 4, 0:keys]
                    nc.tensor.matmul(o, foxT[:, PW // P + f, t * P:(t + 1) * P], foxT[:, PW // P + FH + f, 0:keys], start=True, stop=False)
                    nc.tensor.matmul(o, sel_r[:, f, :], cum_hi[:, 0:keys], start=False, stop=False)
                    nc.tensor.matmul(o, sel_r[:, f, :], cum_lo[:, 0:keys], start=False, stop=True).then_inc(qk_done, 1)
            pe.wait_ge(qk_read, FH * TT)
            pe.wait_ge(diff_ready, len(WINDOWS))
            pe.wait_ge(pool_landed, 16)
            for g in range(len(WINDOWS)):
                for dt in range(GT):
                    for ct in range(GT):
                        ins = nc.tensor.matmul(misc[:, g, dt * S:(dt + 1) * S], poolw[:, g, ct, dt * P:(dt + 1) * P],
                                               diff[:, g * GT + ct, :], start=ct == 0, stop=ct == GT - 1)
                ins.then_inc(poolT_done, 1)
            pe.wait_ge(normed_ready, 4)
            for p in range(PAIRS):
                transposes(PAIRS + p, p % 4, lambda t, kk: normed[:, t, (2 * p + kk) * P:(2 * p + kk + 1) * P], tr_lo, PAIRS + p + 1)
            n0, items = ITEMS["k"]
            with pe.Fori(0, items // 2) as b:
                for q in range(2):
                    products(b * 2 + (n0 + q), q, t2_hi, t2_lo, True, ready=(tr_lo, PAIRS + 4) if q == 0 else None)
            pe.wait_ge(fp_ready, FH)
            for f in range(FH + 1):
                if f < FH:
                    if f >= 2:
                        pe.wait_ge(pT_copied, f - 1)
                    b = f % 2
                    nc.tensor.transpose(misc[:, b, 0:P], foxs[:, f, 0:P], ident[:, :])
                    nc.tensor.transpose(misc[:, b, P:2 * P], foxs[:, f, P:2 * P], ident[:, :])
                    nc.tensor.transpose(misc[:, b, 2 * P:3 * P], foxs[:, f, 2 * P:3 * P], ident[:, :]).then_inc(pT_done, 1)
                if f:
                    e = f - 1
                    pe.wait_ge(pT_copied, e + 1)
                    if e >= 2:
                        pe.wait_ge(fo_lo, e - 1)
                    o = misc[:, 2 + e % 2, 0:S]
                    nc.tensor.matmul(o, foxv[:, 0, e * P:(e + 1) * P], pT[:, e % 2, 0:2 * P], start=True, stop=False)
                    nc.tensor.matmul(misc[:, 2 + e % 2, P:S], foxv[:, 1, e * P:(e + 1) * P], pT[:, e % 2, 2 * P:3 * P],
                                     start=False, stop=True).then_inc(fo_done, 1)
            n0, items = ITEMS["v"]
            with pe.Fori(0, items // 2) as b:
                for q in range(2):
                    products(b * 2 + (n0 + q), q, t2_hi, t2_lo, False)
            pe.wait_ge(fo_lo, FH)

            def turn(name, pair0, i):
                pe.wait_ge(acc_free, ITEMS[name][0] + i + 3)
                for p in range(2):
                    transposes(None, 2 * (i % 2) + p, lambda t, kk: hs[:, i % 2, t, (2 * p + kk) * P:(2 * p + kk + 1) * P],
                               tr_lo, pair0 + 4 + 2 * i + p - 3)

            def sub_keys():
                pe.wait_ge(sk_landed, 16)
                pe.wait_ge(xo_lo, 2 * XH)
                for p in range(4):
                    for a in range(4):
                        ins = nc.tensor.transpose(misc[:, p, a * P:(a + 1) * P], skraw[:, 4 * p + a, :], ident[:, :])
                    ins.then_inc(skT_done, 1)

            def residual_items(name, hi, lo, pair0, ready=None, first=None):
                n0, items = ITEMS[name]
                for i in range(items):
                    products(n0 + i, i % 2, hi, lo, False, ready=None if i else ready,
                             between=(lambda: turn(name, pair0, i - 1)) if i else first)

            def x_scores(i):
                q = i % 2
                pe.wait_ge(acc_free, ITEMS["q"][0] + i + 3)
                if i >= 2:
                    pe.wait_ge(xexp_done, TT * (i - 1))
                for t in range(TT):
                    for c in range(XT):
                        ins = nc.tensor.matmul(misc[:, 2 * q + t, 0:S], qs[:, q, c, t * P:(t + 1) * P],
                                               memk[:, i * XT + c, :], start=c == 0, stop=c == XT - 1)
                    ins.then_inc(xs_done, 1)

            def x_turn(hd):
                pe.wait_ge(xp_ready, TT * (hd + 1))
                if hd >= 2:
                    pe.wait_ge(xpT_copied, hd - 1)
                else:
                    pe.wait_ge(xexp_done, TT * (XH - 1))
                for m in range(TT):
                    for t in range(TT):
                        ins = nc.tensor.transpose(misc[:, hd % 2, m * S + t * P:m * S + (t + 1) * P],
                                                  xp[:, hd, t, m * P:(m + 1) * P], ident[:, :])
                ins.then_inc(xpT_done, 1)

            def x_values(hd):
                pe.wait_ge(xpT_copied, hd + 1)
                for u in (2 * hd, 2 * hd + 1):
                    if u >= 4:
                        pe.wait_ge(xo_lo, u - 3)
                    elif u >= 2:
                        pe.wait_ge(xexp_done, TT * XH)
                    for d2 in range(2):
                        for m in range(TT):
                            dt = 2 * u + d2
                            ins = nc.tensor.matmul(xo_bank(u)[:, d2 * S:(d2 + 1) * S], memv[:, m, dt * P:(dt + 1) * P],
                                                   xpT[:, hd % 2, m, :], start=m == 0, stop=m == TT - 1)
                    ins.then_inc(xo_done, 1)

            residual_items("out", t1_hi, t1_lo, PAIR0["h1"])
            n0, items = ITEMS["q"]
            for i in range(items):
                products(n0 + i, i % 2, t2_hi, t2_lo, True, ready=None if i else (tr_lo, PAIR0["h1"] + 4),
                         between=(lambda: x_scores(i - 1)) if i else (lambda: turn("out", PAIR0["h1"], ITEMS["out"][1] - 1)))
            x_turn(0)
            x_scores(XH - 1)
            x_turn(1)
            for hd in range(XH):
                x_values(hd)
                if hd + 2 < XH:
                    x_turn(hd + 2)
            residual_items("o", t1_hi, t1_lo, PAIR0["h2"], ready=(xo_lo, 0), first=sub_keys)

            def p_scores(b):
                if b == 0:
                    pe.wait_ge(half_read, 1)
                    i, cs = 0, range(0, 2)
                else:
                    i, cs = b - 1, (range(CT) if b > 1 else range(2, CT))
                    pe.wait_ge(acc_free, ITEMS["peer"][0] + i + 3)
                if b >= 2:
                    pe.wait_ge(scores_ready, b - 1)
                for t in range(TT):
                    for c in cs:
                        at = (c - cs[0]) * KEYS
                        ins = nc.tensor.matmul(misc[:, 2 * (b % 2) + t, at:at + KEYS], pq[:, i % 2, c, t * P:(t + 1) * P],
                                               skT[:, i * CT + c, :], start=True, stop=True)
                    ins.then_inc(ps_done, 1)

            n0, items = ITEMS["peer"]
            pe.wait_ge(acc_free, n0 + 1)
            for j in range(CH):
                head, s = j // HALF, j % RING
                if head == 0:
                    pe.wait_ge(tr_lo, PAIR0["h2"] + 4 + (j + 1) * WKC // 2)
                chunk_ready(n0, j)
                for kk in range(WKC):
                    kt = j % HALF * WKC + kk
                    for ct in range(2):
                        o = acc[:, 0, head, ct * S:(ct + 1) * S]
                        wh, wl = (head_chunk(w[:, s], kk, ct * P, P) for w in (w_hi, w_lo))
                        nc.tensor.matmul(o, wh, t2_hi[:, kt, :], start=kt == 0 and ct == 0, stop=False, skip_group_check=True)
                        nc.tensor.matmul(o, wh, t2_lo[:, kt, :], start=False, stop=False, skip_group_check=True)
                        ins = nc.tensor.matmul(o, wl, t2_hi[:, kt, :], start=False, stop=kt == KT - 1 and ct == 1, skip_group_check=True)
                ins.then_inc(chunk_used, 1)
                if j == 0:
                    turn("o", PAIR0["h2"], ITEMS["o"][1] - 1)
                if j == HALF:
                    pe.wait_ge(skT_copied, 4)
                    p_scores(0)
            products(n0 + 1, 1, t2_hi, t2_lo, True, between=lambda: p_scores(1))
            products(n0 + 2, 0, t2_hi, t2_lo, True, between=lambda: p_scores(2))
            products(n0 + 3, 1, t2_hi, t2_lo, True, between=lambda: p_scores(3))
            p_scores(4)
            pe.wait_ge(scores_ready, items + 1)
            for c in range(TT):
                banks = [misc[:, n, :] for n in range(4)] if c == 0 else [acc[:, n // 2, n % 2, :] for n in range(4)]
                for o in banks:
                    nc.tensor.matmul(o, zeros[:, 0:P], zeros[:, :], start=True, stop=False)
                with pe.Fori(c * PH, (c + 1) * PH - c) as g:
                    for k in range(TOP):
                        pe.wait_ge(v_landed[k % 4], g * (16 * TOP // 4) + 16 * (k // 4 + 1))
                        pe.wait_ge(diag_ready, g * TOP + (k + 1))
                        for n, o in enumerate(banks):
                            ins = nc.tensor.matmul(o, diag[:, k % 4, :], v_ring[:, k % 4, n * CW:(n + 1) * CW], start=False, stop=False)
                        ins.then_inc(v_used, 1)
                if c == TT - 1:
                    g = GROUPS - 1
                    for m, k in enumerate(BY_PE):
                        pe.wait_ge(v_landed[k % 4], g * (16 * TOP // 4) + 16 * (k // 4 + 1))
                        pe.wait_ge(diag_ready, g * TOP + m + 1)
                        for n, o in enumerate(banks):
                            ins = nc.tensor.matmul(o, diag[:, m % 4, :], v_ring[:, k % 4, n * CW:(n + 1) * CW], start=False, stop=False)
                        ins.then_inc(v_used, 1)
                for o in banks:
                    ins = nc.tensor.matmul(o, zeros[:, 0:P], zeros[:, :], start=False, stop=True)
                ins.then_inc(y_done, 1)


_INS = ['x', 'mem', 'mix_norm', 'w_in', 'b_forget', 'pool_w', 'pool_scale', 'w_out', 'xattn_norm', 'mem_norm', 'xattn_wq',
        'xattn_wk', 'xattn_wv', 'xattn_wo', 'peer_norm', 'peer_wq', 'peer_sub_keys', 'peer_u', 'peer_v', 'final_norm']
_OUTS = [((1, 256, 2048), 'float32')]


def kernel(**inputs):
    import numpy as _np
    import concourse.bacc as _bacc
    from concourse import mybir as _mybir
    from concourse.bass_utils import run_bass_kernel_spmd as _run

    nc = _bacc.Bacc("TRN2", target_bir_lowering=False, num_devices=1)
    arrays, args = {}, []
    for name in _INS:
        a = _np.ascontiguousarray(inputs[name])
        arrays[f"in_{name}_dram"] = a
        args.append(nc.dram_tensor(f"in_{name}_dram", a.shape, _mybir.dt.from_np(a.dtype), kind="ExternalInput").ap())
    for i, (shape, dtype) in enumerate(_OUTS):
        dt = _mybir.dt.from_np(_np.dtype(dtype))
        args.append(nc.dram_tensor(f"out_{i}_dram", shape, dt, kind="ExternalOutput").ap())
    hybrid_layer(nc, *args)
    r = _run(nc, [arrays], core_ids=[0])
    return r.results[0]["out_0_dram"]
```

```python
import concourse.bass as bass
from concourse import mybir
from contextlib import ExitStack


class Steps:

    def __init__(self, engine, semaphore, passed=None):
        self.engine, self.semaphore, self.passed, self.n = engine, semaphore, passed, 0

    def __call__(self, instruction, apart=False):
        instruction.then_inc(self.semaphore, 1)
        self.n, self.steps = self.n + 1, self.steps + 1
        self.engine.wait_ge(self.semaphore, self.n)
        if apart:
            self.engine.sem_inc(self.passed, 1)

    steps = 0

    def enter(self, i, per_turn):
        self.start, self.steps, self.per_turn = self.n, 0, per_turn
        self.n = i * per_turn + self.start

    def leave(self, turns):
        assert self.steps == self.per_turn, (self.steps, self.per_turn)
        self.n = self.start + turns * self.per_turn



def hybrid_layer(
    nc: bass.Bass, x, mem, mix_norm, w_in, b_forget, pool_w, pool_scale, w_out, xattn_norm, mem_norm,
    xattn_wq, xattn_wk, xattn_wv, xattn_wo, peer_norm, peer_wq, peer_sub_keys, peer_u, peer_v,
    final_norm, out,
):
    F32, F32R, BF16, U32 = mybir.dt.float32, mybir.dt.float32r, mybir.dt.bfloat16, mybir.dt.uint32
    ALU, ACT, AX = mybir.AluOpType, mybir.ActivationFunctionType, mybir.AxisListType

    P = 128
    S, D = x.shape[1], x.shape[2]
    TT = S // P
    KT = D // P
    PW = pool_scale.shape[1]
    FH = b_forget.shape[1]
    FD = (D - PW) // FH
    WINDOWS = (2, 4, 8, 16)
    GT = PW // len(WINDOWS) // P
    XH = 4
    XT = D // XH // P
    XSCALE, FSCALE = float(D // XH) ** -0.5, float(FD) ** -0.5
    PH = peer_sub_keys.shape[1]
    KEYS = peer_sub_keys.shape[3]
    TOP = 16
    EPS = 1e-6
    LOW, MASKED = -3.0e38, -1.0e30
    assert TT == 2 and FD == P and XT == 4 and KEYS == P and S == mem.shape[1]

    CW, KC = 512, 2
    CH = KT // KC
    RING = 4
    HALF = CH // 2
    CT = CW // P
    assert HALF == RING
    ITEMS = {}
    at = 0
    for name, cols in (("in", PW + 3 * (D - PW)), ("k", D), ("v", D), ("out", D), ("q", D), ("o", D), ("peer", D)):
        ITEMS[name] = (at, cols // CW)
        at += cols // CW
    LAST = at - 1
    T_IN = (PW + 2 * (D - PW)) // CW
    GROUPS = TT * PH

    def rows(w):
        return w.rearrange("o (k p) n -> p (o k) n", p=P)

    base = 16512
    KB = 1024
    at_h, at_t1, at_t2 = base, base + 16 * KB, base + 48 * KB
    at_k, at_v, at_f = base + 80 * KB, base + 96 * KB, base + 120 * KB
    at_raw, at_split, at_small = base + 140 * KB, base + 156 * KB, base + 188 * KB
    small = [at_small]

    def put(name, shape, dt, offset=None):
        size = 4 if dt != BF16 else 2
        for n in shape[1:]:
            size *= n
        if offset is None:
            offset, small[0] = small[0], small[0] + (size + 31) // 32 * 32
        return nc.alloc_sbuf_tensor_at(name, shape, dt, offset=offset)

    h = put("h", [P, TT, D], F32, at_h)
    t1_hi, t1_lo = put("t1_hi", [P, KT, S], F32R, at_t1), put("t1_lo", [P, KT, S], F32R, at_t1 + 16 * KB)
    t2_hi, t2_lo = put("t2_hi", [P, KT, S], F32R, at_t2), put("t2_lo", [P, KT, S], F32R, at_t2 + 16 * KB)
    raw = put("raw", [P, RING, KC, CW], F32, at_raw)
    w_hi = put("w_hi", [P, RING, KC, CW], F32R, at_split)
    w_lo = put("w_lo", [P, RING, KC, CW], F32R, at_split + 16 * KB)
    poolw = put("poolw", [P, len(WINDOWS), GT, GT * P], F32, at_t2)
    inv = put("inv", [P, len(WINDOWS), S], F32, at_t2 + 8 * KB)
    diff = put("diff", [P, len(WINDOWS) * GT, S], F32, at_t2 + 12 * KB)
    sel = put("sel", [FH, FH, P], F32, at_t2 + 20 * KB)
    sel_r = put("sel_r", [FH, FH, P], F32R, at_t2 + 24 * KB)
    cum = put("cum", [FH, S], F32, at_t2 + 28 * KB)
    cum_hi = put("cum_hi", [FH, S], F32R, at_t2 + 29 * KB)
    cum_lo = put("cum_lo", [FH, S], F32R, at_t2 + 30 * KB)
    wf = put("wf", [P, KT, FH], F32, at_t2 + 31 * KB)
    wf_hi = put("wf_hi", [P, KT, P], F32R, at_f)
    wf_lo = put("wf_lo", [P, KT, P], F32R, at_f + 8 * KB)
    normed = put("normed", [P, TT, D], F32, at_k)
    memk = put("memk", [P, KT, S], F32, at_k)
    hn = put("hn", [P, TT, D], F32, at_k)
    foxT = put("foxT", [P, PW // P + 2 * FH, S], F32, at_v)
    memv = put("memv", [P, TT, D], F32, at_v)
    peer_gain = put("peer_gain", [P, D], F32, at_v)
    scores = put("scores", [P, TT, PH * 2 * KEYS], F32, at_v)
    skT = put("skT", [P, PH * 2, KEYS], F32, at_v + 16 * KB)
    foxv = put("foxv", [P, TT, FH * P], F32, at_f)
    foxs = put("foxs", [P, FH, 3 * P], F32, at_f + 8 * KB)
    pad = 16
    winA = put("winA", [P, GT, pad + S], F32, at_f + 8 * KB)
    winB = put("winB", [P, GT, pad + S], F32, at_f + 8 * KB + 2304)
    fz, fa, fe, fones = (put(n, [FH, S], F32, at_f + (16 + k) * KB) for k, n in enumerate(("fz", "fa", "fe", "fones")))
    hs = put("hs", [P, 2, TT, CW], F32, at_f)
    qs = put("qs", [P, 2, XT, S], F32, at_f)
    xp = put("xp", [P, XH, TT, S], F32, at_f + 8 * KB)
    xpT = put("xpT", [P, 2, TT, S], F32, at_f)
    skraw = put("skraw", [P, PH * 2, P], F32, at_f + 8 * KB)
    pq = put("pq", [P, 2, CT, S], F32, at_f)
    u_ring = put("u_ring", [P, 4, D], F32, at_t1)
    v_ring = put("v_ring", [P, 4, D], F32, at_split)
    final_gain = put("final_gain", [P, D], F32, at_raw)
    product = put("product", [P, D], BF16, at_f + 16 * KB)
    y_sum = put("y_sum", [P, TT, D], F32, at_t2)
    y_out = put("y_out", [P, TT, D], F32, at_t2 + 16 * KB)
    ident = put("ident", [P, P], F32)
    mask = put("mask", [P, 2 * P], F32)
    zeros = put("zeros", [P, CW], BF16)
    junk = put("junk", [P, 2, CW], BF16)
    NG = 4 * KT + PW // P
    gain_rows = put("gain_rows", [NG, P], F32)
    gains = put("gains", [P, NG], F32)
    G_MIX, G_MEM, G_X, G_PEER, G_POOL = 0, KT, 2 * KT, 3 * KT, 4 * KT
    bf = put("bf", [FH, 1], F32)
    warm = put("warm", [P, 1], F32)
    sq = put("sq", [P, TT, 4], F32)
    ss = put("ss", [P, TT], F32)
    rt = put("rt", [P, TT], F32)
    rstd = put("rstd", [P, TT], F32)
    xfac = put("xfac", [P, TT], F32)
    fmax = put("fmax", [P, FH, TT], F32)
    fneg = put("fneg", [P, FH, TT], F32)
    fsum = put("fsum", [P, FH, TT], F32)
    frec = put("frec", [P, FH, TT], F32)
    pT = put("pT", [P, 2, 3 * P], F32)
    xmax = put("xmax", [P, 2, TT], F32)
    xneg = put("xneg", [P, 2, TT], F32)
    xsum = put("xsum", [P, 2, TT], F32)
    xrec = put("xrec", [P, 2, TT], F32)
    cur = put("cur", [P, 2, KEYS], F32, at_f + 8 * KB)
    rest = put("rest", [P, 2, KEYS], F32, at_f + 9 * KB)
    top = put("top", [P, 2, TOP], F32)
    top_at = put("top_at", [P, 2, TOP], U32)
    cand = put("cand", [P, TOP, TOP], F32, at_f + 10 * KB)
    cand_rest = put("cand_rest", [P, TOP, TOP], F32, at_f + 11 * KB)
    best = put("best", [P, TOP], F32)
    pos = put("pos", [P, TOP], U32)
    ab = put("ab", [P, 2, TOP], U32)
    hot = put("hot", [P, 2, TOP, TOP], F32, at_f + 12 * KB)
    picked = put("picked", [P, 2, TOP], F32)
    iota = put("iota", [P, TOP], F32)
    neg_best = put("neg_best", [P, 1], F32)
    exps = put("exps", [P, TOP], F32)
    exp_sum = put("exp_sum", [P, 1], F32)
    exp_rec = put("exp_rec", [P, 1], F32)
    gate = put("gate", [P, 2, TOP], F32)
    idx_u = put("idx_u", [P, 2, TOP], U32)
    idx_v = put("idx_v", [P, 2, TOP], U32)
    dots = put("dots", [P, 2, TOP], F32)
    acts = put("acts", [P, 2, TOP], F32)
    wts = put("wts", [P, 2, TOP], F32)
    diag = put("diag", [P, 4, P], F32, at_f + 14 * KB)
    assert small[0] <= 229344, small[0]

    w_in_r, w_k_r, w_v_r, w_out_r = rows(w_in), rows(xattn_wk), rows(xattn_wv), rows(w_out)
    w_q_r, w_o_r, w_peer_r = rows(xattn_wq), rows(xattn_wo), rows(peer_wq)
    u_rows, v_rows = peer_u.rearrange("o n d -> (o n) d"), peer_v.rearrange("o n d -> (o n) d")

    with ExitStack() as ctx:
        acc = ctx.enter_context(nc.psum_tensor("acc", [P, 2, 2, CW], F32))
        misc = ctx.enter_context(nc.psum_tensor("misc", [P, 4, CW], F32))

        def sem(name):
            return ctx.enter_context(nc.semaphore(name))

        mem_landed, small_landed, pool_landed = sem("mem_landed"), sem("small_landed"), sem("pool_landed")
        sk_landed, pgain_landed, fgain_landed, out_landed = sem("sk_landed"), sem("pgain_landed"), sem("fgain_landed"), sem("out_landed")
        x_landed = [sem(f"x_landed{t}") for t in range(TT)]
        raw_landed = [sem(f"raw_landed{s}") for s in range(RING)]
        hi_done, lo_even, lo_odd, chunk_used = sem("hi_done"), sem("lo_even"), sem("lo_odd"), sem("chunk_used")
        acc_free, half_read = sem("acc_free"), sem("half_read")
        consts, gains_T, gains_ready, wf_hi_done, wf_ready = sem("consts"), sem("gains_T"), sem("gains_ready"), sem("wf_hi_done"), sem("wf_ready")
        inv_ready = sem("inv_ready")
        squares, var_ready, root_ready, rstd_ready = sem("squares"), sem("var_ready"), sem("root_ready"), sem("rstd_ready")
        normed_ready = [sem(f"normed_ready{t}") for t in range(TT)]
        tr_ready, tr_hi, tr_lo = sem("tr_ready"), sem("tr_hi"), sem("tr_lo")
        f_done, fa_ready, fl_ready, cum_ready = sem("f_done"), sem("fa_ready"), sem("fl_ready"), sem("cum_ready")
        diff_ready, poolT_done = sem("diff_ready"), sem("poolT_done")
        qk_done, qk_read, fneg_ready, fexp_done, fp_ready = sem("qk_done"), sem("qk_read"), sem("fneg_ready"), sem("fexp_done"), sem("fp_ready")
        pT_done, pT_copied, fo_done, fo_hi, fo_lo = sem("pT_done"), sem("pT_copied"), sem("fo_done"), sem("fo_hi"), sem("fo_lo")
        h_copied = sem("h_copied")
        xs_done, xneg_ready, xexp_done, xp_ready = sem("xs_done"), sem("xneg_ready"), sem("xexp_done"), sem("xp_ready")
        xpT_done, xpT_copied, xo_done, xo_hi, xo_lo = sem("xpT_done"), sem("xpT_copied"), sem("xo_done"), sem("xo_hi"), sem("xo_lo")
        skT_done, skT_copied, ps_done = sem("skT_done"), sem("skT_copied"), sem("ps_done")
        first_scores, scores_ready = sem("first_scores"), sem("scores_ready")
        u_landed = [sem(f"u_landed{s}") for s in range(4)]
        v_landed = [sem(f"v_landed{s}") for s in range(4)]
        routed, idx_v_ready, nbest_ready, gexp_done = sem("routed"), sem("idx_v_ready"), sem("nbest_ready"), sem("gexp_done")
        dot_done, gelu_done, wts_ready, diag_ready, v_used = sem("dot_done"), sem("gelu_done"), sem("wts_ready"), sem("diag_ready"), sem("v_used")
        y_gained, y_rstd = sem("y_gained"), sem("y_rstd")
        y_done, y_added, y_squared, y_var, y_root, y_ready = sem("y_done"), sem("y_added"), sem("y_squared"), sem("y_var"), sem("y_root"), sem("y_ready")
        dve_step, act_step, pool_step, passed = sem("dve_step"), sem("act_step"), sem("pool_step"), sem("passed")
        x_squared, table_ready, zero_ready, v_added, y_scaled = sem("x_squared"), sem("table_ready"), sem("zero_ready"), sem("v_added"), sem("y_scaled")
        block = ctx.enter_context(nc.Block())

        def wait_apart(engine, semaphore, value):
            engine.wait_ge(semaphore, value)
            engine.sem_inc(passed, 1)

        HW = CW // 2
        WKC = KC * CW // HW

        def head_chunk(slot, kt, col, width):
            at = kt * HW + col
            return slot[:, at // CW, at % CW:at % CW + width]

        def xo_bank(u):
            return acc[:, 1, u % 2, :] if u % 4 < 2 else misc[:, u % 4, :]

        PAIRS = KT // 2
        PAIR0 = {"x": 0, "mem": PAIRS, "h1": 2 * PAIRS, "h2": 3 * PAIRS}

        BY_DVE = [2, 5, 8, 11, 12, 13, 14, 15]
        BY_PE = [k for k in range(TOP) if k not in BY_DVE]

        E0 = ITEMS["peer"][0]
        EARLY = [(None, range(0, 4)), ((E0 + 1, 0, (2,)), ()), ((E0 + 1, 1, (HALF,)), range(4, 7)), ((E0 + 1, 1, (HALF + 2,)), ()),
                 ((E0 + 2, 0, (0,)), range(7, 10)), ((E0 + 2, 0, (2,)), ()), ((E0 + 2, 1, (HALF,)), range(10, 11)),
                 ((E0 + 2, 1, (HALF + 2,)), range(11, 13)), ((E0 + 3, 0), range(13, 16)), ((E0 + 3, 1), ())]

        def score_batch(b):
            return (b * HW, HW) if b < 2 else ((b - 1) * CW, CW)

        @block.sync
        def _(sp):
            def item(n, w, i, first=False, chunks=range(CH)):
                for j in chunks:
                    if not (first and j < RING):
                        sp.wait_ge((lo_even, lo_odd)[j % 2], n * HALF + (j // 2 - 1))
                    sp.dma_start(raw[:, j % RING, :, :],
                                 w[:, j * KC:(j + 1) * KC, bass.ts(i, CW)]).then_inc(raw_landed[j % RING], 16)

            for t in range(TT):
                sp.dma_start(h[:, t, :], x[0, t * P:(t + 1) * P, :]).then_inc(x_landed[t], 16)
            n0, _ = ITEMS["in"]
            item(n0, w_in_r, 0, first=True, chunks=range(1))
            for v, r in ((mix_norm, G_MIX), (mem_norm, G_MEM), (xattn_norm, G_X), (peer_norm, G_PEER), (pool_scale, G_POOL)):
                v2 = v.rearrange("o (k p) -> (o k) p", p=P)
                sp.dma_start(gain_rows[r:r + v2.shape[0], :], v2).then_inc(small_landed, 16)
            sp.dma_start(bf[:, :], b_forget.rearrange("o f -> f o")).then_inc(small_landed, 16)
            sp.dma_start(wf[:, :, :], w_in_r[:, :, PW + 3 * FH * P:]).then_inc(small_landed, 16)
            item(n0, w_in_r, 0, first=True, chunks=range(1, CH))
            sp.dma_start(poolw[:, :, :, :], pool_w[0].rearrange("g (c p) d -> p g c d", p=P)).then_inc(pool_landed, 16)
            sp.wait_ge(tr_ready, PAIRS)
            sp.dma_start(normed[:, :, :], mem[0].rearrange("(t p) d -> p t d", p=P)).then_inc(mem_landed, 16)
            with sp.Fori(1, ITEMS["in"][1]) as i:
                item(i, w_in_r, i)
            for name, w in (("k", w_k_r), ("v", w_v_r), ("out", w_out_r), ("q", w_q_r)):
                n0, items = ITEMS[name]
                with sp.Fori(0, items) as i:
                    item(i + n0, w, i)
            n0, items = ITEMS["o"]
            item(n0, w_o_r, 0, chunks=range(HALF))
            sp.wait_ge(xpT_done, XH)
            sp.dma_start(skraw[:, :, :], peer_sub_keys[0].rearrange("h c k d -> k (h c) d")).then_inc(sk_landed, 16)
            item(n0, w_o_r, 0, chunks=range(HALF, CH))
            sp.wait_ge(xo_done, 2 * XH)
            sp.dma_start(peer_gain[:, :], peer_norm[0:1, :].to_broadcast([P, D])).then_inc(pgain_landed, 16)
            with sp.Fori(1, items) as i:
                item(i + n0, w_o_r, i)
            n0, items = ITEMS["peer"]
            for j in range(CH):
                sp.wait_ge((lo_even, lo_odd)[j % 2], n0 * HALF + (j // 2 - 1))
                kt = j % HALF * WKC
                sp.dma_start(raw[:, j % RING, :, :].rearrange("p k (a c) -> p (k a) c", c=HW),
                             w_peer_r[:, kt:kt + WKC, j // HALF * HW:(j // HALF + 1) * HW]).then_inc(raw_landed[j % RING], 16)
            with sp.Fori(1, items) as i:
                item(i + n0, w_peer_r, i)
            sp.wait_ge(scores_ready, items)
            sp.dma_start(final_gain[:, :], final_norm.rearrange("(o d) -> o d", o=1).to_broadcast([P, D])).then_inc(fgain_landed, 16)
            for c in range(TT):
                for half in range(2):
                    sp.wait_ge((y_scaled, y_ready)[half], c + 1)
                    cols = slice(half * D // 2, (half + 1) * D // 2)
                    sp.dma_start(out[0, c * P:(c + 1) * P, cols], y_out[:, c, cols]).then_inc(out_landed, 16)
            sp.wait_ge(out_landed, 16 * 2 * TT)

        @block.gpsimd
        def _(pool):
            step = Steps(pool, pool_step)
            step(nc.gpsimd.memset(ident[:, :], 0.0))
            nc.gpsimd.affine_select(out=ident[:, :], in_=ident[:, :], compare_op=ALU.not_equal, fill=1.0,
                                    base=0, pattern=[[-1, P]], channel_multiplier=1).then_inc(consts, 1)

            def low_parts(n, half, chunks=None):
                for j in chunks or range(half * HALF, half * HALF + HALF, 2):
                    pool.wait_ge(hi_done, n * CH + (j + 1))
                    nc.gpsimd.tensor_tensor(w_lo[:, j % RING, :, :], raw[:, j % RING, :, :],
                                            w_hi[:, j % RING, :, :].bitcast(F32), ALU.subtract).then_inc(lo_even, 1)

            low_parts(0, 0)
            low_parts(0, 1)
            step(nc.gpsimd.memset(mask[:, :], 0.0))
            nc.gpsimd.affine_select(out=mask[:, P:2 * P], in_=mask[:, P:2 * P], compare_op=ALU.is_ge, fill=MASKED,
                                    base=0, pattern=[[-1, P]], channel_multiplier=1).then_inc(consts, 1)
            step(nc.gpsimd.memset(sel[:, :, :], 0.0))
            nc.gpsimd.affine_select(out=sel[:, :, :], in_=sel[:, :, :], compare_op=ALU.not_equal, fill=1.0,
                                    base=0, pattern=[[-1, FH], [0, P]], channel_multiplier=1).then_inc(consts, 1)
            low_parts(1, 0)
            nc.gpsimd.memset(zeros[:, :], 0.0).then_inc(consts, 1)
            nc.gpsimd.memset(fones[:, :], 1.0).then_inc(consts, 1)
            nc.gpsimd.iota(iota[:, :], pattern=[[1, TOP]], base=0, channel_multiplier=0,
                           allow_small_or_imprecise_dtypes=True).then_inc(consts, 1)
            step(nc.gpsimd.iota(inv[:, 0, :], pattern=[[1, S]], base=1, channel_multiplier=0,
                                allow_small_or_imprecise_dtypes=True))
            for g in range(len(WINDOWS) - 1, -1, -1):
                step(nc.gpsimd.tensor_scalar(inv[:, g, :], inv[:, 0, :], float(WINDOWS[g]), None, ALU.min))
            pool.sem_inc(inv_ready, 1)
            with pool.Fori(1, ITEMS["peer"][0]) as n:
                low_parts(n, 1)
                low_parts(n + 1, 0)

            def gather_u(p, q, k, fresh=False):
                if not (fresh and k < 4):
                    wait_apart(pool, dot_done, p * TOP + (k - 3))
                nc.gpsimd.indirect_dma_start(
                    out=u_ring[:, k % 4, :], out_offset=None, in_=u_rows,
                    in_offset=bass.IndirectOffsetOnAxis(ap=idx_u[:, q, k:k + 1], axis=0)).then_inc(u_landed[k % 4], 16)

            def gather_v(g, q, k, fresh=False):
                if not (fresh and k < 4):
                    wait_apart(pool, v_used, g * TOP + (k - 3))
                nc.gpsimd.indirect_dma_start(
                    out=v_ring[:, k % 4, :], out_offset=None, in_=v_rows,
                    in_offset=bass.IndirectOffsetOnAxis(ap=idx_v[:, q, k:k + 1], axis=0)).then_inc(v_landed[k % 4], 16)

            def period(p, q):
                pool.wait_ge(routed, p + 1)
                pool.wait_ge(idx_v_ready, p)
                for k in range(TOP):
                    gather_u(p, q, k)
                    gather_v(p - 1, 1 - q, k)

            n0, _ = ITEMS["peer"]
            low_parts(n0, 1)
            low_parts(n0 + 1, 0, chunks=(0,))
            pool.wait_ge(routed, 1)
            for part, ks in EARLY:
                if part is not None:
                    low_parts(*part)
                for k in ks:
                    gather_u(0, 0, k, fresh=True)
            pool.wait_ge(routed, 2)
            for k in range(4):
                gather_u(1, 1, k)
            pool.wait_ge(idx_v_ready, 1)
            pool.wait_ge(chunk_used, LAST * CH + CH)
            for k in range(TOP):
                gather_v(0, 0, k, fresh=True)
                if k + 4 < TOP:
                    gather_u(1, 1, k + 4)
            with pool.Fori(1, GROUPS // 2) as b:
                period(b * 2, 0)
                period(b * 2 + 1, 1)
            pool.wait_ge(idx_v_ready, GROUPS)
            for k in range(TOP):
                if k - 4 in BY_DVE:
                    pool.wait_ge(v_added, BY_DVE.index(k - 4) + 1)
                elif k >= 4:
                    pool.wait_ge(v_used, (GROUPS - 1) * TOP + BY_PE.index(k - 4) + 1)
                else:
                    pool.wait_ge(v_used, (GROUPS - 1) * TOP + k - 3)
                nc.gpsimd.indirect_dma_start(
                    out=v_ring[:, k % 4, :], out_offset=None, in_=v_rows,
                    in_offset=bass.IndirectOffsetOnAxis(ap=idx_v[:, 1, k:k + 1], axis=0)).then_inc(v_landed[k % 4], 16)

        @block.scalar
        def _(act):
            def high_parts(n, half, first=False, chunks=None):
                for j in chunks or range(half * HALF, half * HALF + HALF):
                    act.wait_ge(raw_landed[j % RING], n * (2 * 16) + 16 * (j // RING + 1))
                    if not first:
                        act.wait_ge(chunk_used, n * CH + (j - RING + 1))
                    nc.scalar.activation(w_hi[:, j % RING, :, :], raw[:, j % RING, :, :], ACT.Copy).then_inc(hi_done, 1)

            def square_sums(src, i, before, fresh=False):
                for t in range(TT):
                    if not fresh:
                        act.wait_ge(squares, before * TT + (t - 1))
                    nc.scalar.activation(junk[:, t, :], src(t), ACT.Square, accum_out=sq[:, t, bass.ds(i, 1)]).then_inc(squares, 1)

            def root(k):
                act.wait_ge(var_ready, k)
                nc.scalar.activation(rt[:, :], ss[:, :], ACT.Sqrt).then_inc(root_ready, 1)

            def pair_hi(pair, bank, hi, kt, gain):
                act.wait_ge(tr_ready, pair + 1)
                for kk in range(2):
                    ins = nc.scalar.activation(hi[:, bass.ds(kt + kk, 1), :], misc[:, bank, kk * S:(kk + 1) * S], ACT.Copy,
                                               scale=gains[:, bass.ds(kt + (gain + kk), 1)])
                ins.then_inc(tr_hi, 1)

            act.wait_ge(zero_ready, 1)
            nc.scalar.activation(rt[:, 0:1], warm[:, :], ACT.Sqrt).then_inc(table_ready, 1)
            act.wait_ge(x_landed[0], 16)
            nc.scalar.activation(normed[:, 0, :], h[:, 0, :], ACT.Square, accum_out=ss[:, 0:1]).then_inc(x_squared, 1)
            act.wait_ge(x_landed[1], 16)
            nc.scalar.activation(normed[:, 1, D // 2:], h[:, 1, D // 2:], ACT.Square, accum_out=sq[:, 1, 1:2]).then_inc(x_squared, 1)
            act.wait_ge(table_ready, 1)
            root(1)
            act.wait_ge(rstd_ready, 1)
            nc.scalar.activation(normed[:, 1, 0:D // 2], h[:, 1, 0:D // 2], ACT.Copy, scale=rstd[:, 1:2]).then_inc(normed_ready[1], 1)
            high_parts(0, 0, first=True, chunks=range(1))
            act.wait_ge(gains_ready, 1)
            for p in range(PAIRS):
                pair_hi(PAIR0["x"] + p, p % 4, t1_hi, 2 * p, G_MIX)
                if p == 0:
                    nc.scalar.activation(normed[:, 1, D // 2:], h[:, 1, D // 2:], ACT.Copy, scale=rstd[:, 1:2]).then_inc(normed_ready[1], 1)
                if p < 3:
                    high_parts(0, 0, first=True, chunks=(p + 1,))
                if p == 5:
                    high_parts(0, 1, chunks=(HALF,))
            high_parts(0, 1, chunks=range(HALF + 1, CH))
            high_parts(1, 0)
            act.wait_ge(small_landed, 16 * 7)
            act.wait_ge(zero_ready, 3)
            nc.scalar.activation(wf_hi[:, :, 0:FH], wf[:, :, :], ACT.Copy).then_inc(wf_hi_done, 1)
            with act.Fori(1, T_IN) as n:
                high_parts(n, 1)
                high_parts(n + 1, 0)
            act.wait_ge(fa_ready, 1)
            nc.scalar.activation(fe[:, :], fa[:, :], ACT.Exp, scale=-1.0).then_inc(act_step, 1)
            act.wait_ge(act_step, 1)
            nc.scalar.activation(fe[:, :], fe[:, :], ACT.Ln, bias=1.0).then_inc(fl_ready, 1)
            act.wait_ge(mem_landed, 16)
            for i in range(4):
                square_sums(lambda t: normed[:, t, i * CW:(i + 1) * CW], i, i, fresh=i == 0)
                high_parts(T_IN, 1, chunks=(HALF + i,))
            root(2)
            high_parts(T_IN + 1, 0)
            act.wait_ge(rstd_ready, 2)
            nc.scalar.activation(normed[:, 1, :], normed[:, 1, :], ACT.Copy, scale=rstd[:, 1:2]).then_inc(normed_ready[1], 1)
            high_parts(T_IN + 1, 1)
            high_parts(T_IN + 2, 0)
            for g in range(len(WINDOWS)):
                act.wait_ge(poolT_done, g + 1)
                for dt in range(GT):
                    col = G_POOL + g * GT + dt
                    ins = nc.scalar.activation(t1_hi[:, g * GT + dt, :], misc[:, g, dt * S:(dt + 1) * S], ACT.Copy,
                                               scale=gains[:, col:col + 1])
                ins.then_inc(tr_hi, 1)
            for p in range(PAIRS):
                act.wait_ge(tr_ready, PAIR0["mem"] + p + 1)
                for kk in range(2):
                    ins = nc.scalar.activation(t2_hi[:, 2 * p + kk, :], misc[:, p % 4, kk * S:(kk + 1) * S], ACT.Copy,
                                               scale=gains[:, G_MEM + 2 * p + kk:G_MEM + 2 * p + kk + 1])
                ins.then_inc(tr_hi, 1)
            n0, _ = ITEMS["k"]
            high_parts(n0, 1)
            high_parts(n0 + 1, 0)
            act.wait_ge(fneg_ready, 1)
            for f in range(FH):
                if f == FH // 2:
                    high_parts(n0 + 1, 1)
                for t in range(TT):
                    part = foxs[:, f, t * P:(2 * t + 1) * P]
                    nc.scalar.activation(part, part, ACT.Exp, bias=fneg[:, f, t:t + 1], scale=FSCALE,
                                         accum_out=fsum[:, f, t:t + 1]).then_inc(fexp_done, 1)
            high_parts(n0 + 2, 0)
            high_parts(n0 + 2, 1)
            high_parts(n0 + 3, 0)

            def fox_hi(f):
                act.wait_ge(fo_done, f + 1)
                nc.scalar.activation(t1_hi[:, PW // P + f, :], misc[:, 2 + f % 2, 0:S], ACT.Copy).then_inc(fo_hi, 1)

            for j in range(CH):
                high_parts(n0 + 3 + (j + HALF) // CH, 1 - j // HALF, chunks=((j + HALF) % CH,))
                if j:
                    fox_hi(j - 1)
            fox_hi(FH - 1)
            n0, items = ITEMS["v"]
            with act.Fori(0, items) as i:
                high_parts(i + n0, 1)
                high_parts(i + (n0 + 1), 0)

            def turn_hi(pair0, i, hi, gain):
                for p in range(2):
                    pair_hi(pair0 + 2 * i + p, 2 * (i % 2) + p, hi, 4 * i + 2 * p, gain)

            def residual_items(name, hi, gain, pair0, squares0):
                n0, items = ITEMS[name]
                for i in range(items):
                    high_parts(n0 + i, 1)
                    if i:
                        turn_hi(pair0, i - 1, hi, gain)
                    high_parts(n0 + i + 1, 0)
                    act.wait_ge(acc_free, n0 + i + 3)
                    nc.scalar.activation(h[:, :, i * CW:(i + 1) * CW], hs[:, i % 2, :, :], ACT.Copy).then_inc(h_copied, 1)
                    square_sums(lambda t: hs[:, i % 2, t, :], i, i + squares0)

            def x_exps(i):
                q = i % 2
                for t in range(TT):
                    act.wait_ge(xneg_ready, i * TT + t + 1)
                    nc.scalar.activation(xp[:, i, t, :], misc[:, 2 * q + t, 0:S], ACT.Exp, bias=xneg[:, q, t:t + 1],
                                         scale=xfac[:, t:t + 1], accum_out=xsum[:, q, t:t + 1]).then_inc(xexp_done, 1)

            residual_items("out", t2_hi, G_X, PAIR0["h1"], 4)
            n0, items = ITEMS["q"]
            for i in range(items):
                high_parts(n0 + i, 1)
                if i:
                    x_exps(i - 1)
                else:
                    turn_hi(PAIR0["h1"], ITEMS["out"][1] - 1, t2_hi, G_X)
                    root(3)
                high_parts(n0 + i + 1, 0)
            x_exps(XH - 1)
            for u in range(2 * XH):
                act.wait_ge(xo_done, u + 1)
                nc.scalar.activation(t1_hi[:, 2 * u:2 * u + 2, :], xo_bank(u).rearrange("p (a s) -> p a s", a=2),
                                     ACT.Copy).then_inc(xo_hi, 1)
            residual_items("o", t2_hi, G_PEER, PAIR0["h2"], 8)
            n0, items = ITEMS["peer"]
            turn_hi(PAIR0["h2"], ITEMS["o"][1] - 1, t2_hi, G_PEER)
            high_parts(n0, 1, chunks=(HALF,))
            root(4)
            high_parts(n0, 1, chunks=range(HALF + 1, CH))
            high_parts(n0 + 1, 0)

            def gate_exp(g):
                act.wait_ge(nbest_ready, g + 1)
                nc.scalar.activation(exps[:, :], best[:, :], ACT.Exp, bias=neg_best[:, 0:1],
                                     accum_out=exp_sum[:, 0:1]).then_inc(gexp_done, 1)

            def diagonals(g, q, ks=range(TOP), fresh=False):
                act.wait_ge(wts_ready, g + 1)
                for k in ks:
                    if not fresh:
                        act.wait_ge(v_used, g * TOP + (k - 3))
                    nc.scalar.activation(diag[:, k % 4, :], ident[:, :], ACT.Copy, scale=wts[:, q, k:k + 1]).then_inc(diag_ready, 1)

            def gelu(g, q, c):
                act.wait_ge(dot_done, g * TOP + TOP)
                nc.scalar.activation(acts[:, q, :], dots[:, q, :], ACT.Gelu, scale=rstd[:, c:c + 1]).then_inc(gelu_done, 1)

            def period(p, q, c, second=False, last=False):
                if second:
                    diagonals(p - 1, 1 - q, range(4), fresh=True)
                if not last:
                    gate_exp(p + 1)
                diagonals(p - 1, 1 - q, range(4 if second else 0, TOP))
                gelu(p, q, c)

            def finish(c):
                for i in range(4):
                    act.wait_ge(y_added, 4 * c + i + 1)
                    if c or i >= 2:
                        act.wait_ge(y_squared, 4 * c + i - 1)
                    nc.scalar.activation(junk[:, i % 2, :], y_sum[:, c, i * CW:(i + 1) * CW], ACT.Square,
                                         accum_out=sq[:, c, i:i + 1]).then_inc(y_squared, 1)
                act.wait_ge(y_var, c + 1)
                nc.scalar.activation(rt[:, c:c + 1], ss[:, c:c + 1], ACT.Sqrt).then_inc(y_root, 1)
                act.wait_ge(y_rstd, c + 1)
                nc.scalar.activation(y_out[:, c, 0:D // 2], y_out[:, c, 0:D // 2], ACT.Copy, scale=rstd[:, c:c + 1]).then_inc(y_scaled, 1)

            def evacuate_queries(i):
                act.wait_ge(chunk_used, (n0 + i) * CH + CH)
                if i >= 2:
                    act.wait_ge(ps_done, TT * i)
                nc.scalar.activation(pq[:, i % 2, :, :], acc[:, i % 2, :, :].rearrange("p b (c s) -> p (b c) s", s=S),
                                     ACT.Copy).then_inc(acc_free, 1)

            def peer_scores(b):
                at, width = score_batch(b)
                act.wait_ge(rstd_ready, 4)
                for t in range(TT):
                    act.wait_ge(ps_done, b * TT + t + 1)
                    ins = nc.scalar.activation(scores[:, t, at:at + width], misc[:, 2 * (b % 2) + t, 0:width], ACT.Copy, scale=rstd[:, t:t + 1])
                ins.then_inc(scores_ready, 1)

            gate_exp(0)
            for i in range(1, items):
                high_parts(n0 + i, 1)
                peer_scores(i)
                if i < items - 1:
                    high_parts(n0 + i + 1, 0)
                    evacuate_queries(i)
            gate_exp(1)
            gelu(0, 0, 0)
            evacuate_queries(items - 1)
            peer_scores(items)
            period(1, 1, 0, second=True)
            for c in range(TT):
                with act.Fori(c * PH // 2 + 1 - c, (c + 1) * PH // 2 - c) as b:
                    period(b * 2, 0, c)
                    period(b * 2 + 1, 1, c)
            finish(0)
            period(GROUPS - 2, 0, 1)
            period(GROUPS - 1, 1, 1, last=True)
            nc.scalar.activation(warm[:, :], zeros[:, 0:1], ACT.Sqrt).then_inc(table_ready, 1)
            act.wait_ge(wts_ready, GROUPS)
            for m, k in enumerate(BY_PE):
                act.wait_ge(v_used, (GROUPS - 1) * TOP + m - 3)
                nc.scalar.activation(diag[:, m % 4, :], ident[:, :], ACT.Copy, scale=wts[:, 1, k:k + 1]).then_inc(diag_ready, 1)
            finish(1)

        @block.vector
        def _(dve):
            step = Steps(dve, dve_step, passed=passed)

            def low_parts(n, half, chunks=None):
                for j in chunks or range(half * HALF + 1, half * HALF + HALF, 2):
                    dve.wait_ge(hi_done, n * CH + (j + 1))
                    nc.vector.tensor_tensor(w_lo[:, j % RING, :, :], raw[:, j % RING, :, :],
                                            w_hi[:, j % RING, :, :].bitcast(F32), ALU.subtract).then_inc(lo_odd, 1)

            def reciprocal_root(k, sums):
                if sums is not None:
                    dve.wait_ge(squares, sums)
                    step(nc.vector.tensor_reduce(ss[:, :], sq[:, :, :], AX.X, ALU.add))
                nc.vector.tensor_scalar(ss[:, :], ss[:, :], 1.0 / D, EPS, ALU.mult, ALU.add).then_inc(var_ready, 1)
                dve.wait_ge(root_ready, k)
                nc.vector.reciprocal(rstd[:, :], rt[:, :]).then_inc(rstd_ready, 1)
                dve.wait_ge(rstd_ready, k)

            def pair_lo(done, count, bank, hi, lo, kt, gain):
                dve.wait_ge(done, count)
                for kk in range(2):
                    ins = nc.vector.scalar_tensor_tensor(
                        lo[:, bass.ds(kt + kk, 1), :], misc[:, bank:bank + 1, kk * S:(kk + 1) * S],
                        gains[:, bass.ds(kt + (gain + kk), 1)], hi[:, bass.ds(kt + kk, 1), :].bitcast(F32),
                        ALU.mult, ALU.subtract)
                ins.then_inc(tr_lo, 1)

            def evacuate(n, q, dst):
                dve.wait_ge(chunk_used, n * CH + CH)
                nc.vector.tensor_copy(dst, acc[:, q, :, :]).then_inc(acc_free, 1)

            def transposed(q):
                return acc[:, q, :, :].rearrange("p b (c s) -> p (b c) s", s=S)

            def evacuate_T(n, q, dst):
                dve.wait_ge(chunk_used, n * CH + CH)
                nc.vector.tensor_copy(dst, transposed(q)).then_inc(acc_free, 1)

            dve.wait_ge(consts, 1)
            dve.sem_inc(acc_free, 2)
            nc.vector.memset(warm[:, :], 0.0).then_inc(zero_ready, 1)
            nc.vector.memset(wf_hi[:, :, :].bitcast(F32), 0.0).then_inc(zero_ready, 1)
            nc.vector.memset(wf_lo[:, :, :].bitcast(F32), 0.0).then_inc(zero_ready, 1)
            dve.wait_ge(x_landed[1], 16)
            step(nc.vector.tensor_tensor_reduce(out=normed[:, 1, 0:D // 2], in0=h[:, 1, 0:D // 2], in1=h[:, 1, 0:D // 2], scale=1.0, scalar=0.0,
                                                op0=ALU.mult, op1=ALU.add, accum_out=sq[:, 1, 0:1]))
            dve.wait_ge(x_squared, 2)
            step(nc.vector.tensor_tensor(ss[:, 1:2], sq[:, 1, 0:1], sq[:, 1, 1:2], ALU.add))
            reciprocal_root(1, None)
            for half in range(2):
                cols = slice(half * D // 2, (half + 1) * D // 2)
                nc.vector.tensor_scalar(normed[:, 0, cols], h[:, 0, cols], rstd[:, 0:1], None, ALU.mult).then_inc(normed_ready[0], 1)
            dve.wait_ge(gains_T, 1)
            nc.vector.tensor_copy(gains[:, :], misc[:, 3, 0:NG]).then_inc(gains_ready, 1)
            dve.wait_ge(gains_ready, 1)
            for p in range(PAIRS):
                pair_lo(tr_hi, PAIR0["x"] + p + 1, p % 4, t1_hi, t1_lo, 2 * p, G_MIX)
                if p in (0, 2):
                    low_parts(0, 0, chunks=(p + 1,))
            low_parts(0, 1)
            low_parts(1, 0, chunks=(1,))
            evacuate_T(0, 0, foxT[:, 0:CT, :])
            low_parts(1, 0, chunks=(3,))
            dve.wait_ge(wf_hi_done, 1)
            dve.wait_ge(zero_ready, 3)
            nc.vector.tensor_tensor(wf_lo[:, :, 0:FH], wf[:, :, :], wf_hi[:, :, 0:FH].bitcast(F32), ALU.subtract).then_inc(wf_ready, 1)
            low_parts(1, 1)
            dve.wait_ge(inv_ready, 1)
            step(nc.vector.reciprocal(inv[:, 0:2, :], inv[:, 0:2, :]))
            low_parts(2, 0, chunks=(1,))
            evacuate_T(1, 1, foxT[:, CT:2 * CT, :])
            low_parts(2, 0, chunks=(3,))
            step(nc.vector.reciprocal(inv[:, 2:4, :], inv[:, 2:4, :]))
            with dve.Fori(1, T_IN // 2) as b:
                for q in range(2):
                    n = b * 2 + q
                    low_parts(n, 1)
                    low_parts(n + 1, 0, chunks=(1,))
                    evacuate_T(n, q, foxT[:, bass.ds(n * CT, CT), :])
                    low_parts(n + 1, 0, chunks=(3,))
            dve.wait_ge(f_done, 1)
            step(nc.vector.tensor_scalar(fz[:, :], misc[0:FH, 0, 0:S], bf[:, 0:1], None, ALU.add))
            nc.vector.scalar_tensor_tensor(fa[:, :], fz[:, :], -1.0, fz[:, :], ALU.mult, ALU.max).then_inc(fa_ready, 1)
            dve.wait_ge(fa_ready, 1)
            step(nc.vector.tensor_scalar(fz[:, :], fz[:, :], 0.0, None, ALU.min))

            def window_diff(g):
                src = foxT[:, g * GT:(g + 1) * GT, :]
                a, b = winA, winB
                step(nc.vector.tensor_copy(a[:, :, pad:], src))
                w = 1
                while w < WINDOWS[g]:
                    step(nc.vector.tensor_tensor(b[:, :, pad:], a[:, :, pad:], a[:, :, pad - w:pad - w + S], ALU.add))
                    a, b, w = b, a, 2 * w
                row = inv[:, g:g + 1, :].to_broadcast([P, GT, S])
                step(nc.vector.tensor_tensor(b[:, :, pad:], a[:, :, pad:], row, ALU.mult))
                nc.vector.tensor_tensor(diff[:, g * GT:(g + 1) * GT, :], b[:, :, pad:], src, ALU.subtract).then_inc(diff_ready, 1)
                dve.wait_ge(diff_ready, len(done_diffs) + 1)
                done_diffs.append(g)

            done_diffs = []
            step(nc.vector.memset(winA[:, :, 0:pad], 0.0))
            step(nc.vector.memset(winB[:, :, 0:pad], 0.0))
            window_diff(3)
            low_parts(T_IN, 1, chunks=(HALF + 1,))
            window_diff(2)
            low_parts(T_IN, 1, chunks=(HALF + 3,))
            reciprocal_root(2, 4 * TT)
            nc.vector.tensor_scalar(normed[:, 0, :], normed[:, 0, :], rstd[:, 0:1], None, ALU.mult).then_inc(normed_ready[0], 1)
            low_parts(T_IN + 1, 0, chunks=(1,))
            evacuate(T_IN, 0, foxv[:, :, 0:CW])
            low_parts(T_IN + 1, 0, chunks=(3,))
            dve.wait_ge(fl_ready, 1)
            step(nc.vector.tensor_tensor(fz[:, :], fz[:, :], fe[:, :], ALU.subtract))
            dve.wait_ge(consts, 6)
            step(nc.vector.tensor_tensor_scan(fa[:, :], fones[:, :], fz[:, :], 0.0, ALU.mult, ALU.add))
            step(nc.vector.tensor_scalar(cum[:, :], fa[:, :], -1.0 / FSCALE, None, ALU.mult))
            step(nc.vector.tensor_copy(cum_hi[:, :], cum[:, :]))
            nc.vector.tensor_tensor(cum_lo[:, :], cum[:, :], cum_hi[:, :].bitcast(F32), ALU.subtract).then_inc(cum_ready, 1)
            nc.vector.tensor_copy(sel_r[:, :, :], sel[:, :, :]).then_inc(cum_ready, 1)
            low_parts(T_IN + 1, 1)
            window_diff(1)
            window_diff(0)
            low_parts(T_IN + 2, 0, chunks=(1,))
            evacuate(T_IN + 1, 1, foxv[:, :, CW:2 * CW])
            low_parts(T_IN + 2, 0, chunks=(3,))
            dve.wait_ge(consts, 6)
            for f in range(FH):
                for t in range(TT):
                    u = f * TT + t
                    dve.wait_ge(qk_done, u + 1)
                    nc.vector.tensor_tensor_reduce(
                        out=foxs[:, f, t * P:(2 * t + 1) * P], in0=misc[:, u % 4, 0:(t + 1) * P], in1=mask[:, (1 - t) * P:2 * P],
                        scale=1.0, scalar=LOW, op0=ALU.add, op1=ALU.max, accum_out=fmax[:, f, t:t + 1]).then_inc(qk_read, 1)
            dve.wait_ge(qk_read, FH * TT)
            nc.vector.tensor_scalar(fneg[:, :, :], fmax[:, :, :], -FSCALE, None, ALU.mult).then_inc(fneg_ready, 1)
            for g in range(len(WINDOWS)):
                dve.wait_ge(tr_hi, PAIRS + g + 1)
                for dt in range(GT):
                    col = G_POOL + g * GT + dt
                    ins = nc.vector.scalar_tensor_tensor(
                        t1_lo[:, g * GT + dt, :], misc[:, g, dt * S:(dt + 1) * S], gains[:, col:col + 1],
                        t1_hi[:, g * GT + dt, :].bitcast(F32), ALU.mult, ALU.subtract)
                ins.then_inc(tr_lo, 1)
            for p in range(PAIRS):
                pair_lo(tr_hi, PAIRS + 4 + p + 1, p % 4, t2_hi, t2_lo, 2 * p, G_MEM)
            n0, items = ITEMS["k"]

            def key_items(b):
                for q in range(2):
                    i = b * 2 + q
                    low_parts(i + n0, 1)
                    low_parts(i + (n0 + 1), 0, chunks=(1,))
                    evacuate_T(i + n0, q, memk[:, bass.ds(i * CT, CT), :])
                    low_parts(i + (n0 + 1), 0, chunks=(3,))

            key_items(0)
            dve.wait_ge(fexp_done, FH * TT)
            step(nc.vector.reciprocal(frec[:, :, :], fsum[:, :, :]))
            for f in range(FH):
                for t in range(TT):
                    part = foxs[:, f, t * P:(2 * t + 1) * P]
                    ins = nc.vector.tensor_scalar(part, part, frec[:, f, t:t + 1], None, ALU.mult)
                ins.then_inc(fp_ready, 1)
            n = n0 + 2
            low_parts(n, 1)
            low_parts(n + 1, 0, chunks=(1,))
            evacuate_T(n, 0, memk[:, 2 * CT:3 * CT, :])
            low_parts(n + 1, 0, chunks=(3,))

            def fox_low(f):
                kt = PW // P + f
                dve.wait_ge(fo_hi, f + 1)
                nc.vector.tensor_tensor(t1_lo[:, kt, :], misc[:, 2 + f % 2, 0:S], t1_hi[:, kt, :].bitcast(F32), ALU.subtract).then_inc(fo_lo, 1)

            n = n0 + 3
            for j in range(CH):
                dve.wait_ge(pT_done, j + 1)
                nc.vector.tensor_copy(pT[:, j % 2, :], misc[:, j % 2, 0:3 * P]).then_inc(pT_copied, 1)
                if j:
                    fox_low(j - 1)
                if j in (1, 3):
                    low_parts(n, 1, chunks=(HALF + j,))
                if j == 5:
                    low_parts(n + 1, 0, chunks=(1,))
            evacuate_T(n, 1, memk[:, 3 * CT:4 * CT, :])
            low_parts(n + 1, 0, chunks=(3,))
            fox_low(FH - 1)
            n0, items = ITEMS["v"]
            with dve.Fori(0, items // 2) as b:
                for q in range(2):
                    i = b * 2 + q
                    low_parts(i + n0, 1)
                    low_parts(i + (n0 + 1), 0, chunks=(1,))
                    evacuate(i + n0, q, memv[:, :, bass.ds(i * CW, CW)])
                    low_parts(i + (n0 + 1), 0, chunks=(3,))

            def turn_lo(pair0, i, hi, lo, gain):
                for p in range(2):
                    pair_lo(tr_hi, pair0 + 4 + 2 * i + p + 1, 2 * (i % 2) + p, hi, lo, 4 * i + 2 * p, gain)

            def residual_items(name, hi, lo, gain, pair0):
                n0, items = ITEMS[name]
                for i in range(items):
                    low_parts(n0 + i, 1)
                    if i:
                        turn_lo(pair0, i - 1, hi, lo, gain)
                    elif name == "o":
                        for p in range(4):
                            dve.wait_ge(skT_done, p + 1)
                            nc.vector.tensor_copy(skT[:, 4 * p:4 * p + 4, :], misc[:, p, :].rearrange("p (a s) -> p a s", a=4)).then_inc(skT_copied, 1)
                    low_parts(n0 + i + 1, 0, chunks=(1,))
                    dve.wait_ge(chunk_used, (n0 + i) * CH + CH)
                    nc.vector.tensor_tensor(hs[:, i % 2, :, :], acc[:, i % 2, :, :], h[:, :, i * CW:(i + 1) * CW],
                                            ALU.add).then_inc(acc_free, 1)
                    low_parts(n0 + i + 1, 0, chunks=(3,))
                    if name == "o":
                        dve.wait_ge(pgain_landed, 16)
                        dve.wait_ge(acc_free, n0 + i + 3)
                        step(nc.vector.tensor_tensor(hn[:, :, i * CW:(i + 1) * CW], hs[:, i % 2, :, :],
                                                     peer_gain[:, i * CW:(i + 1) * CW].unsqueeze(1).to_broadcast([P, TT, CW]), ALU.mult))

            def x_max(i):
                q = i % 2
                for t in range(TT):
                    dve.wait_ge(xs_done, i * TT + t + 1)
                    step(nc.vector.tensor_reduce(xmax[:, q, t:t + 1], misc[:, 2 * q + t, 0:S], AX.X, ALU.max))
                    nc.vector.tensor_scalar(xneg[:, q, t:t + 1], xmax[:, q, t:t + 1], xfac[:, t:t + 1], -1.0,
                                            ALU.mult, ALU.mult).then_inc(xneg_ready, 1)

            def x_norm(i):
                q = i % 2
                for t in range(TT):
                    dve.wait_ge(xexp_done, i * TT + t + 1)
                    step(nc.vector.reciprocal(xrec[:, q, t:t + 1], xsum[:, q, t:t + 1]))
                    nc.vector.tensor_scalar(xp[:, i, t, :], xp[:, i, t, :], xrec[:, q, t:t + 1], None,
                                            ALU.mult).then_inc(xp_ready, 1)

            residual_items("out", t2_hi, t2_lo, G_X, PAIR0["h1"])
            n0, items = ITEMS["q"]
            for i in range(items):
                low_parts(n0 + i, 1)
                if i:
                    x_max(i - 1)
                    x_norm(i - 1)
                else:
                    turn_lo(PAIR0["h1"], ITEMS["out"][1] - 1, t2_hi, t2_lo, G_X)
                    reciprocal_root(3, 2 * 4 * TT)
                    step(nc.vector.tensor_scalar(xfac[:, :], rstd[:, :], XSCALE, None, ALU.mult))
                low_parts(n0 + i + 1, 0, chunks=(1,))
                evacuate_T(n0 + i, i % 2, qs[:, i % 2, :, :])
                low_parts(n0 + i + 1, 0, chunks=(3,))

            def x_turned(hd):
                dve.wait_ge(xpT_done, hd + 1)
                nc.vector.tensor_copy(xpT[:, hd % 2, :, :], misc[:, hd % 2, :].rearrange("p (m s) -> p m s", m=TT)).then_inc(xpT_copied, 1)

            def xo_low(u):
                dve.wait_ge(xo_hi, u + 1)
                nc.vector.tensor_tensor(t1_lo[:, 2 * u:2 * u + 2, :], xo_bank(u).rearrange("p (a s) -> p a s", a=2),
                                        t1_hi[:, 2 * u:2 * u + 2, :].bitcast(F32), ALU.subtract).then_inc(xo_lo, 1)

            x_turned(0)
            x_max(XH - 1)
            x_turned(1)
            x_norm(XH - 1)
            for hd in range(2, XH):
                xo_low(2 * hd - 4)
                xo_low(2 * hd - 3)
                x_turned(hd)
            for u in range(2 * XH - 4, 2 * XH):
                xo_low(u)
            residual_items("o", t2_hi, t2_lo, G_PEER, PAIR0["h2"])
            n0, items = ITEMS["peer"]
            turn_lo(PAIR0["h2"], ITEMS["o"][1] - 1, t2_hi, t2_lo, G_PEER)
            reciprocal_root(4, 3 * 4 * TT)
            low_parts(n0, 1, chunks=(HALF + 1,))

            dve.wait_ge(chunk_used, n0 * CH + HALF)
            nc.vector.tensor_copy(pq[:, 0, 0:2, :], acc[:, 0, 0, :].rearrange("p (c s) -> p c s", s=S)).then_inc(half_read, 1)
            low_parts(n0, 1, chunks=(HALF + 3,))
            at, width = score_batch(0)
            for t in range(TT):
                dve.wait_ge(ps_done, t + 1)
                ins = nc.vector.tensor_scalar(scores[:, t, at:at + width], misc[:, t, 0:width], rstd[:, t:t + 1], None, ALU.mult)
            ins.then_inc(first_scores, 1)
            dve.wait_ge(first_scores, 1)

            def top16(rows):
                def each(op, apart):
                    for row in rows[:-1]:
                        op(*row)
                    step(op(*rows[-1]), apart=apart)

                each(lambda values, left, maxima, places: nc.vector.max(maxima[:, 0:8], values), True)
                for values, left, maxima, places in rows:
                    nc.vector.max_index(places[:, 0:8], maxima[:, 0:8], values)
                each(lambda values, left, maxima, places: nc.vector.match_replace(left, maxima[:, 0:8], values, LOW), True)
                each(lambda values, left, maxima, places: nc.vector.max(maxima[:, 8:16], left), True)
                each(lambda values, left, maxima, places: nc.vector.max_index(places[:, 8:16], maxima[:, 8:16], left), True)

            def route(g, q, c, head, amid=None):
                step(nc.vector.tensor_copy(cur[:, :, :], scores[:, c, bass.ds(head * (2 * KEYS), 2 * KEYS)].rearrange("p (a k) -> p a k", a=2)),
                     apart=True)
                top16([(cur[:, a, :], rest[:, a, :], top[:, a, :], top_at[:, a, :]) for a in range(2)])
                if amid is not None:
                    amid()
                step(nc.vector.tensor_tensor(cand[:, :, :], top[:, 0, :].unsqueeze(2).to_broadcast([P, TOP, TOP]),
                                             top[:, 1, :].unsqueeze(1).to_broadcast([P, TOP, TOP]), ALU.add), apart=True)
                top16([(cand[:, :, :].rearrange("p a b -> p (a b)"), cand_rest[:, :, :].rearrange("p a b -> p (a b)"), best, pos)])
                nc.vector.tensor_scalar(neg_best[:, :], best[:, 0:1], -1.0, None, ALU.mult).then_inc(nbest_ready, 1)
                nc.vector.tensor_scalar(ab[:, 0, :], pos[:, :], 4, None, ALU.logical_shift_right)
                step(nc.vector.tensor_scalar(ab[:, 1, :], pos[:, :], TOP - 1, None, ALU.bitwise_and))
                step(nc.vector.tensor_tensor(hot[:, :, :, :].rearrange("p a k i -> p (a k) i"),
                                             ab[:, :, :].rearrange("p a k -> p (a k)").unsqueeze(2).to_broadcast([P, 2 * TOP, TOP]),
                                             iota[:, :].unsqueeze(1).to_broadcast([P, 2 * TOP, TOP]), ALU.is_equal))
                step(nc.vector.tensor_tensor(hot[:, :, :, :], hot[:, :, :, :],
                                             top_at[:, :, :].unsqueeze(2).to_broadcast([P, 2, TOP, TOP]), ALU.mult))
                step(nc.vector.tensor_reduce(picked[:, :, :], hot[:, :, :, :], AX.X, ALU.add))
                nc.vector.scalar_tensor_tensor(idx_u[:, q, :], picked[:, 0, :], float(KEYS), picked[:, 1, :],
                                               ALU.mult, ALU.add).then_inc(routed, 1)

            def gates(g, q):
                dve.wait_ge(gexp_done, g + 1)
                step(nc.vector.reciprocal(exp_rec[:, :], exp_sum[:, :]))
                step(nc.vector.tensor_scalar(gate[:, q, :], exps[:, :], exp_rec[:, 0:1], None, ALU.mult))

            ROUTE_STEPS = 1 + 4 + 1 + 4 + 4 + 2

            def weights(g, q, fresh=False):
                dve.wait_ge(gelu_done, g + 1)
                if not fresh:
                    dve.wait_ge(diag_ready, g * TOP - (TOP - 1))
                nc.vector.tensor_tensor(wts[:, q, :], acts[:, q, :], gate[:, q, :], ALU.mult).then_inc(wts_ready, 1)

            def dot_products(g, q, c, ks, first=False):
                for k in ks:
                    dve.wait_ge(u_landed[k % 4], g * (16 * TOP // 4) + 16 * (k // 4 + 1))
                    if not (first and k == 0):
                        dve.wait_ge(dot_done, g * TOP + k)
                    nc.vector.tensor_tensor_reduce(out=product[:, :], in0=u_ring[:, k % 4, :], in1=hn[:, c, :], scale=1.0, scalar=0.0,
                                                   op0=ALU.mult, op1=ALU.add, accum_out=dots[:, q, k:k + 1]).then_inc(dot_done, 1)

            def period(g, q, c, next_c, next_head, second=False, last=False):
                if not second:
                    for s in range(4):
                        dve.wait_ge(v_landed[s], g * (16 * TOP // 4) - 16 * TOP // 4)
                dve.wait_ge(routed, g + 1)
                nc.vector.tensor_copy(idx_v[:, q, :], idx_u[:, q, :]).then_inc(idx_v_ready, 1)
                weights(g - 1, 1 - q, fresh=second)
                dve.wait_ge(wts_ready, g)
                if second:
                    dot_products(g, q, c, range(0, 4))
                if not last:
                    route(g + 1, 1 - q, next_c, next_head)
                    gates(g + 1, 1 - q)
                dot_products(g, q, c, range(4 if second else 0, TOP))

            def finish(c):
                k = TOP - 1
                if c == 0:
                    dve.wait_ge(y_done, 1)
                else:
                    dve.wait_ge(v_landed[k % 4], GROUPS * (16 * TOP // 4))
                for i in range(4):
                    cols = slice(i * CW, (i + 1) * CW)
                    if c == 0:
                        ins = nc.vector.tensor_tensor(y_sum[:, c, cols], misc[:, i, :], h[:, c, cols], ALU.add)
                    else:
                        ins = nc.vector.scalar_tensor_tensor(y_sum[:, c, cols], v_ring[:, k % 4, cols], wts[:, 1, k:k + 1],
                                                             y_sum[:, c, cols], ALU.mult, ALU.add)
                    ins.then_inc(y_added, 1)
                dve.wait_ge(fgain_landed, 16)
                dve.wait_ge(y_added, 4 * c + 4)
                step(nc.vector.tensor_tensor(y_out[:, c, 0:D // 2], y_sum[:, c, 0:D // 2], final_gain[:, 0:D // 2], ALU.mult))
                dve.wait_ge(y_squared, 4 * (c + 1))
                step(nc.vector.tensor_reduce(ss[:, c:c + 1], sq[:, c, :], AX.X, ALU.add))
                nc.vector.tensor_scalar(ss[:, c:c + 1], ss[:, c:c + 1], 1.0 / D, EPS, ALU.mult, ALU.add).then_inc(y_var, 1)
                dve.wait_ge(y_root, c + 1)
                nc.vector.reciprocal(rstd[:, c:c + 1], rt[:, c:c + 1]).then_inc(y_rstd, 1)
                dve.wait_ge(y_rstd, c + 1)
                nc.vector.scalar_tensor_tensor(y_out[:, c, D // 2:D], y_sum[:, c, D // 2:D], rstd[:, c:c + 1], final_gain[:, D // 2:D],
                                               ALU.mult, ALU.mult).then_inc(y_ready, 1)

            def two_periods(b, c, next_c, last=False):
                head = b * 2 - c * PH
                period(b * 2, 0, c, c, head + 1)
                period(b * 2 + 1, 1, c, next_c, (head + 2) if next_c == c else 0, last=last)

            route(0, 0, 0, 0)
            low_parts(n0 + 1, 0, chunks=(1,))
            dve.wait_ge(routed, 1)
            nc.vector.tensor_copy(idx_v[:, 0, :], idx_u[:, 0, :]).then_inc(idx_v_ready, 1)
            dve.wait_ge(chunk_used, n0 * CH + CH)
            nc.vector.tensor_copy(pq[:, 0, 2:4, :], acc[:, 0, 1, :].rearrange("p (c s) -> p c s", s=S)).then_inc(acc_free, 1)
            low_parts(n0 + 1, 0, chunks=(3,))
            gates(0, 0)
            low_parts(n0 + 1, 1, chunks=(HALF + 1,))
            dot_products(0, 0, 0, range(0, 3), first=True)
            low_parts(n0 + 1, 1, chunks=(HALF + 3,))
            dot_products(0, 0, 0, range(3, 4))
            low_parts(n0 + 2, 0, chunks=(1,))
            dot_products(0, 0, 0, range(4, 6))
            dve.wait_ge(scores_ready, 1)
            route(1, 1, 0, 1, amid=lambda: low_parts(n0 + 2, 0, chunks=(3,)))
            low_parts(n0 + 2, 1, chunks=(HALF + 1,))
            dot_products(0, 0, 0, range(6, 7))
            low_parts(n0 + 2, 1, chunks=(HALF + 3,))
            dot_products(0, 0, 0, range(7, 9))
            low_parts(n0 + 3, 0, chunks=(1,))
            dot_products(0, 0, 0, range(9, 10))
            low_parts(n0 + 3, 0, chunks=(3,))
            dot_products(0, 0, 0, range(10, 12))
            low_parts(n0 + 3, 1, chunks=(HALF + 1,))
            dot_products(0, 0, 0, range(12, 13))
            low_parts(n0 + 3, 1, chunks=(HALF + 3,))
            dot_products(0, 0, 0, range(13, 16))
            gates(1, 1)
            dve.wait_ge(scores_ready, items)
            period(1, 1, 0, 0, 2, second=True)
            HB = PH // 2
            with dve.Fori(0, HB - 2) as i:
                step.enter(i, 2 * ROUTE_STEPS)
                two_periods(i + 1, 0, 0)
            step.leave(HB - 2)
            two_periods(HB - 1, 0, 1)
            with dve.Fori(0, HB - 1) as i:
                step.enter(i, 2 * ROUTE_STEPS)
                two_periods(i + HB, 1, 1)
            step.leave(HB - 1)
            finish(0)
            two_periods(2 * HB - 1, 1, 1, last=True)
            weights(GROUPS - 1, 1)
            dve.wait_ge(wts_ready, GROUPS)
            for m, k in enumerate(BY_DVE[:-1]):
                dve.wait_ge(v_landed[k % 4], (GROUPS - 1) * (16 * TOP // 4) + 16 * (k // 4 + 1))
                nc.vector.scalar_tensor_tensor(y_sum[:, 1, :], v_ring[:, k % 4, :], wts[:, 1, k:k + 1], (y_sum if m else h)[:, 1, :],
                                               ALU.mult, ALU.add).then_inc(v_added, 1)
                dve.wait_ge(v_added, m + 1)
                if k == TOP - 5:
                    dve.wait_ge(y_done, TT)
                    step(nc.vector.tensor_tensor(y_sum[:, 1, :], acc[:, :, :, :].rearrange("p a b n -> p (a b n)"),
                                                 y_sum[:, 1, :], ALU.add))
            finish(1)

        @block.tensor
        def _(pe):
            def chunk_ready(n, j):
                pe.wait_ge((lo_even, lo_odd)[j % 2], n * HALF + (j // 2 + 1))

            def products(n, q, hi, lo, turned, between={}, ready=None):
                pe.wait_ge(acc_free, n + 1)
                for j in range(CH):
                    if ready is not None:
                        pe.wait_ge(ready[0], ready[1] + j + 1)
                    chunk_ready(n, j)
                    s = j % RING
                    for kk in range(KC):
                        kt = j * KC + kk
                        first, last = kt == 0, kt == KT - 1
                        if turned:
                            for ct in range(CT):
                                o = acc[:, q, ct // 2, ct % 2 * S:(ct % 2 + 1) * S]
                                wh, wl = (w[:, s, kk, ct * P:(ct + 1) * P] for w in (w_hi, w_lo))
                                nc.tensor.matmul(o, wh, hi[:, kt, :], start=first and ct % 2 == 0, stop=False, skip_group_check=True)
                                nc.tensor.matmul(o, wh, lo[:, kt, :], start=False, stop=False, skip_group_check=True)
                                ins = nc.tensor.matmul(o, wl, hi[:, kt, :], start=False, stop=last and ct % 2 == 1, skip_group_check=True)
                        else:
                            for t in range(TT):
                                o = acc[:, q, t, :]
                                xh, xl = (a[:, kt, t * P:(t + 1) * P] for a in (hi, lo))
                                nc.tensor.matmul(o, xh, w_hi[:, s, kk, :], start=first, stop=False)
                                nc.tensor.matmul(o, xh, w_lo[:, s, kk, :], start=False, stop=False)
                                ins = nc.tensor.matmul(o, xl, w_hi[:, s, kk, :], start=False, stop=last)
                    ins.then_inc(chunk_used, 1)
                    if j in between:
                        between[j]()

            def transposes(pair, bank, src, free=None, count=0):
                if free is not None:
                    pe.wait_ge(free, count)
                for kk in range(2):
                    for t in range(TT):
                        ins = nc.tensor.transpose(misc[:, bank, kk * S + t * P:kk * S + (t + 1) * P], src(t, kk), ident[:, :])
                ins.then_inc(tr_ready, 1)

            pe.wait_ge(consts, 1)
            pe.wait_ge(small_landed, 16 * 7)
            nc.tensor.transpose(misc[:, 3, 0:NG], gain_rows[:, :], ident[0:NG, 0:NG]).then_inc(gains_T, 1)
            pe.wait_ge(normed_ready[0], 1)
            pe.wait_ge(normed_ready[1], 1)
            pe.wait_ge(gains_ready, 1)

            def normed_pair(p, wait0=None):
                if p == 4:
                    for t in range(TT):
                        pe.wait_ge(normed_ready[t], 2)
                transposes(p, p % 4, lambda t, kk: normed[:, t, (2 * p + kk) * P:(2 * p + kk + 1) * P],
                           None if wait0 is None else tr_lo, (wait0 or 0) + p)

            for p in range(4):
                normed_pair(p)
            products(0, 0, t1_hi, t1_lo, True, ready=(tr_lo, 0),
                     between={j: lambda j=j: [normed_pair(p, -3) for p in (4 + 2 * j, 5 + 2 * j)] for j in range(2)})
            products(1, 1, t1_hi, t1_lo, True)
            with pe.Fori(1, T_IN // 2) as b:
                for q in range(2):
                    products(b * 2 + q, q, t1_hi, t1_lo, True)
            pe.wait_ge(wf_ready, 1)
            o = misc[:, 0, 0:S]
            for kt in range(KT):
                nc.tensor.matmul(o, wf_hi[:, kt, :], t1_hi[:, kt, :], start=kt == 0, stop=False)
                nc.tensor.matmul(o, wf_hi[:, kt, :], t1_lo[:, kt, :], start=False, stop=False)
                ins = nc.tensor.matmul(o, wf_lo[:, kt, :], t1_hi[:, kt, :], start=False, stop=kt == KT - 1)
            ins.then_inc(f_done, 1)
            products(T_IN, 0, t1_hi, t1_lo, False)
            products(T_IN + 1, 1, t1_hi, t1_lo, False)
            pe.wait_ge(cum_ready, 2)
            pe.wait_ge(consts, 6)
            for f in range(FH):
                for t in range(TT):
                    u = f * TT + t
                    if u >= 4:
                        pe.wait_ge(qk_read, u - 3)
                    keys = (t + 1) * P
                    o = misc[:, u % 4, 0:keys]
                    nc.tensor.matmul(o, foxT[:, PW // P + f, t * P:(t + 1) * P], foxT[:, PW // P + FH + f, 0:keys], start=True, stop=False)
                    nc.tensor.matmul(o, sel_r[:, f, :], cum_hi[:, 0:keys], start=False, stop=False)
                    nc.tensor.matmul(o, sel_r[:, f, :], cum_lo[:, 0:keys], start=False, stop=True).then_inc(qk_done, 1)
            pe.wait_ge(qk_read, FH * TT)
            pe.wait_ge(diff_ready, len(WINDOWS))
            pe.wait_ge(pool_landed, 16)
            for g in range(len(WINDOWS)):
                for dt in range(GT):
                    for ct in range(GT):
                        ins = nc.tensor.matmul(misc[:, g, dt * S:(dt + 1) * S], poolw[:, g, ct, dt * P:(dt + 1) * P],
                                               diff[:, g * GT + ct, :], start=ct == 0, stop=ct == GT - 1)
                ins.then_inc(poolT_done, 1)
            pe.wait_ge(normed_ready[0], 3)
            pe.wait_ge(normed_ready[1], 3)
            for p in range(4):
                normed_pair(p, PAIRS + 1)
            n0, items = ITEMS["k"]
            products(n0, 0, t2_hi, t2_lo, True, ready=(tr_lo, PAIRS + 4),
                     between={j: lambda j=j: [normed_pair(p, PAIRS + 1) for p in (4 + 2 * j, 5 + 2 * j)] for j in range(2)})
            products(n0 + 1, 1, t2_hi, t2_lo, True)

            def fox_values(j):
                if j < FH:
                    if j >= 2:
                        pe.wait_ge(pT_copied, j - 1)
                    else:
                        pe.wait_ge(fp_ready, FH)
                    for part in range(3):
                        ins = nc.tensor.transpose(misc[:, j % 2, part * P:(part + 1) * P], foxs[:, j, part * P:(part + 1) * P], ident[:, :])
                    ins.then_inc(pT_done, 1)
                if j:
                    e = j - 1
                    pe.wait_ge(pT_copied, e + 1)
                    if e >= 2:
                        pe.wait_ge(fo_lo, e - 1)
                    nc.tensor.matmul(misc[:, 2 + e % 2, 0:S], foxv[:, 0, e * P:(e + 1) * P], pT[:, e % 2, 0:2 * P], start=True, stop=False)
                    nc.tensor.matmul(misc[:, 2 + e % 2, P:S], foxv[:, 1, e * P:(e + 1) * P], pT[:, e % 2, 2 * P:3 * P],
                                     start=False, stop=True).then_inc(fo_done, 1)

            assert items == 4 and FH == CH
            products(n0 + 2, 0, t2_hi, t2_lo, True)
            products(n0 + 3, 1, t2_hi, t2_lo, True, between={j: (lambda j=j: fox_values(j)) for j in range(CH)})
            fox_values(FH)
            n0, items = ITEMS["v"]
            with pe.Fori(0, items // 2) as b:
                for q in range(2):
                    products(b * 2 + (n0 + q), q, t2_hi, t2_lo, False)
            pe.wait_ge(fo_lo, FH)

            def turn(name, pair0, i):
                pe.wait_ge(acc_free, ITEMS[name][0] + i + 3)
                for p in range(2):
                    transposes(None, 2 * (i % 2) + p, lambda t, kk: hs[:, i % 2, t, (2 * p + kk) * P:(2 * p + kk + 1) * P],
                               tr_lo, pair0 + 4 + 2 * i + p - 3)

            def sub_keys():
                pe.wait_ge(sk_landed, 16)
                pe.wait_ge(xo_lo, 2 * XH)
                for p in range(4):
                    for a in range(4):
                        ins = nc.tensor.transpose(misc[:, p, a * P:(a + 1) * P], skraw[:, 4 * p + a, :], ident[:, :])
                    ins.then_inc(skT_done, 1)

            def residual_items(name, hi, lo, pair0, ready=None, first={}):
                n0, items = ITEMS[name]
                for i in range(items):
                    products(n0 + i, i % 2, hi, lo, False, ready=None if i else ready,
                             between={HALF - 1: lambda: turn(name, pair0, i - 1)} if i else first)

            def x_scores(i):
                q = i % 2
                pe.wait_ge(acc_free, ITEMS["q"][0] + i + 3)
                if i >= 2:
                    pe.wait_ge(xexp_done, TT * (i - 1))
                for t in range(TT):
                    for c in range(XT):
                        ins = nc.tensor.matmul(misc[:, 2 * q + t, 0:S], qs[:, q, c, t * P:(t + 1) * P],
                                               memk[:, i * XT + c, :], start=c == 0, stop=c == XT - 1)
                    ins.then_inc(xs_done, 1)

            def x_turn(hd):
                pe.wait_ge(xp_ready, TT * (hd + 1))
                if hd >= 2:
                    pe.wait_ge(xpT_copied, hd - 1)
                else:
                    pe.wait_ge(xexp_done, TT * (XH - 1))
                for m in range(TT):
                    for t in range(TT):
                        ins = nc.tensor.transpose(misc[:, hd % 2, m * S + t * P:m * S + (t + 1) * P],
                                                  xp[:, hd, t, m * P:(m + 1) * P], ident[:, :])
                ins.then_inc(xpT_done, 1)

            def x_values(hd):
                pe.wait_ge(xpT_copied, hd + 1)
                for u in (2 * hd, 2 * hd + 1):
                    if u >= 4:
                        pe.wait_ge(xo_lo, u - 3)
                    elif u >= 2:
                        pe.wait_ge(xexp_done, TT * XH)
                    for d2 in range(2):
                        for m in range(TT):
                            dt = 2 * u + d2
                            ins = nc.tensor.matmul(xo_bank(u)[:, d2 * S:(d2 + 1) * S], memv[:, m, dt * P:(dt + 1) * P],
                                                   xpT[:, hd % 2, m, :], start=m == 0, stop=m == TT - 1)
                    ins.then_inc(xo_done, 1)

            residual_items("out", t1_hi, t1_lo, PAIR0["h1"])
            n0, items = ITEMS["q"]
            for i in range(items):
                products(n0 + i, i % 2, t2_hi, t2_lo, True, ready=None if i else (tr_lo, PAIR0["h1"] + 4),
                         between={HALF - 1: (lambda: x_scores(i - 1)) if i else (lambda: turn("out", PAIR0["h1"], ITEMS["out"][1] - 1))})
            x_turn(0)
            x_scores(XH - 1)
            x_turn(1)
            for hd in range(XH):
                x_values(hd)
                if hd + 2 < XH:
                    x_turn(hd + 2)
            residual_items("o", t1_hi, t1_lo, PAIR0["h2"], ready=(xo_lo, 0), first={HALF - 1: sub_keys})

            def p_scores(b):
                if b == 0:
                    pe.wait_ge(half_read, 1)
                    i, cs = 0, range(0, 2)
                else:
                    i, cs = b - 1, (range(CT) if b > 1 else range(2, CT))
                    pe.wait_ge(acc_free, ITEMS["peer"][0] + i + 3)
                if b == 2:
                    pe.wait_ge(first_scores, 1)
                elif b > 2:
                    pe.wait_ge(scores_ready, b - 2)
                for t in range(TT):
                    for c in cs:
                        at = (c - cs[0]) * KEYS
                        ins = nc.tensor.matmul(misc[:, 2 * (b % 2) + t, at:at + KEYS], pq[:, i % 2, c, t * P:(t + 1) * P],
                                               skT[:, i * CT + c, :], start=True, stop=True)
                    ins.then_inc(ps_done, 1)

            n0, items = ITEMS["peer"]
            pe.wait_ge(acc_free, n0 + 1)
            for j in range(CH):
                head, s = j // HALF, j % RING
                if head == 0:
                    pe.wait_ge(tr_lo, PAIR0["h2"] + 4 + (j + 1) * WKC // 2)
                chunk_ready(n0, j)
                for kk in range(WKC):
                    kt = j % HALF * WKC + kk
                    for ct in range(2):
                        o = acc[:, 0, head, ct * S:(ct + 1) * S]
                        wh, wl = (head_chunk(w[:, s], kk, ct * P, P) for w in (w_hi, w_lo))
                        nc.tensor.matmul(o, wh, t2_hi[:, kt, :], start=kt == 0 and ct == 0, stop=False, skip_group_check=True)
                        nc.tensor.matmul(o, wh, t2_lo[:, kt, :], start=False, stop=False, skip_group_check=True)
                        ins = nc.tensor.matmul(o, wl, t2_hi[:, kt, :], start=False, stop=kt == KT - 1 and ct == 1, skip_group_check=True)
                    if j == HALF and kk == 1:
                        pe.wait_ge(skT_copied, 4)
                        p_scores(0)
                ins.then_inc(chunk_used, 1)
                if j == 0:
                    turn("o", PAIR0["h2"], ITEMS["o"][1] - 1)
            products(n0 + 1, 1, t2_hi, t2_lo, True, between={0: lambda: p_scores(1)})
            products(n0 + 2, 0, t2_hi, t2_lo, True, between={HALF - 1: lambda: p_scores(2)})
            products(n0 + 3, 1, t2_hi, t2_lo, True, between={HALF - 1: lambda: p_scores(3)})
            p_scores(4)
            pe.wait_ge(scores_ready, items)
            for c in range(TT):
                banks = [misc[:, n, :] for n in range(4)] if c == 0 else [acc[:, n // 2, n % 2, :] for n in range(4)]
                for o in banks:
                    nc.tensor.matmul(o, zeros[:, 0:P], zeros[:, :], start=True, stop=False)
                with pe.Fori(c * PH, (c + 1) * PH - c) as g:
                    for k in range(TOP):
                        pe.wait_ge(v_landed[k % 4], g * (16 * TOP // 4) + 16 * (k // 4 + 1))
                        pe.wait_ge(diag_ready, g * TOP + (k + 1))
                        for n, o in enumerate(banks):
                            ins = nc.tensor.matmul(o, diag[:, k % 4, :], v_ring[:, k % 4, n * CW:(n + 1) * CW], start=False, stop=False)
                        ins.then_inc(v_used, 1)
                if c == TT - 1:
                    g = GROUPS - 1
                    for m, k in enumerate(BY_PE):
                        pe.wait_ge(v_landed[k % 4], g * (16 * TOP // 4) + 16 * (k // 4 + 1))
                        pe.wait_ge(diag_ready, g * TOP + m + 1)
                        for n, o in enumerate(banks):
                            ins = nc.tensor.matmul(o, diag[:, m % 4, :], v_ring[:, k % 4, n * CW:(n + 1) * CW], start=False, stop=False)
                        ins.then_inc(v_used, 1)
                for o in banks:
                    ins = nc.tensor.matmul(o, zeros[:, 0:P], zeros[:, :], start=False, stop=True)
                ins.then_inc(y_done, 1)


_INS = ['x', 'mem', 'mix_norm', 'w_in', 'b_forget', 'pool_w', 'pool_scale', 'w_out', 'xattn_norm', 'mem_norm', 'xattn_wq',
        'xattn_wk', 'xattn_wv', 'xattn_wo', 'peer_norm', 'peer_wq', 'peer_sub_keys', 'peer_u', 'peer_v', 'final_norm']
_OUTS = [((1, 256, 2048), 'float32')]


def kernel(**inputs):
    import numpy as _np
    import concourse.bacc as _bacc
    from concourse import mybir as _mybir
    from concourse.bass_utils import run_bass_kernel_spmd as _run

    nc = _bacc.Bacc("TRN2", target_bir_lowering=False, num_devices=1)
    arrays, args = {}, []
    for name in _INS:
        a = _np.ascontiguousarray(inputs[name])
        arrays[f"in_{name}_dram"] = a
        args.append(nc.dram_tensor(f"in_{name}_dram", a.shape, _mybir.dt.from_np(a.dtype), kind="ExternalInput").ap())
    for i, (shape, dtype) in enumerate(_OUTS):
        dt = _mybir.dt.from_np(_np.dtype(dtype))
        args.append(nc.dram_tensor(f"out_{i}_dram", shape, dt, kind="ExternalOutput").ap())
    hybrid_layer(nc, *args)
    r = _run(nc, [arrays], core_ids=[0])
    return r.results[0]["out_0_dram"]
```
